# Optimizing a Trainium2 kernel written in Bass

```python
import jax, jax.numpy as jnp
from jax import lax
import numpy as np

D_MODEL = 1024
BATCH = 1
SEQ = 1024
DEPTH = 1

MLSTM_HEADS = 4
MLSTM_HEAD_DIM = 256
MLSTM_WIDTH = MLSTM_HEADS * MLSTM_HEAD_DIM
MLSTM_CHUNK = 64
CONV_WIDTH = 4
ATTN_GROUPS = ((128, 1), (512, 4), (2048, 16))
N_GROUPS = len(ATTN_GROUPS)
HEADS_PER_GROUP = 4
ATTN_HEAD_DIM = 128
ATTN_HEADS = N_GROUPS * HEADS_PER_GROUP
ATTN_QKV_WIDTH = ATTN_HEADS * ATTN_HEAD_DIM
ATTN_OUT_WIDTH = HEADS_PER_GROUP * ATTN_HEAD_DIM
ROPE_DIM = ATTN_HEAD_DIM // 4
ROPE_THETA = 500000.0
EPS = 1e-6
IN_SPLITS = (MLSTM_WIDTH, MLSTM_WIDTH, MLSTM_WIDTH, MLSTM_WIDTH, MLSTM_HEADS, MLSTM_HEADS,
             ATTN_QKV_WIDTH, ATTN_QKV_WIDTH, ATTN_QKV_WIDTH, ATTN_OUT_WIDTH, D_MODEL, D_MODEL)
IN_WIDTH = sum(IN_SPLITS)

kernel_name = 'hybrid_mlstm_dilated_attn_block'

def rms_norm(x, gain):
    xf = x.astype(jnp.float32)
    y = xf * lax.rsqrt(jnp.mean(xf * xf, axis=-1, keepdims=True) + EPS)
    return (y * gain.astype(jnp.float32)).astype(x.dtype)

def causal_depthwise_conv(x, w, b):
    y = lax.conv_general_dilated(x, w[:, None, :], window_strides=(1,),
                                 padding=((CONV_WIDTH - 1, 0),),
                                 dimension_numbers=('NWC', 'WIO', 'NWC'),
                                 feature_group_count=x.shape[-1])
    return y + b

def partial_rotary(t, positions):
    half = ROPE_DIM // 2
    inv_freq = ROPE_THETA ** (-jnp.arange(half, dtype=jnp.float32) / half)
    ang = positions.astype(jnp.float32)[..., None] * inv_freq
    cos = jnp.cos(ang)[:, :, None, :]
    sin = jnp.sin(ang)[:, :, None, :]
    tr = t[..., :ROPE_DIM].astype(jnp.float32)
    x1, x2 = tr[..., :half], tr[..., half:]
    rot = jnp.concatenate([x1 * cos - x2 * sin, x2 * cos + x1 * sin], axis=-1)
    return jnp.concatenate([rot.astype(t.dtype), t[..., ROPE_DIM:]], axis=-1)

def mlstm_chunkwise(q, k, v, i_pre, f_pre):
    B, S, H, Dh = q.shape
    L = MLSTM_CHUNK
    NC = S // L
    f32 = jnp.float32

    def to_chunks(t):
        t = t.reshape((B, NC, L, H) + t.shape[3:])
        return jnp.moveaxis(t, (1, 3), (0, 2))

    qc = to_chunks(q.astype(f32))
    kc = to_chunks(k.astype(f32))
    vc = to_chunks(v.astype(f32))
    igc = to_chunks(i_pre.astype(f32))
    ac = jnp.cumsum(to_chunks(jax.nn.log_sigmoid(f_pre.astype(f32))), axis=-1)
    causal = jnp.tril(jnp.ones((L, L), dtype=bool))

    def step(carry, inp):
        C, n, m = carry
        qj, kj, vj, aj, ij = inp
        g = aj[..., -1]
        dmat = aj[..., :, None] - aj[..., None, :] + ij[..., None, :]
        dmat = jnp.where(causal, dmat, -jnp.inf)
        inter = aj + m[..., None]
        m_row = jnp.maximum(inter, jnp.max(dmat, axis=-1))
        w_intra = jnp.exp(dmat - m_row[..., None])
        w_inter = jnp.exp(inter - m_row)
        s = jnp.einsum('bhld,bhsd->bhls', qj, kj) * w_intra
        num = jnp.einsum('bhls,bhse->bhle', s, vj) + w_inter[..., None] * jnp.einsum('bhld,bhde->bhle', qj, C)
        den = jnp.sum(s, axis=-1) + w_inter * jnp.einsum('bhld,bhd->bhl', qj, n)
        h = num / jnp.maximum(jnp.abs(den), jnp.exp(-m_row))[..., None]
        w_state = g[..., None] - aj + ij
        m_new = jnp.maximum(g + m, jnp.max(w_state, axis=-1))
        decay = jnp.exp(g + m - m_new)
        kw = jnp.exp(w_state - m_new[..., None])[..., None] * kj
        C_new = decay[..., None, None] * C + jnp.einsum('bhld,bhle->bhde', kw, vj)
        n_new = decay[..., None] * n + jnp.sum(kw, axis=2)
        return (C_new, n_new, m_new), h

    init = (jnp.zeros((B, H, Dh, Dh), f32), jnp.zeros((B, H, Dh), f32), jnp.zeros((B, H), f32))
    _, hs = lax.scan(step, init, (qc, kc, vc, ac, igc))
    return hs.transpose(1, 0, 3, 2, 4).reshape(B, S, H, Dh)

def dilated_window_attention(q, k, v, window, dilation):
    B, S, H, Dh = q.shape
    span = window // dilation
    blk = span
    U = S // dilation
    nb = -(-U // blk)
    Up = nb * blk

    def strided(t):
        t = t.reshape(B, U, dilation, H, Dh).transpose(0, 3, 2, 1, 4)
        t = jnp.pad(t, ((0, 0), (0, 0), (0, 0), (0, Up - U), (0, 0)))
        return t.reshape(B, H, dilation, nb, blk, Dh)

    def with_prev(t):
        prev = jnp.pad(t, ((0, 0), (0, 0), (0, 0), (1, 0), (0, 0), (0, 0)))[:, :, :, :nb]
        return jnp.concatenate([prev, t], axis=4)

    qb = strided(q)
    kb = with_prev(strided(k))
    vb = with_prev(strided(v))
    scores = jnp.einsum('bhrnqd,bhrnkd->bhrnqk', qb, kb,
                        preferred_element_type=jnp.float32) * (Dh ** -0.5)
    p = jnp.arange(blk)[:, None]
    sk = jnp.arange(2 * blk)[None, :]
    delta = p + blk - sk
    band = (delta >= 0) & (delta <= span)
    key_u = jnp.arange(nb)[:, None, None] * blk - blk + sk[None]
    valid = band[None] & (key_u >= 0)
    scores = jnp.where(valid, scores, -jnp.inf)
    mx = jnp.max(scores, axis=-1, keepdims=True)
    e = jnp.exp(scores - mx)
    den = jnp.sum(e, axis=-1)
    out = jnp.einsum('bhrnqk,bhrnkd->bhrnqd', e, vb.astype(jnp.float32)) / den[..., None]
    lse = mx[..., 0] + jnp.log(den)
    out = out.reshape(B, H, dilation, Up, Dh)[:, :, :, :U].transpose(0, 3, 2, 1, 4).reshape(B, S, H, Dh)
    lse = lse.reshape(B, H, dilation, Up)[:, :, :, :U].transpose(0, 3, 2, 1).reshape(B, S, H)
    return out, lse

def setup_inputs(seed: int = 0) -> dict:
    key = jax.random.key(seed)
    ks = jax.random.split(key, 20)
    f32 = jnp.float32

    def nrm(k, shape, s):
        return jax.random.normal(k, shape, f32) * s

    x = nrm(ks[0], (BATCH, SEQ, D_MODEL), 1.0)
    c = nrm(ks[1], (BATCH, D_MODEL), 1.0)
    positions = (jax.random.randint(ks[2], (BATCH, 1), 0, 1024) + jnp.arange(SEQ)[None, :]).astype(jnp.int32)
    w_ada = nrm(ks[3], (DEPTH, D_MODEL, 3 * D_MODEL), D_MODEL ** -0.5)
    b_ada = nrm(ks[4], (DEPTH, 3 * D_MODEL), 0.02)
    g_norm = 1.0 + nrm(ks[5], (DEPTH, D_MODEL), 0.02)
    w_in = nrm(ks[6], (DEPTH, D_MODEL, IN_WIDTH), D_MODEL ** -0.5)
    b_igate = nrm(ks[7], (DEPTH, MLSTM_HEADS), 0.1)
    b_fgate = 3.0 + 3.0 * jax.random.uniform(ks[8], (DEPTH, MLSTM_HEADS), f32)
    w_conv = nrm(ks[9], (DEPTH, CONV_WIDTH, MLSTM_WIDTH), CONV_WIDTH ** -0.5)
    b_conv = nrm(ks[10], (DEPTH, MLSTM_WIDTH), 0.02)
    w_q_mlstm = nrm(ks[11], (DEPTH, MLSTM_HEADS, MLSTM_HEAD_DIM, MLSTM_HEAD_DIM), MLSTM_HEAD_DIM ** -0.5)
    w_k_mlstm = nrm(ks[12], (DEPTH, MLSTM_HEADS, MLSTM_HEAD_DIM, MLSTM_HEAD_DIM), MLSTM_HEAD_DIM ** -0.5)
    g_mlstm_head = 1.0 + nrm(ks[13], (DEPTH, MLSTM_HEADS, MLSTM_HEAD_DIM), 0.02)
    skip_mlstm = 1.0 + nrm(ks[14], (DEPTH, MLSTM_WIDTH), 0.02)
    w_out_mlstm = nrm(ks[15], (DEPTH, MLSTM_WIDTH, D_MODEL), MLSTM_WIDTH ** -0.5)
    w_out_attn = nrm(ks[16], (DEPTH, ATTN_OUT_WIDTH, D_MODEL), ATTN_OUT_WIDTH ** -0.5)
    w_out = nrm(ks[17], (DEPTH, D_MODEL, D_MODEL), D_MODEL ** -0.5)
    g_final = 1.0 + nrm(ks[18], (D_MODEL,), 0.02)
    return {'x': x, 'c': c, 'positions': positions, 'w_ada': w_ada, 'b_ada': b_ada,
            'g_norm': g_norm, 'w_in': w_in, 'b_igate': b_igate, 'b_fgate': b_fgate,
            'w_conv': w_conv, 'b_conv': b_conv, 'w_q_mlstm': w_q_mlstm, 'w_k_mlstm': w_k_mlstm,
            'g_mlstm_head': g_mlstm_head, 'skip_mlstm': skip_mlstm, 'w_out_mlstm': w_out_mlstm,
            'w_out_attn': w_out_attn, 'w_out': w_out, 'g_final': g_final}

def reference(x, c, positions, w_ada, b_ada, g_norm, w_in, b_igate, b_fgate, w_conv, b_conv,
              w_q_mlstm, w_k_mlstm, g_mlstm_head, skip_mlstm, w_out_mlstm, w_out_attn, w_out, g_final):
    B, S, _ = x.shape
    f32 = jnp.float32
    split_at = np.cumsum(IN_SPLITS)[:-1].tolist()
    for l in range(DEPTH):
        mod = jax.nn.silu(c) @ w_ada[l] + b_ada[l]
        shift, scale, gate = jnp.split(mod[:, None, :], 3, axis=-1)
        h = rms_norm(x, g_norm[l]) * (1.0 + scale) + shift
        proj = h @ w_in[l]
        xa, va, oa, za, ia, fa, qa, ka, vat, zb, ga, gb = jnp.split(proj, split_at, axis=-1)

        xc = jax.nn.silu(causal_depthwise_conv(xa, w_conv[l], b_conv[l]))
        xc_h = xc.reshape(B, S, MLSTM_HEADS, MLSTM_HEAD_DIM)
        q_m = jnp.einsum('bshd,hde->bshe', xc_h, w_q_mlstm[l])
        k_m = jnp.einsum('bshd,hde->bshe', xc_h, w_k_mlstm[l]) * (MLSTM_HEAD_DIM ** -0.5)
        v_m = va.reshape(B, S, MLSTM_HEADS, MLSTM_HEAD_DIM)
        h_m = mlstm_chunkwise(q_m, k_m, v_m, ia + b_igate[l], fa + b_fgate[l])
        h_m = jax.nn.sigmoid(oa.reshape(B, S, MLSTM_HEADS, MLSTM_HEAD_DIM).astype(f32)) * h_m
        h_m = rms_norm(h_m, g_mlstm_head[l]).reshape(B, S, MLSTM_WIDTH).astype(x.dtype)
        h_m = h_m + skip_mlstm[l] * xc
        y_m = (h_m * jax.nn.silu(za)) @ w_out_mlstm[l]

        qh = partial_rotary(qa.reshape(B, S, ATTN_HEADS, ATTN_HEAD_DIM), positions)
        kh = partial_rotary(ka.reshape(B, S, ATTN_HEADS, ATTN_HEAD_DIM), positions)
        vh = vat.reshape(B, S, ATTN_HEADS, ATTN_HEAD_DIM)
        outs = []
        lses = []
        for gi, (window, dilation) in enumerate(ATTN_GROUPS):
            sl = slice(gi * HEADS_PER_GROUP, (gi + 1) * HEADS_PER_GROUP)
            o_g, lse_g = dilated_window_attention(qh[:, :, sl], kh[:, :, sl], vh[:, :, sl], window, dilation)
            outs.append(o_g)
            lses.append(lse_g)
        wts = jax.nn.softmax(jnp.stack(lses, axis=0), axis=0)
        o_a = jnp.sum(wts[..., None] * jnp.stack(outs, axis=0), axis=0)
        o_a = o_a.reshape(B, S, ATTN_OUT_WIDTH).astype(x.dtype)
        y_a = (o_a * jax.nn.silu(zb)) @ w_out_attn[l]

        merged = jax.nn.sigmoid(ga) * y_m + jax.nn.sigmoid(gb) * y_a
        x = x + gate * (merged @ w_out[l])
    return rms_norm(x, g_final)


_drawn_inputs = setup_inputs


def setup_inputs(seed=0):
    import zlib

    import numpy as np

    out = dict(_drawn_inputs(seed))
    spreads = {}
    factors = {'g_norm': 3.55,
     'b_igate': 64.0,
     'b_conv': 5.349,
     'g_mlstm_head': 64.0,
     'skip_mlstm': 24.437,
     'g_final': 8.685}
    for name, (base, spread) in spreads.items():
        noise = np.random.default_rng([zlib.crc32(name.encode()), seed]).standard_normal(out[name].shape)
        drawn = base * np.exp(spread * noise) if base else spread * noise
        out[name] = __import__('jax').numpy.asarray(drawn.astype(out[name].dtype))
    for name, factor in factors.items():
        out[name] = (out[name] * factor).astype(out[name].dtype)
    return out
```

```python
from contextlib import ExitStack

import numpy as np
import concourse.bass as bass
from concourse import mybir

F32, F32R, I32 = mybir.dt.float32, mybir.dt.float32r, mybir.dt.int32
ACT, ALU, AX = mybir.ActivationFunctionType, mybir.AluOpType, mybir.AxisListType

P = 128
D = 1024
S = 1024
KT = D // P
HALF = 512
HEADS, DH = 4, 256
NCH = S // P
GROUPS = 3
DIL = (1, 4, 16)
ROPE, THETA = 32, 500000.0
EPS = 1e-6
NEG = -1e30
SCALE = 128.0 ** -0.5
KSCALE = DH ** -0.5
MAIN = 18
XA, VA, OA, QKV, ZA, ZB = 0, 2, 4, 6, 15, 17
PI = float(np.pi)


class Steps:

    def __init__(self, eng, sem, turn=0, per_turn=0):
        self.eng, self.sem, self.base, self.per, self.n = eng, sem, turn * per_turn, per_turn, 0

    def __call__(self, ins):
        self.n += 1
        ins.then_inc(self.sem, 1)
        self.eng.wait_ge(self.sem, self.base + self.n)

    def end(self):
        assert not self.per or self.n == self.per, self.n


def order(ap, g, lo=0, n=S):
    return ap[:, lo:lo + n].rearrange("p (u r) -> p r u", r=DIL[g])


def stored(ap, g, lo=0, n=S):
    d = DIL[g]
    return ap.rearrange("p (r u) -> p r u", r=d)[:, :, lo // d:(lo + n) // d]


def build(nc, a, out):
    with ExitStack() as top:
        def sem(name):
            return top.enter_context(nc.semaphore(name))

        def sb(name, shape, dt=F32, ctx=top):
            return ctx.enter_context(nc.sbuf_tensor(name, shape, dt))

        def dram(name, shape):
            return nc.dram_tensor(name, shape, F32, kind="Internal").ap()

        ps = top.enter_context(nc.psum_tensor("banks", [P, 8, HALF], F32))
        mod_d = dram("mod_rows", [1, 3 * D])
        r1_d = dram("log_weight_rows", [HEADS, S])
        wi_d = dram("chunk_decay_rows", [HEADS, NCH])
        stat_d = dram("softmax_stats", [GROUPS, S, 2])
        coef_d = dram("group_weights", [GROUPS, S])
        um_d = dram("mlstm_branch", [HEADS, 2, P, S])
        ua_d = dram("attn_branch", [HEADS, P, S])
        mg_d = dram("merged", [KT, P, S])

        ident = sb("ident", [P, P])
        zero = sb("zero", [P, 1])
        band = sb("band", [P, 2 * P])
        diag = sb("diag", [P, P])

        h_ctx = top.enter_context(ExitStack())
        h_hi = sb("h_hi", [P, KT, S], F32R, h_ctx)
        h_lo = sb("h_lo", [P, KT, S], F32R, h_ctx)
        mix_ctx = h_ctx.enter_context(ExitStack())
        cols = sb("gate_cols", [P, NCH, 4, HEADS], F32, mix_ctx)
        cosT = sb("cosT", [ROPE, S], F32, mix_ctx)
        sinT = sb("sinT", [ROPE, S], F32, mix_ctx)
        setup(nc, a, sem, sb, ps, locals())
        mix(nc, a, sem, sb, ps, locals())
        mix_ctx.close()
        merge(nc, a, sem, sb, ps, locals())
        h_ctx.close()
        finish(nc, a, out, sem, sb, ps, locals())


def setup(nc, a, sem, sb, ps, T):
    ident, zero, band, diag = T["ident"], T["zero"], T["band"], T["diag"]
    h_hi, h_lo, cols, cosT, sinT = T["h_hi"], T["h_lo"], T["cols"], T["cosT"], T["sinT"]
    mod_d, r1_d, wi_d = T["mod_d"], T["r1_d"], T["wi_d"]
    NA = 3
    with ExitStack() as ctx:
        def buf(name, shape, dt=F32):
            return sb(name, shape, dt, ctx)

        xnT = buf("xnT", [P, KT, S])
        xt = buf("xt", [P, 2, D])
        sq = buf("sq", [P, D])
        wada = buf("wada", [P, NA, 3 * D])
        brow = buf("brow", [1, 3 * D])
        modrow = buf("modrow", [1, 3 * D])
        cc = buf("cc", [P, 4, KT])
        gn = buf("gn", [P, KT])
        ms = buf("ms", [P, 3, KT])
        one = buf("one", [1, 1])
        xs = buf("xs", [P, 6, KT])
        gb = buf("gb", [P, 2])
        rc = buf("rc", [ROPE, 2])
        halfpi = buf("halfpi", [P, 1])
        posi = buf("posi", [ROPE, S], I32)
        wraw = buf("wraw_g", [P, KT, P])
        whi = buf("whi_g", [P, KT, P], F32R)
        wlo = buf("wlo_g", [P, KT, P], F32R)

        small_in, c_in, x_in, pos_in = sem("small_in"), sem("c_in"), [sem("x_in0"), sem("x_in1")], sem("pos_in")
        ada_in = [sem(f"ada_in{j}") for j in range(NA)]
        ada_used, gw_in, gw_split = sem("ada_used"), sem("gw_in"), sem("gw_split")
        consts = sem("consts")
        c_exp, c_silu = sem("c_exp"), sem("c_silu")
        x_sq, x_ln, x_norm, x_turned, x_kept = sem("x_sq"), sem("x_ln"), sem("x_norm"), sem("x_turned"), sem("x_kept")
        x_var = sem("x_var")
        mod_row, mod_col, h_full, h_ready = (sem(n) for n in ("mod_row", "mod_col", "h_full", "h_ready"))
        ms_ready = sem("ms_ready")
        g_ready, dve_s, act_s, pool_s = sem("g_ready"), sem("dve_setup"), sem("act_setup"), sem("pool_setup")
        setup_out = sem("setup_out")
        rope_arg, rope_abs = sem("rope_arg"), sem("rope_abs")
        gate_abs, gate_ls, gate_arg, gate_exp, gate_min = (sem(n) for n in ("gate_abs", "gate_ls", "gate_arg", "gate_exp", "gate_min"))
        cols_ready = sem("cols_ready")
        rows_ready = sem("rows_ready")

        block = ctx.enter_context(nc.Block())

        @block.sync
        def _(sp):
            sp.dma_start(cc[:, 0, :], a["c_cols"]).then_inc(c_in, 16)
            for k in range(KT):
                if k >= NA:
                    sp.wait_ge(ada_used, k - NA + 1)
                sp.dma_start(wada[:, k % NA, :], a["w_ada"][k * P:(k + 1) * P, :]).then_inc(ada_in[k % NA], 16)
            sp.dma_start(wraw[:], a["w_gates"].rearrange("p (k c) -> p k c", k=KT)).then_inc(gw_in, 16)
            sp.wait_ge(mod_row, 6)
            sp.dma_start(mod_d, modrow[:]).then_inc(setup_out, 16)
            sp.wait_ge(gate_arg, 1)
            sp.dma_start(r1_d, xnT[0:HEADS, 4, :]).then_inc(setup_out, 16)
            sp.wait_ge(rows_ready, 2)
            sp.dma_start(wi_d, sq[0:HEADS, 0:NCH]).then_inc(setup_out, 16)
            sp.wait_ge(setup_out, 48)

        @block.gpsimd
        def _(pool):
            nc.gpsimd.memset(zero[:], 0.0).then_inc(pool_s, 1)
            nc.gpsimd.memset(ident[:], 0.0).then_inc(pool_s, 1)
            nc.gpsimd.memset(band[:], 0.0).then_inc(pool_s, 1)
            nc.gpsimd.memset(diag[:], 0.0).then_inc(pool_s, 1)
            nc.gpsimd.memset(one[:], 1.0).then_inc(pool_s, 1)
            nc.gpsimd.memset(halfpi[:], PI / 2).then_inc(pool_s, 1)
            pool.wait_ge(pool_s, 6)
            nc.gpsimd.affine_select(out=ident[:], in_=ident[:], compare_op=ALU.not_equal, fill=1.0, base=0,
                                    pattern=[[-1, P]], channel_multiplier=1).then_inc(consts, 1)
            nc.gpsimd.affine_select(out=band[:, 0:P], in_=band[:, 0:P], compare_op=ALU.is_ge, fill=NEG, base=0,
                                    pattern=[[1, P]], channel_multiplier=-1).then_inc(consts, 1)
            nc.gpsimd.affine_select(out=band[:, P:], in_=band[:, P:], compare_op=ALU.is_ge, fill=NEG, base=0,
                                    pattern=[[-1, P]], channel_multiplier=1).then_inc(consts, 1)
            nc.gpsimd.affine_select(out=diag[:], in_=diag[:], compare_op=ALU.is_ge, fill=NEG, base=0,
                                    pattern=[[-1, P]], channel_multiplier=1).then_inc(consts, 1)
            pool.wait_ge(consts, 4)
            nc.gpsimd.memset(diag[64:128, 0:64], NEG).then_inc(consts, 1)
            pool.wait_ge(consts, 5)
            pool.wait_ge(gw_in, 16)
            nc.gpsimd.tensor_tensor(whi[:], wraw[:], zero[:].unsqueeze(2).broadcast_to([P, KT, P]), ALU.add).then_inc(gw_split, 1)
            pool.wait_ge(gw_split, 1)
            nc.gpsimd.tensor_tensor(wlo[:], wraw[:], whi[:].bitcast(F32), ALU.subtract).then_inc(gw_split, 1)

        @block.scalar
        def _(act):
            step = Steps(act, act_s)
            act.dma_start(xt[:, 0, :], a["x"][0:P, :]).then_inc(x_in[0], 16)
            act.dma_start(xt[:, 1, :], a["x"][P:2 * P, :]).then_inc(x_in[1], 16)
            act.dma_start(brow[:], a["b_ada"]).then_inc(small_in, 16)
            act.dma_start(gn[:], a["g_cols"]).then_inc(small_in, 16)
            act.dma_start(gb[:], a["gate_bias"]).then_inc(small_in, 16)
            act.dma_start(rc[:], a["rope_const"]).then_inc(small_in, 16)
            act.dma_start(posi[:], a["positions"].partition_broadcast(ROPE)).then_inc(pos_in, 16)
            act.wait_ge(c_in, 16)
            nc.scalar.activation(cc[:, 1, :], cc[:, 0, :], ACT.Exp, scale=-1.0).then_inc(c_exp, 1)
            for t in range(NCH):
                act.wait_ge(x_in[t % 2], 16 * (t // 2 + 1))
                if t:
                    act.wait_ge(x_sq, t)
                nc.scalar.activation(sq[:], xt[:, t % 2, :], ACT.Square, accum_out=xs[:, 0, t:t + 1]).then_inc(x_sq, 1)
                act.wait_ge(x_var, t + 1)
                step(nc.scalar.activation(xs[:, 2, t:t + 1], xs[:, 1, t:t + 1], ACT.Ln))
                nc.scalar.activation(xs[:, 3, t:t + 1], xs[:, 2, t:t + 1], ACT.Exp, scale=-0.5).then_inc(x_ln, 1)
                if t + 2 < NCH:
                    act.wait_ge(x_norm, t + 1)
                    act.wait_ge(x_turned, t + 1)
                    act.dma_start(xt[:, t % 2, :], a["x"][(t + 2) * P:(t + 3) * P, :]).then_inc(x_in[t % 2], 16)
            act.wait_ge(ms_ready, 1)
            act.wait_ge(x_kept, 2 * NCH)
            for k in range(KT):
                nc.scalar.activation(xnT[:, k, :], xnT[:, k, :], ACT.Identity, scale=ms[:, 0, k:k + 1],
                                     bias=ms[:, 1, k:k + 1]).then_inc(h_full, 1)
            act.wait_ge(rope_arg, 1)
            act.wait_ge(consts, 5)
            nc.scalar.activation(sinT[:], sq[0:ROPE, :], ACT.Sin).then_inc(rope_abs, 1)
            step(nc.scalar.activation(xt[0:ROPE, 1, :], sq[0:ROPE, :], ACT.Abs))
            nc.scalar.activation(cosT[:], xt[0:ROPE, 1, :], ACT.Sin, scale=-1.0, bias=halfpi[0:ROPE, :]).then_inc(rope_abs, 1)
            act.wait_ge(g_ready, 2)
            act.wait_ge(h_ready, 2 * KT)
            nc.scalar.activation(xnT[0:HEADS, 0, :], ps[0:HEADS, 0:2, :], ACT.Identity, bias=gb[0:HEADS, 0:1])\
                .then_inc(gate_abs, 1)
            nc.scalar.activation(xnT[0:HEADS, 2, :], ps[32:32 + HEADS, 0:2, :], ACT.Abs, bias=gb[32:32 + HEADS, 1:2])\
                .then_inc(gate_abs, 1)
            act.wait_ge(gate_abs, 2)
            step(nc.scalar.activation(xnT[0:HEADS, 2, :], xnT[0:HEADS, 2, :], ACT.Exp, scale=-1.0))
            nc.scalar.activation(xnT[0:HEADS, 2, :], xnT[0:HEADS, 2, :], ACT.Ln, bias=1.0).then_inc(gate_ls, 1)
            act.wait_ge(gate_arg, 2)
            nc.scalar.activation(xnT[0:HEADS, 1, :], xnT[0:HEADS, 1, :], ACT.Exp).then_inc(rows_ready, 1)
            act.wait_ge(rows_ready, 1)
            nc.scalar.copy(sq[0:HEADS, 0:NCH], xnT[0:HEADS, 1, P - 1::P]).then_inc(rows_ready, 1)
            nc.scalar.activation(xnT[0:HEADS, 2, :], xnT[0:HEADS, 2, :], ACT.Exp, scale=-1.0).then_inc(gate_exp, 1)
            nc.scalar.activation(xnT[0:HEADS, 3, :], xnT[0:HEADS, 3, :], ACT.Exp).then_inc(gate_exp, 1)

        @block.vector
        def _(dve):
            step = Steps(dve, dve_s)
            v = nc.vector
            dve.wait_ge(c_exp, 1)
            step(v.tensor_scalar(cc[:, 2, :], cc[:, 1, :], 1.0, None, ALU.add))
            step(v.reciprocal(cc[:, 3, :], cc[:, 2, :]))
            v.tensor_tensor(cc[:, 1, :], cc[:, 0, :], cc[:, 3, :], ALU.mult).then_inc(c_silu, 1)
            for t in range(NCH):
                dve.wait_ge(x_sq, t + 1)
                v.tensor_scalar(xs[:, 1, t:t + 1], xs[:, 0, t:t + 1], 1.0 / D, EPS, ALU.mult, ALU.add).then_inc(x_var, 1)
                dve.wait_ge(x_ln, t + 1)
                dve.wait_ge(x_var, t + 1)
                r, w = xs[:, 3, t:t + 1], xs[:, 4, t:t + 1]
                step(v.scalar_tensor_tensor(w, r, xs[:, 1, t:t + 1], r, ALU.mult, ALU.mult))
                step(v.tensor_scalar(w, w, -0.5, 1.5, ALU.mult, ALU.add))
                step(v.tensor_tensor(xs[:, 5, t:t + 1], r, w, ALU.mult))
                v.tensor_scalar(xt[:, t % 2, :], xt[:, t % 2, :], xs[:, 5, t:t + 1], None, ALU.mult).then_inc(x_norm, 1)
                for h in range(2):
                    dve.wait_ge(x_turned, t + 1)
                    v.tensor_copy(xnT[:, 4 * h:4 * h + 4, t * P:(t + 1) * P],
                                  ps[:, 6 + h, :].rearrange("p (k c) -> p k c", k=4)).then_inc(x_kept, 1)
            dve.wait_ge(small_in, 64)
            dve.wait_ge(pos_in, 16)
            dve.wait_ge(x_sq, NCH)
            ang, kk, tmp = xt[0:ROPE, 0, :], xt[0:ROPE, 1, :], sq[0:ROPE, :]
            dve.wait_ge(x_turned, NCH)
            step(v.tensor_copy(tmp, posi[:]))
            step(v.tensor_scalar(ang, tmp, rc[:, 0:1], None, ALU.mult))
            step(v.tensor_scalar(kk, ang, 1.0 / (2 * PI), 12582912.0, ALU.mult, ALU.add))
            step(v.tensor_scalar(kk, kk, 12582912.0, None, ALU.subtract))
            c1 = 6.28125
            c2 = float(np.float32(np.round((2 * PI - c1) * 2 ** 19) / 2 ** 19))
            c3 = float(np.float32(2 * PI - c1 - c2))
            for c in (c1, c2, c3):
                step(v.scalar_tensor_tensor(ang, kk, -c, ang, ALU.mult, ALU.add))
            v.tensor_scalar(tmp, ang, 3.1415925, -3.1415925, ALU.min, ALU.max).then_inc(rope_arg, 1)
            dve.wait_ge(ada_used, KT)
            for n in range(6):
                v.tensor_tensor(modrow[:, n * HALF:(n + 1) * HALF], ps[0:1, n, :], brow[:, n * HALF:(n + 1) * HALF],
                                ALU.add).then_inc(mod_row, 1)
            dve.wait_ge(mod_col, 1)
            step(v.tensor_scalar(ms[:, 2, :], ps[:, 7, KT:2 * KT], 1.0, None, ALU.add))
            step(v.tensor_copy(ms[:, 1, :], ps[:, 7, 0:KT]))
            v.tensor_tensor(ms[:, 0, :], ms[:, 2, :], gn[:], ALU.mult).then_inc(ms_ready, 1)
            for k in range(KT):
                dve.wait_ge(h_full, k + 1)
                v.tensor_copy(h_hi[:, k, :], xnT[:, k, :]).then_inc(h_ready, 1)
                dve.wait_ge(h_ready, 2 * k + 1)
                v.tensor_tensor(h_lo[:, k, :], xnT[:, k, :], h_hi[:, k, :].bitcast(F32), ALU.subtract).then_inc(h_ready, 1)
            dve.wait_ge(rope_abs, 2)
            step(v.tensor_scalar(sinT[:], sinT[:], rc[:, 1:2], None, ALU.mult))
            row = lambda j: xnT[0:HEADS, j, :]
            by_chunk = lambda j: row(j).rearrange("p (c t) -> p c t", c=NCH)
            last = lambda j: by_chunk(j)[:, :, P - 1:P]
            dve.wait_ge(gate_abs, 2)
            step(v.memset(row(6), 1.0))
            step(v.memset(by_chunk(6)[:, :, 0:1], 0.0))
            step(v.tensor_scalar(row(7), ps[32:32 + HEADS, 0:2, :], gb[32:32 + HEADS, 1:2], 0.0, ALU.add, ALU.min))
            dve.wait_ge(gate_ls, 1)
            step(v.tensor_tensor(row(7), row(7), row(2), ALU.subtract))
            step(v.tensor_tensor_scan(row(5), row(6), row(7), 0.0, ALU.mult, ALU.add))
            step(v.tensor_tensor_scan(row(2), row(7), row(0), 0.0, ALU.add, ALU.max))
            step(v.tensor_tensor(row(4), row(5), row(2), ALU.subtract))
            step(v.memset(row(6)[:, 0:NCH], 0.0))
            step(v.tensor_copy(row(6)[:, 1:NCH], row(2)[:, P - 1:S - P:P]))
            v.tensor_tensor(by_chunk(1), by_chunk(4), row(6)[:, 0:NCH].unsqueeze(2).broadcast_to([HEADS, NCH, P]),
                            ALU.add).then_inc(gate_arg, 1)
            step(v.tensor_tensor(row(0), row(0), row(5), ALU.subtract))
            v.tensor_tensor(by_chunk(3), by_chunk(0), last(4).broadcast_to([HEADS, NCH, P]), ALU.add).then_inc(gate_arg, 1)
            dve.wait_ge(cols_ready, 1)
            v.tensor_copy(cols[:], ps[:, 2, 0:P].rearrange("p (c q h) -> p c q h", c=NCH, q=4)).then_inc(dve_s, 1)

        @block.tensor
        def _(pe):
            t_ = nc.tensor
            pe.wait_ge(consts, 1)
            pe.wait_ge(c_silu, 1)
            for k in range(KT):
                pe.wait_ge(ada_in[k % NA], 16 * (k // NA + 1))
                for n in range(6):
                    mm = t_.matmul(ps[0:1, n, :], cc[:, 1, k:k + 1], wada[:, k % NA, n * HALF:(n + 1) * HALF],
                                   start=(k == 0), stop=(k == KT - 1))
                mm.then_inc(ada_used, 1)
                pe.wait_ge(x_norm, k + 1)
                if k:
                    pe.wait_ge(x_kept, 2 * k)
                for d in range(KT):
                    mm = t_.transpose(ps[:, 6 + d // 4, (d % 4) * P:(d % 4 + 1) * P], xt[:, k % 2, d * P:(d + 1) * P],
                                      ident[:])
                mm.then_inc(x_turned, 1)
            pe.wait_ge(x_kept, 2 * NCH)
            for j in range(2 * KT):
                if j % 4 == 0:
                    pe.wait_ge(mod_row, j // 4 + 1)
                mm = t_.matmul(ps[:, 7, j:j + 1], modrow[:, j * P:(j + 1) * P], one[:], start=True, stop=True)
            mm.then_inc(mod_col, 1)
            pe.wait_ge(gw_split, 2)
            pe.wait_ge(mod_row, 6)
            for h in range(2):
                for k in range(KT):
                    if h == 0:
                        pe.wait_ge(h_ready, 2 * k + 2)
                    mm = three_pass(t_, ps[:, h, :], whi[:, k, :], wlo[:, k, :], h_hi[:, k, h * HALF:(h + 1) * HALF],
                                    h_lo[:, k, h * HALF:(h + 1) * HALF], k == 0, k == KT - 1)
                mm.then_inc(g_ready, 1)
            pe.wait_ge(gate_exp, 2)
            pe.wait_ge(rows_ready, 1)
            for c in range(NCH):
                for q in range(4):
                    mm = t_.transpose(ps[:, 2, (c * 4 + q) * 4:(c * 4 + q) * 4 + 4], xnT[0:HEADS, q, c * P:(c + 1) * P],
                                      ident[0:HEADS, 0:HEADS])
            mm.then_inc(cols_ready, 1)


def three_pass(t_, out, w_hi, w_lo, x_hi, x_lo, first, last):
    t_.matmul(out, w_hi, x_hi, start=first, stop=False)
    t_.matmul(out, w_hi, x_lo, start=False, stop=False)
    return t_.matmul(out, w_lo, x_hi, start=False, stop=last)


def mix(nc, a, sem, sb, ps, T):
    ident, zero, band, diag = T["ident"], T["zero"], T["band"], T["diag"]
    h_hi, h_lo, cols, cosT, sinT = T["h_hi"], T["h_lo"], T["cols"], T["cosT"], T["sinT"]
    r1_d, wi_d, stat_d, coef_d, um_d, ua_d = (T[n] for n in ("r1_d", "wi_d", "stat_d", "coef_d", "um_d", "ua_d"))
    DVE_STEPS = 69
    M0, M1, M2, A0, A1, A2 = (ps[:, b, :] for b in range(2, 8))
    with ExitStack() as ctx:
        def buf(name, shape, dt=F32):
            return sb(name, shape, dt, ctx)

        wraw = buf("wraw", [P, 2, D])
        whi = buf("whi", [P, 2, D], F32R)
        wlo = buf("wlo", [P, 2, D], F32R)
        hpa = buf("head_params_all", [P, HEADS, 2, 8])
        hp = buf("head_params", [P, 2, 8])
        hc = buf("head_cols", [P, NCH, 4])
        turn = buf("turned_from", [P, 2, 3 + S])
        cv = buf("conv", [P, S])
        sg = buf("sig", [P, S])
        xc = buf("xc", [P, 2, S])
        v1 = buf("v_and_ones", [P, NCH, DH + 2])
        og = buf("gated_out", [P, NCH, DH])
        qm = buf("q_mlstm", [P, 2, S])
        km = buf("k_mlstm", [P, 2, S])
        wqk = buf("wqk", [P, 2, 2, DH])
        ew = buf("intra_weights", [P, NCH, P])
        dec = buf("chunk_decay", [P, NCH])
        sw = buf("weighted_scores", [P, 2, P])
        kw = buf("weighted_keys", [P, 2, DH])
        cst = buf("state", [P, 2, DH + 1])
        hin = buf("inter_part", [P, DH + 1])
        hnb = buf("numerator", [P, DH + 1])
        small = buf("small", [P, 4])
        vr = buf("variances", [P, 6, NCH])
        qa = buf("qk_attn", [P, 2, 2, S])
        vt = buf("v_attn", [P, NCH, P])
        sm = buf("softmax", [P, 2, 2, 2 * P])
        pT = buf("probs_turned", [P, 2, 2, P])
        nm = buf("minus_max", [P, 2, 2])
        st = buf("stats", [P, GROUPS, NCH, 2])
        num1 = buf("num1", [P, S])
        ct = buf("stats_by_token", [P, GROUPS, NCH, 2])
        cw = buf("weights_by_token", [P, 4, GROUPS, NCH])
        og_flat = og[:].rearrange("p c e -> p (c e)")
        szb = og_flat[:, 0:S]
        num = [cv[:], num1[:], km[:, 1, :]]
        cb = [qm[:, 0, :], qm[:, 1, :], km[:, 0, :]]
        tn = [turn[:, b, 3:3 + S] for b in range(2)]

        w_in = [sem("w_in0"), sem("w_in1")]
        w_split, pool_s, proj, hp_in = sem("w_split"), sem("pool_mix"), sem("proj"), sem("hp_in")
        kept = [sem("kept0"), sem("kept1")]
        ready = sem("mix_ready")
        conv_done, conv_sig, xc_done, e_in, dec_in, wqk_in = (sem(n) for n in ("conv_done", "conv_sig", "xc_done", "e_in", "dec_in", "wqk_in"))
        e_arg, e_exp, turned, turned_kept, qk_out, qk_kept = (sem(n) for n in ("e_arg", "e_exp", "turned", "turned_kept", "qk_out", "qk_kept"))
        sk_out, sw_done, num_out, inter_kept, num_kept, gated = (sem(n) for n in ("sk_out", "sw_done", "num_out", "inter_kept", "num_kept", "gated"))
        squares, upd_out, state_done, var_done, ln_done, normed = (sem(n) for n in ("squares", "upd_out", "state_done", "var_done", "ln_done", "normed"))
        out_turned, out_used, z_sig, um_done, dve_s, act_s = (sem(n) for n in ("out_turned", "out_used", "z_sig", "um_done", "dve_mix", "act_mix"))
        um_out = [sem("um_out0"), sem("um_out1")]
        roped, v_turned, v_kept, score_out, masked, max_done = (sem(n) for n in ("roped", "v_turned", "v_kept", "score_out", "masked", "max_done"))
        exp_done, p_turned, p_kept, pv_out, pv_kept = (sem(n) for n in ("exp_done", "p_turned", "p_kept", "pv_out", "pv_kept"))
        stat_out = [sem(f"stat_out{g}") for g in range(GROUPS)]
        ct_in, ct_arg, ct_exp, cw_done, coef_out, ua_done, ua_out = (sem(n) for n in ("ct_in", "ct_arg", "ct_exp", "cw_done", "coef_out", "ua_done", "ua_out"))
        cb_in = [sem(f"cb_in{g}") for g in range(GROUPS)]

        block = ctx.enter_context(nc.Block())

        def stat_dest(g):
            if g == 0:
                return [(st[:, 0], stat_d[0].rearrange("(c p) w -> p c w", p=P))]
            if g == 1:
                x = stat_d[1].rearrange("(b p r) w -> r p b w", p=P, r=4)
                return [(st[:, 1, 2 * r:2 * r + 2, :], x[r]) for r in range(4)]
            x = stat_d[2].rearrange("(u c h) w -> h u c w", c=NCH, h=2)
            return [(st[64 * h:64 * h + 64, 2], x[h]) for h in range(2)]

        STATS = (1, 4, 2)

        @block.sync
        def _(sp):
            sp.dma_start(hpa[:], a["head_params"]).then_inc(hp_in, 16)
            for b in range(2):
                sp.sem_inc(um_out[b], 16)
            sp.sem_inc(ua_out, 16)
            with sp.Fori(0, HEADS) as i:
                sp.wait_ge(normed, i + 1)
                sp.dma_start(wqk[:], a["w_qk"][bass.ds(i, 1)].rearrange("o p j k e -> (o p) j k e")).then_inc(wqk_in, 16)
                sp.dma_start(ew[:].rearrange("p c t -> p (c t)"), r1_d[bass.ds(i, 1), :].broadcast_to([P, S])).then_inc(e_in, 16)
                sp.dma_start(dec[:], wi_d[bass.ds(i, 1), :].broadcast_to([P, NCH])).then_inc(dec_in, 16)
                for n in range(MAIN):
                    sp.wait_ge(w_split, i * MAIN + n + 1)
                    sp.dma_start(wraw[:, n % 2, :], a["w_main"][bass.ds(i, 1), n].rearrange("o p c -> (o p) c"))\
                      .then_inc(w_in[n % 2], 16)
                    if n in (12, 15):
                        g = (n - 12) // 3
                        sp.wait_ge(exp_done, i * 24 + 8 * g + 8)
                        for src, dst in stat_dest(g):
                            sp.dma_start(dst, src).then_inc(stat_out[g], 16)
                    if n == 17:
                        for q in range(2):
                            sp.wait_ge(um_done, i * 2 + q + 1)
                            sp.dma_start(um_d[bass.ds(i, 1), q].rearrange("o p s -> (o p) s"), xc[:, q, :]).then_inc(um_out[q], 16)
            sp.wait_ge(um_out[0], 16 * HEADS + 16)
            sp.wait_ge(um_out[1], 16 * HEADS + 16)

        @block.gpsimd
        def _(pool):
            pool.sem_inc(w_split, 2)
            with pool.Fori(0, HEADS) as i:
                for n in range(MAIN):
                    raw, hi, lo = wraw[:, n % 2, :], whi[:, n % 2, :], wlo[:, n % 2, :]
                    pool.wait_ge(proj, i * 2 * MAIN + 2 * n + 2)
                    pool.wait_ge(w_in[n % 2], (i * (MAIN // 2) + n // 2 + 1) * 16)
                    nc.gpsimd.tensor_tensor(hi, raw, zero[:].broadcast_to([P, D]), ALU.add).then_inc(pool_s, 1)
                    pool.wait_ge(pool_s, i * MAIN + n + 1)
                    nc.gpsimd.tensor_tensor(lo, raw, hi.bitcast(F32), ALU.subtract).then_inc(w_split, 1)

        def blocks(g, tile):
            return 2 if (g == 0 and tile > 0) or (g == 1 and tile % 2 == 1) else 1

        @block.tensor
        def _(pe):
            t_ = nc.tensor
            pe.sem_inc(proj, 4)

            with pe.Fori(0, HEADS) as i:
                def project(n, h):
                    pe.wait_ge(w_split, i * MAIN + n + 3)
                    pe.wait_ge(kept[h], i * MAIN + n + 1)
                    for k in range(KT):
                        mm = three_pass(t_, ps[:, h, :], whi[:, n % 2, k * P:(k + 1) * P], wlo[:, n % 2, k * P:(k + 1) * P],
                                        h_hi[:, k, h * HALF:(h + 1) * HALF], h_lo[:, k, h * HALF:(h + 1) * HALF],
                                        k == 0, k == KT - 1)
                    mm.then_inc(proj, 1)

                def chunk_kept(n):
                    for h in range(2):
                        pe.wait_ge(kept[h], i * MAIN + n + 2)

                def turn_chunk(n):
                    chunk_kept(n)
                    if n == VA:
                        pe.wait_ge(masked, i * 24 + 1)
                        pe.wait_ge(p_kept, i * 12 + 1)
                    for j in range(2):
                        m = (n - VA) * 2 + j
                        pe.wait_ge(turned_kept, i * 8 + m + 1)
                        for c in range(4):
                            mm = t_.transpose((A0, A1)[j][:, c * P:(c + 1) * P], tn[n % 2][:, (4 * j + c) * P:(4 * j + c + 1) * P],
                                              ident[:])
                        mm.then_inc(turned, 1)

                def head_qk(js):
                    pe.wait_ge(wqk_in, (i + 1) * 16)
                    pe.wait_ge(xc_done, i * 2 + 2)
                    pe.wait_ge(out_used, i * 4 + 4)
                    for j in js:
                        pe.wait_ge(qk_kept, i * 8 + j + 1)
                        w, e, h = j // 4, j // 2 % 2, j % 2
                        for d in range(2):
                            mm = t_.matmul((M0, M1)[h], wqk[:, w, d, e * P:(e + 1) * P], xc[:, d, h * HALF:(h + 1) * HALF],
                                           start=(d == 0), stop=(d == 1))
                        mm.then_inc(qk_out, 1)

                def scores_and_keys(c):
                    pe.wait_ge(qk_kept, i * 8 + 10)
                    if c:
                        pe.wait_ge(sw_done, i * 16 + 2 * c)
                    cs = slice(c * P, (c + 1) * P)
                    for d in range(2):
                        t_.matmul(M0[:, 0:P], km[:, d, cs], qm[:, d, cs], start=(d == 0), stop=(d == 1))
                    for d in range(2):
                        mm = t_.matmul(M0[:, P:P + DH], xc[:, d, cs], wqk[:, 1, d, :], start=(d == 0), stop=(d == 1))
                    mm.then_inc(sk_out, 1)

                def numerator(c):
                    pe.wait_ge(sw_done, i * 16 + 2 * c + 2)
                    if c:
                        pe.wait_ge(state_done, i * 14 + 2 * c)
                    t_.matmul(M1[:, 0:DH + 1], sw[:, c % 2, :], v1[:, c, 0:DH + 1], start=True, stop=True)
                    for d in range(2):
                        mm = t_.matmul(M2[:, 0:DH + 1], qm[:, d, c * P:(c + 1) * P], cst[:, d, :], start=(d == 0), stop=(d == 1))
                    mm.then_inc(num_out, 1)

                def state_update(c):
                    pe.wait_ge(num_kept, i * 8 + c + 2)
                    for d in range(2):
                        mm = t_.matmul((M1, M2)[d][:, 0:DH + 1], kw[:, c % 2, d * P:(d + 1) * P], v1[:, c, 0:DH + 1],
                                       start=True, stop=True)
                    mm.then_inc(upd_out, 1)

                def turn_output():
                    pe.wait_ge(normed, i + 2)
                    for j in range(4):
                        if j == 3:
                            pe.wait_ge(out_used, i * 4 + 5)
                        for c in range(4):
                            mm = t_.transpose((M0, M1, M2, M0)[j][:, c * P:(c + 1) * P],
                                              og[:, 4 * (j % 2) + c, (j // 2) * P:(j // 2 + 1) * P], ident[:])
                        mm.then_inc(out_turned, 1)

                def turn_values(g):
                    chunk_kept(8 + 3 * g)
                    pe.wait_ge(turned_kept, i * 8 + 10)
                    pe.wait_ge(p_kept, i * 12 + 4 * g + 1)
                    pe.wait_ge(pv_kept, i * 12 + 4 * g + 1)
                    for j in range(2):
                        for c in range(4):
                            k = 4 * j + c
                            mm = t_.transpose((A1, A2)[j][:, c * P:(c + 1) * P], tn[g % 2][:, k * P:(k + 1) * P], ident[:])
                        mm.then_inc(v_turned, 1)

                def attend(g, x):
                    if x == 0:
                        turn_values(g)
                    if x < 4:
                        pe.wait_ge(roped, i * 6 + 2 * g + 2)
                        pe.wait_ge(masked, i * 24 + 8 * g + 2 * x + 1)
                        for u in range(2):
                            t, b = 2 * x + u, blocks(g, 2 * x + u)
                            mm = t_.matmul(A0[:, u * 2 * P:u * 2 * P + b * P], qa[:, g % 2, 0, t * P:(t + 1) * P],
                                           qa[:, g % 2, 1, (t + 1 - b) * P:(t + 1) * P], start=True, stop=True)
                        mm.then_inc(score_out, 1)
                    if x >= 2:
                        pe.wait_ge(p_kept, i * 12 + 4 * g + x)
                        pe.wait_ge(v_kept, i * 6 + 2 * g + 2)
                        pe.wait_ge(pv_kept, i * 12 + 4 * g + x - 1)
                        for u in range(2):
                            t, b = 2 * (x - 2) + u, blocks(g, 2 * (x - 2) + u)
                            for j in range(b):
                                mm = t_.matmul(A2[:, u * P:(u + 1) * P], vt[:, t + 1 - b + j, :], pT[:, u, j, :],
                                               start=(j == 0), stop=(j == b - 1))
                        mm.then_inc(pv_out, 1)
                    if 1 <= x <= 4:
                        pe.wait_ge(exp_done, i * 24 + 8 * g + 2 * x)
                        pe.wait_ge(p_kept, i * 12 + 4 * g + x)
                        pe.wait_ge(v_kept, i * 6 + 2 * g + 2)
                        for u in range(2):
                            for j in range(blocks(g, 2 * (x - 1) + u)):
                                mm = t_.transpose(A1[:, (2 * u + j) * P:(2 * u + j + 1) * P],
                                                  sm[:, (x - 1) % 2, u, j * P:(j + 1) * P], ident[:])
                        mm.then_inc(p_turned, 1)

                for n in range(MAIN):
                    c, g = n - 7, (n - 9) // 3
                    project(n, 0)
                    if 3 <= n <= 6:
                        turn_chunk(n - 1)
                    if n == 4:
                        head_qk(range(0, 4))
                    if n == 5:
                        head_qk(range(4, 8))
                    if n == 6:
                        scores_and_keys(0)
                    if 0 <= c < NCH:
                        numerator(c)
                    if n >= 9:
                        attend(g, 2 * (n - 9 - 3 * g))
                    project(n, 1)
                    if 0 <= c < NCH - 1:
                        state_update(c)
                        scores_and_keys(c + 1)
                    if n == 15:
                        turn_output()
                    if n >= 9:
                        attend(g, 2 * (n - 9 - 3 * g) + 1)

        @block.scalar
        def _(act):
            A = nc.scalar.activation
            for h in range(2):
                act.sem_inc(kept[h], 1)
            act.sem_inc(qk_kept, 2)
            act.sem_inc(pv_kept, 1)

            with act.Fori(0, HEADS) as i:
                def keep(n, h):
                    act.wait_ge(proj, i * 2 * MAIN + 2 * n + h + 5)
                    src, fn = ps[:, h, :], ACT.Copy
                    tok = slice(h * HALF, (h + 1) * HALF)
                    if n < 2:
                        if n == 1 and h == 0:
                            act.wait_ge(ua_done, i + 1)
                        dst = tn[n][:, tok]
                    elif n < QKV:
                        if n < 4 and h == 0:
                            act.wait_ge(conv_done, i * 2 + n - 1)
                        dst, fn = tn[n % 2][:, tok], (ACT.Copy if n < OA else ACT.Sigmoid)
                    elif n < ZA:
                        g, j = (n - QKV) // 3, (n - QKV) % 3
                        dst = stored(tn[g % 2] if j == 2 else qa[:, g % 2, j, :], g, h * HALF, HALF)
                        src = src.rearrange("p (u r) -> p r u", r=DIL[g])
                    elif n < ZB:
                        if n == ZA and h == 0:
                            act.wait_ge(roped, i * 6 + 6)
                        if n == ZA + 1 and h == 0:
                            act.wait_ge(um_done, i * 2 + 1)
                        dst = sg[:, tok]
                    else:
                        if h == 0:
                            act.wait_ge(out_used, i * 4 + 8)
                        dst = szb[:, tok]
                    A(dst, src, fn).then_inc(kept[h], 1)

                def z_sigmoid(n):
                    act.wait_ge(kept[0], i * MAIN + n + 2)
                    act.wait_ge(kept[1], i * MAIN + n + 2)
                    if n > ZA:
                        act.wait_ge(um_done, i * 2 + n - ZA)
                    A(tn[1], szb if n == ZB else sg[:], ACT.Sigmoid).then_inc(z_sig, 1)

                def conv_sigmoid(q):
                    act.wait_ge(conv_done, i * 2 + q + 1)
                    if q:
                        act.wait_ge(xc_done, i * 2 + 1)
                    A(sg[:], cv[:], ACT.Sigmoid).then_inc(conv_sig, 1)

                def head_keep(js):
                    for j in js:
                        w, e, h = j // 4, j // 2 % 2, j % 2
                        act.wait_ge(qk_out, i * 8 + j + 1)
                        A((qm, km)[w][:, e, h * HALF:(h + 1) * HALF], (M0, M1)[h], ACT.Copy,
                          scale=KSCALE if w else 1.0).then_inc(qk_kept, 1)

                def intra_weights():
                    act.wait_ge(e_arg, i + 1)
                    for c in range(NCH):
                        ins = A(ew[:, c, :], ew[:, c, :], ACT.Exp, bias=hc[:, c, 0:1])
                    ins.then_inc(e_exp, 1)

                def inter(c):
                    act.wait_ge(num_out, i * 8 + c + 1)
                    act.wait_ge(num_kept, i * 8 + c + 1)
                    if c:
                        act.wait_ge(squares, i * 8 + c)
                    A(hin[:], M2[:, 0:DH + 1], ACT.Copy, scale=hc[:, c, 1:2]).then_inc(inter_kept, 1)
                    act.wait_ge(gated, i * 8 + c + 1)
                    A(hin[:, 0:DH], og[:, c, :], ACT.Square, accum_out=vr[:, 0, c:c + 1]).then_inc(squares, 1)

                def rstd():
                    act.wait_ge(var_done, i + 1)
                    A(vr[:, 2, :], vr[:, 1, :], ACT.Ln).then_inc(act_s, 1)
                    act.wait_ge(act_s, i + 1)
                    A(vr[:, 3, :], vr[:, 2, :], ACT.Exp, scale=-0.5).then_inc(ln_done, 1)

                def attend(g, x):
                    if x >= 2:
                        s = x - 2
                        act.wait_ge(pv_out, i * 12 + 4 * g + s + 1)
                        A(num[g][:, 2 * P * s:2 * P * (s + 1)], A2[:, 0:2 * P], ACT.Copy).then_inc(pv_kept, 1)
                    if x < 4:
                        act.wait_ge(max_done, i * 12 + 4 * g + x + 1)
                        for u in range(2):
                            b = blocks(g, 2 * x + u)
                            A(sm[:, x % 2, u, 0:b * P], sm[:, x % 2, u, 0:b * P], ACT.Exp, bias=nm[:, x % 2, u:u + 1],
                              accum_out=st[:, g, 2 * x + u, 1:2]).then_inc(exp_done, 1)

                def group_weights():
                    act.wait_ge(exp_done, i * 24 + 24)
                    for src, dst in stat_dest(2):
                        act.dma_start(dst, src).then_inc(stat_out[2], 16)
                    for g in range(GROUPS):
                        act.wait_ge(stat_out[g], (i + 1) * (16 * STATS[g]))
                    act.dma_start(ct[:].rearrange("p g c w -> p g (c w)"),
                                  stat_d.rearrange("g (p c) w -> p g (c w)", c=NCH)).then_inc(ct_in, 16)
                    act.wait_ge(ct_arg, i + 1)
                    A(cw[:, 1], cw[:, 1], ACT.Exp).then_inc(ct_exp, 1)
                    act.wait_ge(cw_done, i + 1)
                    act.dma_start(coef_d.rearrange("g (p c) -> p g c", c=NCH), cw[:, 2]).then_inc(coef_out, 16)
                    act.wait_ge(coef_out, (i + 1) * 16)
                    for g in range(GROUPS):
                        act.dma_start(cb[g], coef_d[g:g + 1, :].broadcast_to([P, S])).then_inc(cb_in[g], 16)

                for n in range(MAIN):
                    c, g = n - 7, (n - 9) // 3
                    keep(n, 0)
                    if 1 <= n <= 2:
                        conv_sigmoid(n - 1)
                    if n == 3:
                        intra_weights()
                    if n == 4:
                        head_keep(range(0, 4))
                    if n == 5:
                        head_keep(range(4, 8))
                    if 0 <= c < NCH:
                        inter(c)
                    if n >= 9:
                        attend(g, 2 * (n - 9 - 3 * g))
                    keep(n, 1)
                    if n == 14:
                        rstd()
                    if n >= ZA:
                        z_sigmoid(n)
                    if n >= 9:
                        attend(g, 2 * (n - 9 - 3 * g) + 1)
                group_weights()
                act.wait_ge(ua_done, i + 2)
                act.dma_start(ua_d[bass.ds(i, 1)].rearrange("o p s -> (o p) s"), szb).then_inc(ua_out, 16)
            act.wait_ge(ua_out, 16 * HEADS + 16)

        @block.vector
        def _(dve):
            v = nc.vector
            ones = v.memset(v1[:, :, DH:DH + 2], 1.0)
            ones.then_inc(ready, 1)
            v.memset(turn[:, :, 0:3], 0.0).then_inc(ready, 1)
            for s, k in ((turned_kept, 2), (num_kept, 1), (normed, 1), (out_used, 4), (p_kept, 1), (masked, 1), (ua_done, 1)):
                dve.sem_inc(s, k)
            dve.wait_ge(hp_in, 16)
            dve.wait_ge(ready, 2)

            with dve.Fori(0, HEADS) as i:
                step = Steps(dve, dve_s, i, DVE_STEPS)

                def chunk_kept(n):
                    for h in range(2):
                        dve.wait_ge(kept[h], i * MAIN + n + 2)

                def conv(q):
                    chunk_kept(q)
                    if q:
                        dve.wait_ge(xc_done, i * 2 + 1)
                    else:
                        dve.wait_ge(ua_done, i + 1)
                    x = turn[:, q, :]
                    step(v.tensor_scalar(cv[:], x[:, 3:3 + S], hp[:, q, 3:4], hp[:, q, 4:5], ALU.mult, ALU.add))
                    for j in range(3):
                        ins = v.scalar_tensor_tensor(cv[:], x[:, j:j + S], hp[:, q, j:j + 1], cv[:], ALU.mult, ALU.add)
                        if j < 2:
                            step(ins)
                    ins.then_inc(conv_done, 1)

                def conv_gate(q):
                    dve.wait_ge(conv_sig, i * 2 + q + 1)
                    dve.wait_ge(um_out[q], (i + 1) * 16)
                    v.tensor_tensor(xc[:, q, :], cv[:], sg[:], ALU.mult).then_inc(xc_done, 1)

                def intra_args():
                    dve.wait_ge(e_in, (i + 1) * 16)
                    v.tensor_tensor(ew[:], ew[:], band[:, 0:P].unsqueeze(1).broadcast_to([P, NCH, P]), ALU.add).then_inc(e_arg, 1)

                def turn_chunk(n):
                    if n == OA:
                        dve.wait_ge(ua_out, (i + 1) * 16)
                    for j in range(2):
                        dve.wait_ge(turned, i * 8 + (n - VA) * 2 + j + 1)
                        to = (v1 if n < OA else og)[:, 4 * j:4 * j + 4, (n % 2) * P:(n % 2 + 1) * P]
                        v.tensor_copy(to, (A0, A1)[j].rearrange("p (c e) -> p c e", c=4)).then_inc(turned_kept, 1)

                def rope(n):
                    g, j = (n - QKV) // 3, (n - QKV) % 3
                    chunk_kept(n)
                    if g + j:
                        dve.wait_ge(roped, i * 6 + 2 * g + j)
                    else:
                        dve.wait_ge(xc_done, i * 2 + 2)
                    v.tensor_copy(small[:, 3:4], zero[:])
                    x, rot = qa[0:ROPE, g % 2, j, :], sg[0:ROPE, :]
                    step(v.stream_shuffle(rot, x, [(m + ROPE // 2) % ROPE for m in range(ROPE)]))
                    step(v.tensor_tensor(stored(rot, g), stored(rot, g), order(sinT, g), ALU.mult))
                    step(v.tensor_tensor(stored(x, g), stored(x, g), order(cosT, g), ALU.mult))
                    v.tensor_tensor(x, x, rot, ALU.add).then_inc(roped, 1)

                def weigh(c):
                    dve.wait_ge(sk_out, i * 8 + c + 1)
                    if c == 0:
                        dve.wait_ge(e_exp, i + 1)
                    v.tensor_tensor(sw[:, c % 2, :], M0[:, 0:P], ew[:, c, :], ALU.mult).then_inc(sw_done, 1)
                    v.tensor_scalar(kw[:, c % 2, :], M0[:, P:P + DH], hc[:, c, 3:4], KSCALE, ALU.mult, ALU.mult).then_inc(sw_done, 1)

                def head_out(c):
                    dve.wait_ge(inter_kept, i * 8 + c + 1)
                    if c:
                        dve.wait_ge(gated, i * 8 + c)
                    v.tensor_tensor(hnb[:], M1[:, 0:DH + 1], hin[:], ALU.add).then_inc(num_kept, 1)
                    dve.wait_ge(num_kept, i * 8 + c + 2)
                    den = hnb[:, DH:DH + 1]
                    step(v.tensor_scalar(small[:, 0:1], den, -1.0, None, ALU.mult))
                    step(v.scalar_tensor_tensor(small[:, 1:2], den, hc[:, c, 2:3], small[:, 0:1], ALU.max, ALU.max))
                    step(v.reciprocal(small[:, 2:3], small[:, 1:2]))
                    v.scalar_tensor_tensor(og[:, c, :], hnb[:, 0:DH], small[:, 2:3], og[:, c, :], ALU.mult, ALU.mult)\
                        .then_inc(gated, 1)

                def state(c):
                    dve.wait_ge(upd_out, i * 7 + c + 1)
                    if c == 0:
                        dve.wait_ge(dec_in, (i + 1) * 16)
                    for d in range(2):
                        v.scalar_tensor_tensor(cst[:, d, :], cst[:, d, :], dec[:, c:c + 1], (M1, M2)[d][:, 0:DH + 1],
                                               ALU.mult, ALU.add).then_inc(state_done, 1)

                def head_norm():
                    dve.wait_ge(squares, i * 8 + 8)
                    v.tensor_scalar(vr[:, 1, :], vr[:, 0, :], 1.0 / DH, EPS, ALU.mult, ALU.add).then_inc(var_done, 1)
                    for q in range(2):
                        v.tensor_scalar(xc[:, q, :], xc[:, q, :], hp[:, q, 5:6], None, ALU.mult)
                    dve.wait_ge(ln_done, i + 1)
                    step(v.tensor_tensor(vr[:, 4, :], vr[:, 3, :], vr[:, 3, :], ALU.mult))
                    step(v.tensor_tensor(vr[:, 4, :], vr[:, 4, :], vr[:, 1, :], ALU.mult))
                    step(v.tensor_scalar(vr[:, 4, :], vr[:, 4, :], -0.5, 1.5, ALU.mult, ALU.add))
                    step(v.tensor_tensor(vr[:, 5, :], vr[:, 4, :], vr[:, 3, :], ALU.mult))
                    v.tensor_tensor(og[:], og[:], vr[:, 5, :].unsqueeze(2).broadcast_to([P, NCH, DH]), ALU.mult).then_inc(normed, 1)

                def head_scaled():
                    for j in range(4):
                        q, h = j // 2, j % 2
                        dve.wait_ge(out_turned, i * 4 + j + 1)
                        part = xc[:, q, h * HALF:(h + 1) * HALF]
                        v.scalar_tensor_tensor(part, (M0, M1, M2, M0)[j], hp[:, q, 6:7], part, ALU.mult, ALU.add).then_inc(out_used, 1)

                def silu_za(q):
                    dve.wait_ge(z_sig, i * 3 + q + 1)
                    step(v.tensor_tensor(sg[:], sg[:], tn[1], ALU.mult))
                    if q == 0:
                        dve.wait_ge(out_used, i * 4 + 8)
                    v.tensor_tensor(xc[:, q, :], xc[:, q, :], sg[:], ALU.mult).then_inc(um_done, 1)

                def attend(g, x):
                    if x == 0:
                        for j in range(2):
                            dve.wait_ge(v_turned, i * 6 + 2 * g + j + 1)
                            v.tensor_copy(vt[:, 4 * j:4 * j + 4, :], (A1, A2)[j].rearrange("p (c e) -> p c e", c=4)).then_inc(v_kept, 1)
                    if x < 4:
                        dve.wait_ge(score_out, i * 12 + 4 * g + x + 1)
                        v.tensor_copy(small[:, 3:4], zero[:])
                        for u in range(2):
                            t, b = 2 * x + u, blocks(g, 2 * x + u)
                            mask = diag[:] if g == 2 else band[:, (2 - b) * P:2 * P]
                            v.tensor_tensor_reduce(sm[:, x % 2, u, 0:b * P], A0[:, u * 2 * P:u * 2 * P + b * P], mask, SCALE, -3e38,
                                                   ALU.add, ALU.max, st[:, g, t, 0:1]).then_inc(masked, 1)
                        dve.wait_ge(masked, i * 24 + 8 * g + 2 * x + 3)
                        v.tensor_scalar(nm[:, x % 2, :], st[:, g, 2 * x:2 * x + 2, 0], -1.0, None, ALU.mult).then_inc(max_done, 1)
                    if 1 <= x <= 4:
                        dve.wait_ge(p_turned, i * 12 + 4 * g + x)
                        bs = [blocks(g, 2 * (x - 1) + u) for u in range(2)]
                        bank = A1.rearrange("p (u b q) -> p u b q", u=2, b=2)
                        if bs[0] == bs[1]:
                            ins = v.tensor_copy(pT[:, :, 0:bs[0], :], bank[:, :, 0:bs[0], :])
                        else:
                            for u in range(2):
                                ins = v.tensor_copy(pT[:, u, 0:bs[u], :], bank[:, u, 0:bs[u], :])
                        ins.then_inc(p_kept, 1)

                def merge_groups():
                    dve.wait_ge(z_sig, i * 3 + 3)
                    step(v.tensor_tensor(szb, szb, tn[1], ALU.mult))
                    dve.wait_ge(ct_in, (i + 1) * 16)
                    mx, dn = ct[:, :, :, 0], ct[:, :, :, 1]
                    top, ex, wt, pr = cw[:, 3, 0, :], cw[:, 1], cw[:, 2], cw[:, 0]
                    step(v.tensor_tensor(top, mx[:, 0, :], mx[:, 1, :], ALU.max))
                    step(v.tensor_tensor(top, top, mx[:, 2, :], ALU.max))
                    v.tensor_tensor(ex, mx, top.unsqueeze(1).broadcast_to([P, GROUPS, NCH]), ALU.subtract).then_inc(ct_arg, 1)
                    dve.wait_ge(ct_exp, i + 1)
                    step(v.tensor_tensor(pr, ex, dn, ALU.mult))
                    step(v.tensor_tensor(cw[:, 3, 1, :], pr[:, 0, :], pr[:, 1, :], ALU.add))
                    step(v.tensor_tensor(cw[:, 3, 1, :], cw[:, 3, 1, :], pr[:, 2, :], ALU.add))
                    step(v.reciprocal(cw[:, 3, 2, :], cw[:, 3, 1, :]))
                    v.tensor_tensor(wt, ex, cw[:, 3, 2, :].unsqueeze(1).broadcast_to([P, GROUPS, NCH]), ALU.mult).then_inc(cw_done, 1)
                    dve.wait_ge(pv_kept, i * 12 + 13)
                    for g in range(GROUPS):
                        dve.wait_ge(cb_in[g], (i + 1) * 16)
                        step(v.tensor_tensor(stored(num[g], g), stored(num[g], g), order(cb[g], g), ALU.mult))
                    for g in (1, 2):
                        step(v.tensor_tensor(order(num[0], g), order(num[0], g), stored(num[g], g), ALU.add))
                    v.tensor_tensor(szb, szb, num[0], ALU.mult).then_inc(ua_done, 1)

                step(v.tensor_copy(hp[:], hpa[:, bass.ds(i, 1)].rearrange("p o q w -> p (o q) w")))
                step(v.tensor_copy(hc[:], cols[:, :, :, bass.ds(i, 1)].rearrange("p c q o -> p c (q o)")))
                step(v.memset(cst[:], 0.0))
                for n in range(MAIN):
                    c, g = n - 7, (n - 9) // 3
                    if 1 <= n <= 2:
                        conv(n - 1)
                        if n == 1:
                            conv_gate(0)
                    if n == 2:
                        conv_gate(1)
                        intra_args()
                    if QKV <= n - 1 < ZA and (n - 1 - QKV) % 3 < 2:
                        rope(n - 1)
                    if 3 <= n <= 6:
                        turn_chunk(n - 1)
                    if n == 6:
                        weigh(0)
                    if 0 <= c < NCH:
                        head_out(c)
                    if n >= 9:
                        attend(g, 2 * (n - 9 - 3 * g))
                    if 0 <= c < NCH - 1:
                        state(c)
                        weigh(c + 1)
                    if n == 14:
                        head_norm()
                    if n == 15:
                        head_scaled()
                    if n == 15 or n == 16:
                        silu_za(n - 15)
                    if n >= 9:
                        attend(g, 2 * (n - 9 - 3 * g) + 1)
                merge_groups()
                step.end()


def merge(nc, a, sem, sb, ps, T):
    h_hi, h_lo, um_d, ua_d, mg_d, zero = (T[n] for n in ("h_hi", "h_lo", "um_d", "ua_d", "mg_d", "zero"))
    KA = HEADS
    KB = KT + KA
    with ExitStack() as ctx:
        def buf(name, shape, dt=F32):
            return sb(name, shape, dt, ctx)

        b_hi = buf("b_hi", [P, KB, S], F32R)
        b_lo = buf("b_lo", [P, KB, S], F32R)
        raw = buf("raw_m", [P, 2, D])
        whi = buf("whi_m", [P, 2, D], F32R)
        wlo = buf("wlo_m", [P, 2, D], F32R)
        sa = buf("sig_a", [P, S])
        sc = buf("sig_b", [P, S])
        mg = buf("merged_rows", [P, S])
        braw = [sa, sc]

        b_in = [sem("b_in0"), sem("b_in1")]
        b_hi_done, b_lo_done = sem("b_hi_done"), sem("b_lo_done")
        w_in = [sem("wm_in0"), sem("wm_in1")]
        w_split, pool_s = sem("wm_split"), sem("pool_merge")
        bank_out = [sem(f"gate_out{j}") for j in range(4)]
        sig_done, merged_half, dve_s, mg_out = sem("sig_done"), sem("merged_half"), sem("dve_merge"), sem("mg_out")
        block = ctx.enter_context(nc.Block())

        @block.sync
        def _(sp):
            sp.sem_inc(mg_out, 16)
            with sp.Fori(0, KT) as m:
                for j in range(4):
                    sp.wait_ge(w_split, m * 4 + j + 1)
                    n = D if j < 3 else KA * P
                    sp.dma_start(raw[:, j % 2, 0:n], a["w_merge"][bass.ds(m, 1), j, :, 0:n].rearrange("o p c -> (o p) c"))\
                      .then_inc(w_in[j % 2], 16)
            sp.wait_ge(mg_out, 16 * KT + 16)

        @block.gpsimd
        def _(pool):
            pool.sem_inc(w_split, 2)
            with pool.Fori(0, KT) as m:
                for j in range(4):
                    n = D if j < 3 else KA * P
                    pool.wait_ge(bank_out[(j + 2) % 4], m * 2 + 2)
                    pool.wait_ge(w_in[j % 2], (m * 2 + j // 2 + 1) * 16)
                    nc.gpsimd.tensor_tensor(whi[:, j % 2, 0:n], raw[:, j % 2, 0:n], zero[:].broadcast_to([P, n]), ALU.add)\
                      .then_inc(pool_s, 1)
                    pool.wait_ge(pool_s, m * 4 + j + 1)
                    nc.gpsimd.tensor_tensor(wlo[:, j % 2, 0:n], raw[:, j % 2, 0:n], whi[:, j % 2, 0:n].bitcast(F32), ALU.subtract)\
                      .then_inc(w_split, 1)

        @block.tensor
        def _(pe):
            t_ = nc.tensor
            for j in (2, 3):
                pe.sem_inc(bank_out[j], 2)
            with pe.Fori(0, KT) as m:
                for j in range(4):
                    pe.wait_ge(w_split, m * 4 + j + 3)
                    if j == 2:
                        pe.wait_ge(b_lo_done, KB)
                    x_hi, x_lo, k0, kn = ((h_hi, h_lo, 0, KT), (h_hi, h_lo, 0, KT), (b_hi, b_lo, 0, KT), (b_hi, b_lo, KT, KA))[j]
                    for h in range(2):
                        if j < 2:
                            pe.wait_ge(sig_done, m * 4 + 2 * j + h + 1)
                        else:
                            pe.wait_ge(merged_half, m * 4 + 2 * h + 1)
                        for k in range(kn):
                            mm = three_pass(t_, ps[:, 2 * j + h, :], whi[:, j % 2, k * P:(k + 1) * P], wlo[:, j % 2, k * P:(k + 1) * P],
                                            x_hi[:, k0 + k, h * HALF:(h + 1) * HALF], x_lo[:, k0 + k, h * HALF:(h + 1) * HALF],
                                            k == 0, k == kn - 1)
                        mm.then_inc(bank_out[j], 1)

        @block.scalar
        def _(act):
            A = nc.scalar.activation
            act.sem_inc(sig_done, 4)
            for k in range(KB):
                if k >= 2:
                    act.wait_ge(b_lo_done, k - 1)
                src = um_d[k // 2, k % 2] if k < KT else ua_d[k - KT]
                act.dma_start(braw[k % 2][:], src).then_inc(b_in[k % 2], 16)
                if k >= 1:
                    act.wait_ge(b_in[(k - 1) % 2], 16 * ((k - 1) // 2 + 1))
                    A(b_hi[:, k - 1, :], braw[(k - 1) % 2][:], ACT.Copy).then_inc(b_hi_done, 1)
            act.wait_ge(b_in[(KB - 1) % 2], 16 * (KB // 2))
            A(b_hi[:, KB - 1, :], braw[(KB - 1) % 2][:], ACT.Copy).then_inc(b_hi_done, 1)
            act.wait_ge(b_lo_done, KB)
            with act.Fori(0, KT) as m:
                for j in range(2):
                    for h in range(2):
                        act.wait_ge(bank_out[j], m * 2 + h + 1)
                        if h == 0:
                            act.wait_ge(merged_half, m * 4 + 4)
                        A((sa, sc)[j][:, h * HALF:(h + 1) * HALF], ps[:, 2 * j + h, :], ACT.Sigmoid).then_inc(sig_done, 1)
                act.wait_ge(merged_half, m * 4 + 8)
                act.dma_start(mg_d[bass.ds(m, 1)].rearrange("o p s -> (o p) s"), mg[:]).then_inc(mg_out, 16)

        @block.vector
        def _(dve):
            v = nc.vector
            for k in range(KB):
                dve.wait_ge(b_hi_done, k + 1)
                v.tensor_tensor(b_lo[:, k, :], braw[k % 2][:], b_hi[:, k, :].bitcast(F32), ALU.subtract).then_inc(b_lo_done, 1)
            dve.sem_inc(merged_half, 4)
            with dve.Fori(0, KT) as m:
                for h in range(2):
                    tok = slice(h * HALF, (h + 1) * HALF)
                    dve.wait_ge(sig_done, m * 4 + 8)
                    dve.wait_ge(bank_out[2], m * 2 + h + 3)
                    dve.wait_ge(bank_out[3], m * 2 + h + 3)
                    if h == 0:
                        dve.wait_ge(mg_out, (m + 1) * 16)
                    v.tensor_tensor(mg[:, tok], sa[:, tok], ps[:, 4 + h, :], ALU.mult).then_inc(dve_s, 1)
                    v.tensor_tensor(sc[:, tok], sc[:, tok], ps[:, 6 + h, :], ALU.mult).then_inc(merged_half, 1)
                    dve.wait_ge(dve_s, m * 2 + h + 1)
                    dve.wait_ge(merged_half, m * 4 + 2 * h + 5)
                    v.tensor_tensor(mg[:, tok], mg[:, tok], sc[:, tok], ALU.add).then_inc(merged_half, 1)


def finish(nc, a, out, sem, sb, ps, T):
    mg_d, mod_d = T["mg_d"], T["mod_d"]
    with ExitStack() as ctx:
        def buf(name, shape, dt=F32):
            return sb(name, shape, dt, ctx)

        w_hi = buf("wo_hi", [P, KT, D], F32R)
        w_lo = buf("wo_lo", [P, KT, D], F32R)
        wr = buf("wo_raw", [P, 2, D])
        mr = buf("m_raw", [P, 2, KT, P])
        m_hi = buf("m_hi", [P, 2, KT, P], F32R)
        m_lo = buf("m_lo", [P, 2, KT, P], F32R)
        gate = buf("gate_row", [P, D])
        gf = buf("g_final_row", [P, D])
        xt = buf("x_rows", [P, 2, D])
        y = buf("y_rows", [P, 2, D])
        junk = buf("junk", [P, D])
        sc = buf("row_stats", [P, 2, 6])

        row_in, w_in, m_in, x_in = sem("row_in"), [sem("wo_in0"), sem("wo_in1")], [sem("m_in0"), sem("m_in1")], [sem("xr_in0"), sem("xr_in1")]
        w_hi_done, w_lo_done, m_hi_done, m_split, prod, added = (sem(n) for n in ("wo_hi_done", "wo_lo_done", "m_hi_done", "m_split", "prod", "added"))
        sq_done, ln_done, var_done, y_done, act_s, dve_s = (sem(n) for n in ("sq_done", "lnf_done", "varf_done", "y_done", "act_fin", "dve_fin"))
        y_out = [sem("y_out0"), sem("y_out1")]
        block = ctx.enter_context(nc.Block())
        PER = 12

        @block.sync
        def _(sp):
            for b in range(2):
                sp.sem_inc(y_out[b], 16)
            for k in range(KT):
                if k >= 2:
                    sp.wait_ge(w_lo_done, k - 1)
                sp.dma_start(wr[:, k % 2, :], a["w_out"][k * P:(k + 1) * P, :]).then_inc(w_in[k % 2], 16)
                if k == 1:
                    sp.dma_start(gate[:], mod_d[0:1, 2 * D:3 * D].broadcast_to([P, D])).then_inc(row_in, 16)
                    sp.dma_start(gf[:], a["g_final"].broadcast_to([P, D])).then_inc(row_in, 16)
            with sp.Fori(0, NCH // 2) as t:
                for b in range(2):
                    sp.wait_ge(y_done, t * 2 + b + 1)
                    sp.dma_start(out[bass.ds((t * 2 + b) * P, P), :], y[:, b, :]).then_inc(y_out[b], 16)
            for b in range(2):
                sp.wait_ge(y_out[b], 16 * (NCH // 2) + 16)

        @block.gpsimd
        def _(pool):
            pool.sem_inc(m_split, 2)
            with pool.Fori(0, NCH // 2) as t:
                for b in range(2):
                    pool.wait_ge(m_split, t * 2 + b + 1)
                    pool.dma_start(mr[:, b], mg_d.rearrange("k p s -> p k s")[:, :, bass.ds((t * 2 + b) * P, P)]).then_inc(m_in[b], 16)
                    pool.wait_ge(added, t * 2 + b + 1)
                    pool.dma_start(xt[:, b, :], a["x"][bass.ds((t * 2 + b) * P, P), :]).then_inc(x_in[b], 16)

        @block.tensor
        def _(pe):
            t_ = nc.tensor
            with pe.Fori(0, NCH // 2) as t:
                for b in range(2):
                    pe.wait_ge(m_split, t * 2 + b + 3)
                    for h in range(2):
                        pe.wait_ge(added, t * 2 + b + 1)
                        for k in range(KT):
                            if b == 0 and h == 0:
                                pe.wait_ge(w_lo_done, k + 1)
                            cols = slice(h * HALF, (h + 1) * HALF)
                            mm = three_pass(t_, ps[:, 2 * b + h, :], m_hi[:, b, k, :], m_lo[:, b, k, :], w_hi[:, k, cols],
                                            w_lo[:, k, cols], k == 0, k == KT - 1)
                        mm.then_inc(prod, 1)

        @block.scalar
        def _(act):
            A = nc.scalar.activation
            for k in range(KT):
                act.wait_ge(w_in[k % 2], 16 * (k // 2 + 1))
                A(w_hi[:, k, :], wr[:, k % 2, :], ACT.Copy).then_inc(w_hi_done, 1)
            with act.Fori(0, NCH // 2) as t:
                for b in range(2):
                    act.wait_ge(m_in[b], (t + 1) * 16)
                    A(m_hi[:, b], mr[:, b], ACT.Copy).then_inc(m_hi_done, 1)
                    act.wait_ge(var_done, t * 4 + 2 * b + 1)
                    A(junk[:], y[:, b, :], ACT.Square, accum_out=sc[:, b, 0:1]).then_inc(sq_done, 1)
                    act.wait_ge(var_done, t * 4 + 2 * b + 2)
                    A(sc[:, b, 2:3], sc[:, b, 1:2], ACT.Ln).then_inc(act_s, 1)
                    act.wait_ge(act_s, t * 2 + b + 1)
                    A(sc[:, b, 3:4], sc[:, b, 2:3], ACT.Exp, scale=-0.5).then_inc(ln_done, 1)

        @block.vector
        def _(dve):
            v = nc.vector
            dve.sem_inc(added, 2)
            for k in range(KT):
                dve.wait_ge(w_hi_done, k + 1)
                v.tensor_tensor(w_lo[:, k, :], wr[:, k % 2, :], w_hi[:, k, :].bitcast(F32), ALU.subtract).then_inc(w_lo_done, 1)
            dve.wait_ge(row_in, 32)
            with dve.Fori(0, NCH // 2) as t:
                step = Steps(dve, dve_s, t, PER)
                for b in range(2):
                    dve.wait_ge(m_hi_done, t * 2 + b + 1)
                    v.tensor_tensor(m_lo[:, b], mr[:, b], m_hi[:, b].bitcast(F32), ALU.subtract).then_inc(m_split, 1)
                    dve.wait_ge(prod, t * 4 + 2 * b + 2)
                    dve.wait_ge(y_out[b], (t + 1) * 16)
                    step(v.tensor_tensor(y[:, b, :], gate[:], ps[:, 2 * b:2 * b + 2, :].rearrange("p h c -> p (h c)"), ALU.mult))
                    dve.wait_ge(x_in[b], (t + 1) * 16)
                    step(v.tensor_tensor(y[:, b, :], y[:, b, :], xt[:, b, :], ALU.add))
                    v.tensor_copy(sc[:, b, 5:6], y[:, b, 0:1]).then_inc(var_done, 1)
                    v.tensor_copy(sc[:, b, 4:5], y[:, b, 0:1]).then_inc(added, 1)
                    dve.wait_ge(sq_done, t * 2 + b + 1)
                    v.tensor_scalar(sc[:, b, 1:2], sc[:, b, 0:1], 1.0 / D, EPS, ALU.mult, ALU.add).then_inc(var_done, 1)
                    dve.wait_ge(ln_done, t * 2 + b + 1)
                    r, w = sc[:, b, 3:4], sc[:, b, 4:5]
                    step(v.scalar_tensor_tensor(w, r, sc[:, b, 1:2], r, ALU.mult, ALU.mult))
                    step(v.tensor_scalar(w, w, -0.5, 1.5, ALU.mult, ALU.add))
                    step(v.tensor_tensor(sc[:, b, 5:6], r, w, ALU.mult))
                    step(v.tensor_scalar(y[:, b, :], y[:, b, :], sc[:, b, 5:6], None, ALU.mult))
                    v.tensor_tensor(y[:, b, :], y[:, b, :], gf[:], ALU.mult).then_inc(y_done, 1)
                step.end()


def kernel(**inputs):
    import concourse.bacc as bacc
    from concourse.bass_utils import run_bass_kernel_spmd

    x = {k: np.asarray(v) for k, v in inputs.items()}
    w_in = x["w_in"][0]

    def tiles(w):
        return np.ascontiguousarray(w.reshape(-1, P, w.shape[1]).transpose(1, 0, 2)).reshape(P, -1)

    mw = HEADS * DH
    gate0 = 4 * mw
    att0 = gate0 + 2 * HEADS
    qkv = GROUPS * HEADS * P
    zb0 = att0 + 3 * qkv
    main = np.empty((HEADS, MAIN, P, D), np.float32)
    for i in range(HEADS):
        starts = [0 + DH * i, DH * i + P, mw + DH * i, mw + DH * i + P, 2 * mw + DH * i, 2 * mw + DH * i + P]
        for g in range(GROUPS):
            starts += [att0 + j * qkv + (g * HEADS + i) * P for j in range(3)]
        starts += [3 * mw + DH * i, 3 * mw + DH * i + P, zb0 + i * P]
        for n, c in enumerate(starts):
            main[i, n] = tiles(w_in[:, c:c + P])
    gates = np.zeros((D, P), np.float32)
    gates[:, 0:HEADS] = w_in[:, gate0:gate0 + HEADS]
    gates[:, 32:32 + HEADS] = w_in[:, gate0 + HEADS:gate0 + 2 * HEADS]
    gate_bias = np.zeros((P, 2), np.float32)
    gate_bias[0:HEADS, 0] = x["b_igate"][0]
    gate_bias[32:32 + HEADS, 1] = x["b_fgate"][0]
    ga0 = zb0 + HEADS * P
    wm = np.zeros((KT, 4, P, D), np.float32)
    for m in range(KT):
        c = slice(m * P, (m + 1) * P)
        wm[m, 0] = tiles(w_in[:, ga0:ga0 + D][:, c])
        wm[m, 1] = tiles(w_in[:, ga0 + D:ga0 + 2 * D][:, c])
        wm[m, 2] = tiles(x["w_out_mlstm"][0][:, c])
        wm[m, 3, :, 0:HEADS * P] = tiles(x["w_out_attn"][0][:, c])
    hp = np.zeros((P, HEADS, 2, 8), np.float32)
    per = lambda w: w.reshape(HEADS, 2, P).transpose(2, 0, 1)
    for j in range(4):
        hp[..., j] = per(x["w_conv"][0, j])
    hp[..., 4], hp[..., 5], hp[..., 6] = per(x["b_conv"][0]), per(x["skip_mlstm"][0]), per(x["g_mlstm_head"][0])
    wqk = np.stack([x["w_q_mlstm"][0], x["w_k_mlstm"][0]], 1)
    wqk = np.ascontiguousarray(wqk.reshape(HEADS, 2, 2, P, DH).transpose(0, 3, 1, 2, 4))
    half = ROPE // 2
    freq = THETA ** (-np.arange(half, dtype=np.float32) / half)
    rope = np.stack([np.tile(freq, 2), np.repeat([-1.0, 1.0], half)], 1).astype(np.float32)
    arrays = {
        "x": x["x"][0], "c_cols": np.ascontiguousarray(x["c"].reshape(KT, P).T), "positions": x["positions"].astype(np.int32),
        "w_ada": x["w_ada"][0], "b_ada": x["b_ada"], "g_cols": np.ascontiguousarray(x["g_norm"].reshape(KT, P).T),
        "gate_bias": gate_bias, "rope_const": rope, "w_gates": tiles(gates), "w_main": main, "head_params": hp, "w_qk": wqk,
        "w_merge": wm, "w_out": x["w_out"][0], "g_final": x["g_final"].reshape(1, D),
    }
    nc = bacc.Bacc("TRN2", target_bir_lowering=False, num_devices=1)
    feed, aps = {}, {}
    for k, v in arrays.items():
        feed["in_" + k] = np.ascontiguousarray(v)
        aps[k] = nc.dram_tensor("in_" + k, v.shape, mybir.dt.from_np(v.dtype), kind="ExternalInput").ap()
    out = nc.dram_tensor("out_rows", (S, D), F32, kind="ExternalOutput").ap()
    build(nc, aps, out)
    r = run_bass_kernel_spmd(nc, [feed], core_ids=[0])
    return r.results[0]["out_rows"].reshape(1, S, D)
```

```python
from contextlib import ExitStack

import numpy as np
import concourse.bass as bass
from concourse import mybir

F32, F32R, I32 = mybir.dt.float32, mybir.dt.float32r, mybir.dt.int32
ACT, ALU, AX = mybir.ActivationFunctionType, mybir.AluOpType, mybir.AxisListType

P = 128
D = 1024
S = 1024
KT = D // P
HALF = 512
HEADS, DH = 4, 256
NCH = S // P
GROUPS = 3
DIL = (1, 4, 16)
ROPE, THETA = 32, 500000.0
EPS = 1e-6
NEG = -1e30
SCALE = 128.0 ** -0.5
KSCALE = DH ** -0.5
MAIN = 18
XA, VA, OA, QKV, ZA, ZB = 0, 2, 4, 6, 15, 17
AHEAD = 3
PI = float(np.pi)


class Steps:

    def __init__(self, eng, sem, turn=0, per_turn=0):
        self.eng, self.sem, self.base, self.per, self.n = eng, sem, turn * per_turn, per_turn, 0

    def __call__(self, ins):
        self.n += 1
        ins.then_inc(self.sem, 1)
        self.eng.wait_ge(self.sem, self.base + self.n)

    def end(self):
        assert not self.per or self.n == self.per, self.n


def order(ap, g, lo=0, n=S):
    return ap[:, lo:lo + n].rearrange("p (u r) -> p r u", r=DIL[g])


def stored(ap, g, lo=0, n=S):
    d = DIL[g]
    return ap.rearrange("p (r u) -> p r u", r=d)[:, :, lo // d:(lo + n) // d]


def build(nc, a, out):
    with ExitStack() as top:
        def sem(name):
            return top.enter_context(nc.semaphore(name))

        def sb(name, shape, dt=F32, ctx=top):
            return ctx.enter_context(nc.sbuf_tensor(name, shape, dt))

        def dram(name, shape):
            return nc.dram_tensor(name, shape, F32, kind="Internal").ap()

        ps = top.enter_context(nc.psum_tensor("banks", [P, 8, HALF], F32))
        mod_d = dram("mod_rows", [1, 3 * D])
        r1_d = dram("log_weight_rows", [HEADS, S])
        wi_d = dram("chunk_decay_rows", [HEADS, NCH])
        stat_d = dram("softmax_stats", [GROUPS, S, 2])
        coef_d = dram("group_weights", [GROUPS, S])
        um_d = dram("mlstm_branch", [HEADS, 2, P, S])
        ua_d = dram("attn_branch", [HEADS, P, S])
        mg_d = dram("merged", [KT, P, S])

        ident = sb("ident", [P, P])
        zero = sb("zero", [P, 1])
        band = sb("band", [P, 2 * P])
        diag = sb("diag", [P, P])

        h_hi = sb("h_hi", [P, KT, S], F32R)
        with ExitStack() as ctx:
            w_out_raw = sb("w_out_raw", [P, KT, D], F32, ctx)
        h_lo = sb("h_lo", [P, KT, S], F32R)

        with ExitStack() as ctx:
            kept_on = buffers(sb, ctx, STREAM)
            with ExitStack() as inner:
                mixing = buffers(sb, inner, MIXING)
            with ExitStack() as inner:
                b_hi = sb("b_hi", [P, KT + HEADS, S], F32R, inner)
                with ExitStack() as raw:
                    b_raw = sb("b_raw", [P, KT + HEADS, S], F32, raw)
                b_lo = sb("b_lo", [P, KT + HEADS, S], F32R, inner)
            with ExitStack() as inner:
                finishing = buffers(sb, inner, FINISHING)

        setup(nc, a, sem, sb, ps, locals())

        w_in, um_out = [[sem(f"{n}{b}") for b in range(2)] for n in ("w_in", "um_out")]
        kept = [sem("kept0"), sem("kept1")]
        tile_in = [sem(f"tile_in{k}") for k in range(KT + HEADS)]
        w_split, pool_s, proj = sem("w_split"), sem("pool_split"), sem("proj")
        out_used, masked, p_kept, pv_kept, ua_done, ua_out = (sem(n) for n in ("out_used", "masked", "p_kept", "pv_kept", "ua_done", "ua_out"))
        w_hi_done, w_lo_done, sig_done, mg_out = sem("wo_hi_done"), sem("wo_lo_done"), sem("sig_done"), sem("mg_out")
        merged_half, b_hi_done, b_lo_done = sem("merged_half"), sem("b_hi_done"), sem("b_lo_done")
        stages = [mix(nc, a, sem, ps, locals()), merge(nc, a, sem, ps, locals()), finish(nc, a, out, sem, ps, locals())]
        block = top.enter_context(nc.Block())

        @block.sync
        def _(sp):
            for stage in stages:
                stage["sync"](sp)

        @block.gpsimd
        def _(pool):
            for stage in stages:
                stage["gpsimd"](pool)

        @block.tensor
        def _(pe):
            for stage in stages:
                stage["tensor"](pe)

        @block.scalar
        def _(act):
            for stage in stages:
                stage["scalar"](act)

        @block.vector
        def _(dve):
            for stage in stages:
                stage["vector"](dve)


def buffers(sb, ctx, table):
    return {name: sb(name, shape, dt, ctx) for name, shape, dt in table}


STREAM = [
    ("wraw", [P, 2, D], F32), ("whi", [P, 2, D], F32R), ("wlo", [P, 2, D], F32R),
    ("qa", [P, 2, 2, S], F32),
    ("num1", [P, S], F32),
]
MIXING = [
    ("hpa", [P, HEADS, 2, 8], F32), ("hp", [P, 2, 8], F32), ("hc", [P, NCH, 4], F32),
    ("turn", [P, 2, 3 + S], F32),
    ("cv", [P, S], F32), ("sg", [P, S], F32), ("xc", [P, 2, S], F32),
    ("v1", [P, NCH, DH + 2], F32), ("og", [P, NCH, DH], F32),
    ("qm", [P, 2, S], F32), ("km", [P, 2, S], F32), ("wqk", [P, 2, 2, DH], F32),
    ("ew", [P, NCH, P], F32), ("dec", [P, NCH], F32),
    ("sw", [P, 2, P], F32), ("kw", [P, 2, DH], F32), ("cst", [P, 2, DH + 1], F32),
    ("hin", [P, DH + 1], F32), ("hnb", [P, DH + 1], F32), ("small", [P, 4], F32), ("vr", [P, 6, NCH], F32),
    ("vt", [P, NCH, P], F32), ("sm", [P, 2, 2, 2 * P], F32), ("pT", [P, 2, 2, P], F32),
    ("nm", [P, 2, 2], F32), ("st", [P, GROUPS, NCH, 2], F32), ("ct", [P, GROUPS, NCH, 2], F32), ("cw", [P, 4, GROUPS, NCH], F32),
    ("cols", [P, NCH, 4, HEADS], F32), ("cosT", [ROPE, S], F32), ("sinT", [ROPE, S], F32),
]
FINISHING = [
    ("m_hi", [P, 2, KT, P], F32R), ("m_lo", [P, 2, KT, P], F32R),
    ("gate", [P, D], F32), ("gf", [P, D], F32), ("xt", [P, 2, D], F32), ("y", [P, 2, D], F32),
    ("junk", [P, D], F32), ("row_stats", [P, 2, 6], F32),
]


def setup(nc, a, sem, sb, ps, T):
    ident, zero, band, diag = T["ident"], T["zero"], T["band"], T["diag"]
    h_hi, h_lo = T["h_hi"], T["h_lo"]
    cols, cosT, sinT = (T["mixing"][n] for n in ("cols", "cosT", "sinT"))
    mod_d, r1_d, wi_d = T["mod_d"], T["r1_d"], T["wi_d"]
    NA = 3
    with ExitStack() as ctx:
        def buf(name, shape, dt=F32):
            return sb("setup_" + name, shape, dt, ctx)

        xnT = buf("xnT", [P, KT, S])
        xt = buf("xt", [P, 2, D])
        sq = buf("sq", [P, D])
        wada = buf("wada", [P, NA, 3 * D])
        brow = buf("brow", [1, 3 * D])
        modrow = buf("modrow", [1, 3 * D])
        cc = buf("cc", [P, 4, KT])
        gn = buf("gn", [P, KT])
        ms = buf("ms", [P, 3, KT])
        one = buf("one", [1, 1])
        xs = buf("xs", [P, 6, KT])
        gb = buf("gb", [P, 2])
        rc = buf("rc", [ROPE, 2])
        halfpi = buf("halfpi", [P, 1])
        posi = buf("posi", [ROPE, S], I32)
        wraw = buf("wraw_g", [P, KT, P])
        whi = buf("whi_g", [P, KT, P], F32R)
        wlo = buf("wlo_g", [P, KT, P], F32R)

        small_in, c_in, x_in, pos_in = sem("small_in"), sem("c_in"), [sem("x_in0"), sem("x_in1")], sem("pos_in")
        ada_in = [sem(f"ada_in{j}") for j in range(NA)]
        ada_used, gw_in, gw_split = sem("ada_used"), sem("gw_in"), sem("gw_split")
        consts = sem("consts")
        c_exp, c_silu = sem("c_exp"), sem("c_silu")
        x_sq, x_ln, x_norm, x_turned, x_kept = sem("x_sq"), sem("x_ln"), sem("x_norm"), sem("x_turned"), sem("x_kept")
        x_var = sem("x_var")
        mod_row, mod_col, h_full, h_ready = (sem(n) for n in ("mod_row", "mod_col", "h_full", "h_ready"))
        ms_ready = sem("ms_ready")
        g_ready, dve_s, act_s, pool_s = sem("g_ready"), sem("dve_setup"), sem("act_setup"), sem("pool_setup")
        setup_out = sem("setup_out")
        rope_arg, rope_abs = sem("rope_arg"), sem("rope_abs")
        gate_abs, gate_ls, gate_arg, gate_exp, gate_min = (sem(n) for n in ("gate_abs", "gate_ls", "gate_arg", "gate_exp", "gate_min"))
        cols_ready = sem("cols_ready")
        rows_ready = sem("rows_ready")

        block = ctx.enter_context(nc.Block())

        @block.sync
        def _(sp):
            sp.dma_start(cc[:, 0, :], a["c_cols"]).then_inc(c_in, 16)
            for k in range(KT):
                if k >= NA:
                    sp.wait_ge(ada_used, k - NA + 1)
                sp.dma_start(wada[:, k % NA, :], a["w_ada"][k * P:(k + 1) * P, :]).then_inc(ada_in[k % NA], 16)
            sp.dma_start(wraw[:], a["w_gates"].rearrange("p (k c) -> p k c", k=KT)).then_inc(gw_in, 16)
            sp.wait_ge(mod_row, 6)
            sp.dma_start(mod_d, modrow[:]).then_inc(setup_out, 16)
            sp.wait_ge(gate_arg, 1)
            sp.dma_start(r1_d, xnT[0:HEADS, 4, :]).then_inc(setup_out, 16)
            sp.wait_ge(rows_ready, 2)
            sp.dma_start(wi_d, sq[0:HEADS, 0:NCH]).then_inc(setup_out, 16)
            sp.wait_ge(setup_out, 48)

        @block.gpsimd
        def _(pool):
            nc.gpsimd.memset(zero[:], 0.0).then_inc(pool_s, 1)
            nc.gpsimd.memset(ident[:], 0.0).then_inc(pool_s, 1)
            nc.gpsimd.memset(band[:], 0.0).then_inc(pool_s, 1)
            nc.gpsimd.memset(diag[:], 0.0).then_inc(pool_s, 1)
            nc.gpsimd.memset(one[:], 1.0).then_inc(pool_s, 1)
            nc.gpsimd.memset(halfpi[:], PI / 2).then_inc(pool_s, 1)
            pool.wait_ge(pool_s, 6)
            nc.gpsimd.affine_select(out=ident[:], in_=ident[:], compare_op=ALU.not_equal, fill=1.0, base=0,
                                    pattern=[[-1, P]], channel_multiplier=1).then_inc(consts, 1)
            nc.gpsimd.affine_select(out=band[:, 0:P], in_=band[:, 0:P], compare_op=ALU.is_ge, fill=NEG, base=0,
                                    pattern=[[1, P]], channel_multiplier=-1).then_inc(consts, 1)
            nc.gpsimd.affine_select(out=band[:, P:], in_=band[:, P:], compare_op=ALU.is_ge, fill=NEG, base=0,
                                    pattern=[[-1, P]], channel_multiplier=1).then_inc(consts, 1)
            nc.gpsimd.affine_select(out=diag[:], in_=diag[:], compare_op=ALU.is_ge, fill=NEG, base=0,
                                    pattern=[[-1, P]], channel_multiplier=1).then_inc(consts, 1)
            pool.wait_ge(consts, 4)
            nc.gpsimd.memset(diag[64:128, 0:64], NEG).then_inc(consts, 1)
            pool.wait_ge(consts, 5)
            pool.wait_ge(gw_in, 16)
            nc.gpsimd.tensor_tensor(whi[:], wraw[:], zero[:].unsqueeze(2).broadcast_to([P, KT, P]), ALU.add).then_inc(gw_split, 1)
            pool.wait_ge(gw_split, 1)
            nc.gpsimd.tensor_tensor(wlo[:], wraw[:], whi[:].bitcast(F32), ALU.subtract).then_inc(gw_split, 1)

        @block.scalar
        def _(act):
            step = Steps(act, act_s)
            act.dma_start(xt[:, 0, :], a["x"][0:P, :]).then_inc(x_in[0], 16)
            act.dma_start(xt[:, 1, :], a["x"][P:2 * P, :]).then_inc(x_in[1], 16)
            act.dma_start(brow[:], a["b_ada"]).then_inc(small_in, 16)
            act.dma_start(gn[:], a["g_cols"]).then_inc(small_in, 16)
            act.dma_start(gb[:], a["gate_bias"]).then_inc(small_in, 16)
            act.dma_start(rc[:], a["rope_const"]).then_inc(small_in, 16)
            act.dma_start(posi[:], a["positions"].partition_broadcast(ROPE)).then_inc(pos_in, 16)
            act.wait_ge(c_in, 16)
            nc.scalar.activation(cc[:, 1, :], cc[:, 0, :], ACT.Exp, scale=-1.0).then_inc(c_exp, 1)
            for t in range(NCH):
                act.wait_ge(x_in[t % 2], 16 * (t // 2 + 1))
                if t:
                    act.wait_ge(x_sq, t)
                nc.scalar.activation(sq[:], xt[:, t % 2, :], ACT.Square, accum_out=xs[:, 0, t:t + 1]).then_inc(x_sq, 1)
                act.wait_ge(x_var, t + 1)
                step(nc.scalar.activation(xs[:, 2, t:t + 1], xs[:, 1, t:t + 1], ACT.Ln))
                nc.scalar.activation(xs[:, 3, t:t + 1], xs[:, 2, t:t + 1], ACT.Exp, scale=-0.5).then_inc(x_ln, 1)
                if t + 2 < NCH:
                    act.wait_ge(x_norm, t + 1)
                    act.wait_ge(x_turned, t + 1)
                    act.dma_start(xt[:, t % 2, :], a["x"][(t + 2) * P:(t + 3) * P, :]).then_inc(x_in[t % 2], 16)
            act.wait_ge(ms_ready, 1)
            act.wait_ge(x_kept, 2 * NCH)
            for k in range(KT):
                nc.scalar.activation(xnT[:, k, :], xnT[:, k, :], ACT.Identity, scale=ms[:, 0, k:k + 1],
                                     bias=ms[:, 1, k:k + 1]).then_inc(h_full, 1)
            act.wait_ge(rope_arg, 1)
            act.wait_ge(consts, 5)
            nc.scalar.activation(sinT[:], sq[0:ROPE, :], ACT.Sin).then_inc(rope_abs, 1)
            step(nc.scalar.activation(xt[0:ROPE, 1, :], sq[0:ROPE, :], ACT.Abs))
            nc.scalar.activation(cosT[:], xt[0:ROPE, 1, :], ACT.Sin, scale=-1.0, bias=halfpi[0:ROPE, :]).then_inc(rope_abs, 1)
            act.wait_ge(g_ready, 2)
            act.wait_ge(h_ready, 2 * KT)
            nc.scalar.activation(xnT[0:HEADS, 0, :], ps[0:HEADS, 0:2, :], ACT.Identity, bias=gb[0:HEADS, 0:1])\
                .then_inc(gate_abs, 1)
            nc.scalar.activation(xnT[0:HEADS, 2, :], ps[32:32 + HEADS, 0:2, :], ACT.Abs, bias=gb[32:32 + HEADS, 1:2])\
                .then_inc(gate_abs, 1)
            act.wait_ge(gate_abs, 2)
            step(nc.scalar.activation(xnT[0:HEADS, 2, :], xnT[0:HEADS, 2, :], ACT.Exp, scale=-1.0))
            nc.scalar.activation(xnT[0:HEADS, 2, :], xnT[0:HEADS, 2, :], ACT.Ln, bias=1.0).then_inc(gate_ls, 1)
            act.wait_ge(gate_arg, 2)
            nc.scalar.activation(xnT[0:HEADS, 1, :], xnT[0:HEADS, 1, :], ACT.Exp).then_inc(rows_ready, 1)
            act.wait_ge(rows_ready, 1)
            nc.scalar.copy(sq[0:HEADS, 0:NCH], xnT[0:HEADS, 1, P - 1::P]).then_inc(rows_ready, 1)
            nc.scalar.activation(xnT[0:HEADS, 2, :], xnT[0:HEADS, 2, :], ACT.Exp, scale=-1.0).then_inc(gate_exp, 1)
            nc.scalar.activation(xnT[0:HEADS, 3, :], xnT[0:HEADS, 3, :], ACT.Exp).then_inc(gate_exp, 1)

        @block.vector
        def _(dve):
            step = Steps(dve, dve_s)
            v = nc.vector
            dve.wait_ge(c_exp, 1)
            step(v.tensor_scalar(cc[:, 2, :], cc[:, 1, :], 1.0, None, ALU.add))
            step(v.reciprocal(cc[:, 3, :], cc[:, 2, :]))
            v.tensor_tensor(cc[:, 1, :], cc[:, 0, :], cc[:, 3, :], ALU.mult).then_inc(c_silu, 1)
            for t in range(NCH):
                dve.wait_ge(x_sq, t + 1)
                v.tensor_scalar(xs[:, 1, t:t + 1], xs[:, 0, t:t + 1], 1.0 / D, EPS, ALU.mult, ALU.add).then_inc(x_var, 1)
                dve.wait_ge(x_ln, t + 1)
                dve.wait_ge(x_var, t + 1)
                r, w = xs[:, 3, t:t + 1], xs[:, 4, t:t + 1]
                step(v.scalar_tensor_tensor(w, r, xs[:, 1, t:t + 1], r, ALU.mult, ALU.mult))
                step(v.tensor_scalar(w, w, -0.5, 1.5, ALU.mult, ALU.add))
                step(v.tensor_tensor(xs[:, 5, t:t + 1], r, w, ALU.mult))
                v.tensor_scalar(xt[:, t % 2, :], xt[:, t % 2, :], xs[:, 5, t:t + 1], None, ALU.mult).then_inc(x_norm, 1)
                for h in range(2):
                    dve.wait_ge(x_turned, t + 1)
                    v.tensor_copy(xnT[:, 4 * h:4 * h + 4, t * P:(t + 1) * P],
                                  ps[:, 6 + h, :].rearrange("p (k c) -> p k c", k=4)).then_inc(x_kept, 1)
            dve.wait_ge(small_in, 64)
            dve.wait_ge(pos_in, 16)
            dve.wait_ge(x_sq, NCH)
            ang, kk, tmp = xt[0:ROPE, 0, :], xt[0:ROPE, 1, :], sq[0:ROPE, :]
            dve.wait_ge(x_turned, NCH)
            step(v.tensor_copy(tmp, posi[:]))
            step(v.tensor_scalar(ang, tmp, rc[:, 0:1], None, ALU.mult))
            step(v.tensor_scalar(kk, ang, 1.0 / (2 * PI), 12582912.0, ALU.mult, ALU.add))
            step(v.tensor_scalar(kk, kk, 12582912.0, None, ALU.subtract))
            c1 = 6.28125
            c2 = float(np.float32(np.round((2 * PI - c1) * 2 ** 19) / 2 ** 19))
            c3 = float(np.float32(2 * PI - c1 - c2))
            for c in (c1, c2, c3):
                step(v.scalar_tensor_tensor(ang, kk, -c, ang, ALU.mult, ALU.add))
            v.tensor_scalar(tmp, ang, 3.1415925, -3.1415925, ALU.min, ALU.max).then_inc(rope_arg, 1)
            dve.wait_ge(ada_used, KT)
            for n in range(6):
                v.tensor_tensor(modrow[:, n * HALF:(n + 1) * HALF], ps[0:1, n, :], brow[:, n * HALF:(n + 1) * HALF],
                                ALU.add).then_inc(mod_row, 1)
            dve.wait_ge(mod_col, 1)
            step(v.tensor_scalar(ms[:, 2, :], ps[:, 7, KT:2 * KT], 1.0, None, ALU.add))
            step(v.tensor_copy(ms[:, 1, :], ps[:, 7, 0:KT]))
            v.tensor_tensor(ms[:, 0, :], ms[:, 2, :], gn[:], ALU.mult).then_inc(ms_ready, 1)
            for k in range(KT):
                dve.wait_ge(h_full, k + 1)
                v.tensor_copy(h_hi[:, k, :], xnT[:, k, :]).then_inc(h_ready, 1)
                dve.wait_ge(h_ready, 2 * k + 1)
                v.tensor_tensor(h_lo[:, k, :], xnT[:, k, :], h_hi[:, k, :].bitcast(F32), ALU.subtract).then_inc(h_ready, 1)
            dve.wait_ge(rope_abs, 2)
            step(v.tensor_scalar(sinT[:], sinT[:], rc[:, 1:2], None, ALU.mult))
            row = lambda j: xnT[0:HEADS, j, :]
            by_chunk = lambda j: row(j).rearrange("p (c t) -> p c t", c=NCH)
            last = lambda j: by_chunk(j)[:, :, P - 1:P]
            dve.wait_ge(gate_abs, 2)
            step(v.memset(row(6), 1.0))
            step(v.memset(by_chunk(6)[:, :, 0:1], 0.0))
            step(v.tensor_scalar(row(7), ps[32:32 + HEADS, 0:2, :], gb[32:32 + HEADS, 1:2], 0.0, ALU.add, ALU.min))
            dve.wait_ge(gate_ls, 1)
            step(v.tensor_tensor(row(7), row(7), row(2), ALU.subtract))
            step(v.tensor_tensor_scan(row(5), row(6), row(7), 0.0, ALU.mult, ALU.add))
            step(v.tensor_tensor_scan(row(2), row(7), row(0), 0.0, ALU.add, ALU.max))
            step(v.tensor_tensor(row(4), row(5), row(2), ALU.subtract))
            step(v.memset(row(6)[:, 0:NCH], 0.0))
            step(v.tensor_copy(row(6)[:, 1:NCH], row(2)[:, P - 1:S - P:P]))
            v.tensor_tensor(by_chunk(1), by_chunk(4), row(6)[:, 0:NCH].unsqueeze(2).broadcast_to([HEADS, NCH, P]),
                            ALU.add).then_inc(gate_arg, 1)
            step(v.tensor_tensor(row(0), row(0), row(5), ALU.subtract))
            v.tensor_tensor(by_chunk(3), by_chunk(0), last(4).broadcast_to([HEADS, NCH, P]), ALU.add).then_inc(gate_arg, 1)
            dve.wait_ge(cols_ready, 1)
            v.tensor_copy(cols[:], ps[:, 2, 0:P].rearrange("p (c q h) -> p c q h", c=NCH, q=4)).then_inc(dve_s, 1)

        @block.tensor
        def _(pe):
            t_ = nc.tensor
            pe.wait_ge(consts, 1)
            pe.wait_ge(c_silu, 1)
            for k in range(KT):
                pe.wait_ge(ada_in[k % NA], 16 * (k // NA + 1))
                for n in range(6):
                    mm = t_.matmul(ps[0:1, n, :], cc[:, 1, k:k + 1], wada[:, k % NA, n * HALF:(n + 1) * HALF],
                                   start=(k == 0), stop=(k == KT - 1))
                mm.then_inc(ada_used, 1)
                pe.wait_ge(x_norm, k + 1)
                if k:
                    pe.wait_ge(x_kept, 2 * k)
                for d in range(KT):
                    mm = t_.transpose(ps[:, 6 + d // 4, (d % 4) * P:(d % 4 + 1) * P], xt[:, k % 2, d * P:(d + 1) * P],
                                      ident[:])
                mm.then_inc(x_turned, 1)
            pe.wait_ge(x_kept, 2 * NCH)
            for j in range(2 * KT):
                if j % 4 == 0:
                    pe.wait_ge(mod_row, j // 4 + 1)
                mm = t_.matmul(ps[:, 7, j:j + 1], modrow[:, j * P:(j + 1) * P], one[:], start=True, stop=True)
            mm.then_inc(mod_col, 1)
            pe.wait_ge(gw_split, 2)
            pe.wait_ge(mod_row, 6)
            for h in range(2):
                for k in range(KT):
                    if h == 0:
                        pe.wait_ge(h_ready, 2 * k + 2)
                    mm = three_pass(t_, ps[:, h, :], whi[:, k, :], wlo[:, k, :], h_hi[:, k, h * HALF:(h + 1) * HALF],
                                    h_lo[:, k, h * HALF:(h + 1) * HALF], k == 0, k == KT - 1)
                mm.then_inc(g_ready, 1)
            pe.wait_ge(gate_exp, 2)
            pe.wait_ge(rows_ready, 1)
            for c in range(NCH):
                for q in range(4):
                    mm = t_.transpose(ps[:, 2, (c * 4 + q) * 4:(c * 4 + q) * 4 + 4], xnT[0:HEADS, q, c * P:(c + 1) * P],
                                      ident[0:HEADS, 0:HEADS])
            mm.then_inc(cols_ready, 1)


def three_pass(t_, out, w_hi, w_lo, x_hi, x_lo, first, last):
    t_.matmul(out, w_hi, x_hi, start=first, stop=False)
    t_.matmul(out, w_hi, x_lo, start=False, stop=False)
    return t_.matmul(out, w_lo, x_hi, start=False, stop=last)


def mix(nc, a, sem, ps, T):
    ident, zero, band, diag, h_hi, h_lo = (T[n] for n in ("ident", "zero", "band", "diag", "h_hi", "h_lo"))
    r1_d, wi_d, stat_d, coef_d, um_d, ua_d = (T[n] for n in ("r1_d", "wi_d", "stat_d", "coef_d", "um_d", "ua_d"))
    w_in, um_out, kept, w_split, pool_s, proj = (T[n] for n in ("w_in", "um_out", "kept", "w_split", "pool_s", "proj"))
    out_used, masked, p_kept, pv_kept, ua_done, ua_out = (T[n] for n in ("out_used", "masked", "p_kept", "pv_kept", "ua_done", "ua_out"))
    wraw, whi, wlo, qa, num1 = (T["kept_on"][n] for n in ("wraw", "whi", "wlo", "qa", "num1"))
    hpa, hp, hc, turn, cv, sg, xc, v1, og, qm, km, wqk, ew, dec, sw, kw, cst, hin, hnb, small, vr, vt, sm, pT, nm, st, ct, cw, \
        cols, cosT, sinT = T["mixing"].values()
    DVE_STEPS = 69
    M0, M1, M2, A0, A1, A2 = (ps[:, b, :] for b in range(2, 8))
    og_flat = og[:].rearrange("p c e -> p (c e)")
    szb = og_flat[:, 0:S]
    num = [cv[:], num1[:], km[:, 1, :]]
    cb = [qm[:, 0, :], qm[:, 1, :], km[:, 0, :]]
    tn = [turn[:, b, 3:3 + S] for b in range(2)]

    hp_in, ready = sem("hp_in"), sem("mix_ready")
    conv_done, conv_sig, xc_done, e_in, dec_in, wqk_in = (sem(n) for n in ("conv_done", "conv_sig", "xc_done", "e_in", "dec_in", "wqk_in"))
    e_arg, e_exp, turned, turned_kept, qk_out, qk_kept = (sem(n) for n in ("e_arg", "e_exp", "turned", "turned_kept", "qk_out", "qk_kept"))
    sk_out, sw_done, num_out, inter_kept, num_kept, gated = (sem(n) for n in ("sk_out", "sw_done", "num_out", "inter_kept", "num_kept", "gated"))
    squares, upd_out, state_done, var_done, ln_done, normed = (sem(n) for n in ("squares", "upd_out", "state_done", "var_done", "ln_done", "normed"))
    out_turned, z_sig, um_done, dve_s, act_s = (sem(n) for n in ("out_turned", "z_sig", "um_done", "dve_mix", "act_mix"))
    roped, v_turned, v_kept, score_out, max_done = (sem(n) for n in ("roped", "v_turned", "v_kept", "score_out", "max_done"))
    exp_done, p_turned, pv_out = (sem(n) for n in ("exp_done", "p_turned", "pv_out"))
    stat_out = [sem(f"stat_out{g}") for g in range(GROUPS)]
    ct_in, ct_arg, ct_exp, cw_done, coef_out = (sem(n) for n in ("ct_in", "ct_arg", "ct_exp", "cw_done", "coef_out"))
    cb_in = [sem(f"cb_in{g}") for g in range(GROUPS)]

    def stat_dest(g):
        if g == 0:
            return [(st[:, 0], stat_d[0].rearrange("(c p) w -> p c w", p=P))]
        if g == 1:
            x = stat_d[1].rearrange("(b p r) w -> r p b w", p=P, r=4)
            return [(st[:, 1, 2 * r:2 * r + 2, :], x[r]) for r in range(4)]
        x = stat_d[2].rearrange("(u c h) w -> h u c w", c=NCH, h=2)
        return [(st[64 * h:64 * h + 64, 2], x[h]) for h in range(2)]

    STATS = (1, 4, 2)

    def sync(sp):
        ahead = a["w_all"][AHEAD:AHEAD + HEADS * MAIN].rearrange("(i n) p c -> i n p c", n=MAIN)

        def weigh_groups(i):
            for g in range(GROUPS):
                sp.wait_ge(stat_out[g], i * (16 * STATS[g]) + 16 * STATS[g])
            sp.dma_start(ct[:].rearrange("p g c w -> p g (c w)"), stat_d.rearrange("g (p c) w -> p g (c w)", c=NCH)).then_inc(ct_in, 16)
            sp.wait_ge(cw_done, i + 1)
            sp.dma_start(coef_d.rearrange("g (p c) -> p g c", c=NCH), cw[:, 2]).then_inc(coef_out, 16)
            sp.wait_ge(coef_out, i * 16 + 16)
            for g in range(GROUPS):
                sp.dma_start(cb[g], coef_d[g:g + 1, :].broadcast_to([P, S])).then_inc(cb_in[g], 16)

        for q in range(AHEAD):
            if q >= 2:
                sp.wait_ge(w_split, q + 1)
            sp.dma_start(wraw[:, q % 2, :], a["w_all"][q]).then_inc(w_in[q % 2], 16)
        sp.dma_start(hpa[:], a["head_params"]).then_inc(hp_in, 16)
        for b in range(2):
            sp.sem_inc(um_out[b], 16)
        sp.sem_inc(ua_out, 16)
        with sp.Fori(0, HEADS) as i:
            sp.wait_ge(normed, i + 1)
            sp.dma_start(wqk[:], a["w_qk"][bass.ds(i, 1)].rearrange("o p j k e -> (o p) j k e")).then_inc(wqk_in, 16)
            sp.dma_start(ew[:].rearrange("p c t -> p (c t)"), r1_d[bass.ds(i, 1), :].broadcast_to([P, S])).then_inc(e_in, 16)
            sp.dma_start(dec[:], wi_d[bass.ds(i, 1), :].broadcast_to([P, NCH])).then_inc(dec_in, 16)
            for n in range(MAIN):
                if n == MAIN - 1:
                    weigh_groups(i)
                b = (n + AHEAD) % 2
                sp.wait_ge(w_split, i * MAIN + (n + AHEAD + 1))
                sp.dma_start(wraw[:, b, :], ahead[bass.ds(i, 1), n].rearrange("o p c -> (o p) c")).then_inc(w_in[b], 16)
                if n in (12, 15, 16):
                    g = (12, 15, 16).index(n)
                    sp.wait_ge(exp_done, i * 24 + 8 * g + 8)
                    for src, dst in stat_dest(g):
                        sp.dma_start(dst, src).then_inc(stat_out[g], 16)
            for q in range(2):
                sp.wait_ge(um_done, i * 2 + q + 1)
                sp.dma_start(um_d[bass.ds(i, 1), q].rearrange("o p s -> (o p) s"), xc[:, q, :]).then_inc(um_out[q], 16)
            sp.wait_ge(ua_done, i + 2)
            sp.dma_start(ua_d[bass.ds(i, 1)].rearrange("o p s -> (o p) s"), szb).then_inc(ua_out, 16)

    def gpsimd(pool):
        pool.sem_inc(w_split, 2)
        with pool.Fori(0, HEADS) as i:
            for n in range(MAIN):
                raw, hi, lo = wraw[:, n % 2, :], whi[:, n % 2, :], wlo[:, n % 2, :]
                pool.wait_ge(proj, i * 2 * MAIN + 2 * n + 2)
                pool.wait_ge(w_in[n % 2], (i * (MAIN // 2) + n // 2 + 1) * 16)
                nc.gpsimd.tensor_tensor(hi, raw, zero[:].broadcast_to([P, D]), ALU.add).then_inc(pool_s, 1)
                pool.wait_ge(pool_s, i * MAIN + n + 1)
                nc.gpsimd.tensor_tensor(lo, raw, hi.bitcast(F32), ALU.subtract).then_inc(w_split, 1)

    def blocks(g, tile):
        return 2 if (g == 0 and tile > 0) or (g == 1 and tile % 2 == 1) else 1

    def tensor(pe):
        t_ = nc.tensor
        pe.sem_inc(proj, 4)

        with pe.Fori(0, HEADS) as i:
            def project(n, h):
                pe.wait_ge(w_split, i * MAIN + n + 3)
                pe.wait_ge(kept[h], i * MAIN + n + 1)
                for k in range(KT):
                    mm = three_pass(t_, ps[:, h, :], whi[:, n % 2, k * P:(k + 1) * P], wlo[:, n % 2, k * P:(k + 1) * P],
                                    h_hi[:, k, h * HALF:(h + 1) * HALF], h_lo[:, k, h * HALF:(h + 1) * HALF],
                                    k == 0, k == KT - 1)
                mm.then_inc(proj, 1)

            def chunk_kept(n):
                for h in range(2):
                    pe.wait_ge(kept[h], i * MAIN + n + 2)

            def turn_chunk(n):
                chunk_kept(n)
                if n == VA:
                    pe.wait_ge(masked, i * 24 + 1)
                    pe.wait_ge(p_kept, i * 12 + 1)
                for j in range(2):
                    m = (n - VA) * 2 + j
                    pe.wait_ge(turned_kept, i * 8 + m + 1)
                    for c in range(4):
                        mm = t_.transpose((A0, A1)[j][:, c * P:(c + 1) * P], tn[n % 2][:, (4 * j + c) * P:(4 * j + c + 1) * P],
                                          ident[:])
                    mm.then_inc(turned, 1)

            def head_qk(js):
                pe.wait_ge(wqk_in, (i + 1) * 16)
                pe.wait_ge(xc_done, i * 2 + 2)
                pe.wait_ge(out_used, i * 4 + 4)
                for j in js:
                    pe.wait_ge(qk_kept, i * 8 + j + 1)
                    w, e, h = j // 4, j // 2 % 2, j % 2
                    for d in range(2):
                        mm = t_.matmul((M0, M1)[h], wqk[:, w, d, e * P:(e + 1) * P], xc[:, d, h * HALF:(h + 1) * HALF],
                                       start=(d == 0), stop=(d == 1))
                    mm.then_inc(qk_out, 1)

            def scores_and_keys(c):
                pe.wait_ge(qk_kept, i * 8 + 10)
                if c:
                    pe.wait_ge(sw_done, i * 16 + 2 * c)
                cs = slice(c * P, (c + 1) * P)
                for d in range(2):
                    t_.matmul(M0[:, 0:P], km[:, d, cs], qm[:, d, cs], start=(d == 0), stop=(d == 1))
                for d in range(2):
                    mm = t_.matmul(M0[:, P:P + DH], xc[:, d, cs], wqk[:, 1, d, :], start=(d == 0), stop=(d == 1))
                mm.then_inc(sk_out, 1)

            def numerator(c):
                pe.wait_ge(sw_done, i * 16 + 2 * c + 2)
                if c:
                    pe.wait_ge(state_done, i * 14 + 2 * c)
                t_.matmul(M1[:, 0:DH + 1], sw[:, c % 2, :], v1[:, c, 0:DH + 1], start=True, stop=True)
                for d in range(2):
                    mm = t_.matmul(M2[:, 0:DH + 1], qm[:, d, c * P:(c + 1) * P], cst[:, d, :], start=(d == 0), stop=(d == 1))
                mm.then_inc(num_out, 1)

            def state_update(c):
                pe.wait_ge(num_kept, i * 8 + c + 2)
                for d in range(2):
                    mm = t_.matmul((M1, M2)[d][:, 0:DH + 1], kw[:, c % 2, d * P:(d + 1) * P], v1[:, c, 0:DH + 1],
                                   start=True, stop=True)
                mm.then_inc(upd_out, 1)

            def turn_output():
                pe.wait_ge(normed, i + 2)
                for j in range(4):
                    if j == 3:
                        pe.wait_ge(out_used, i * 4 + 5)
                    for c in range(4):
                        mm = t_.transpose((M0, M1, M2, M0)[j][:, c * P:(c + 1) * P],
                                          og[:, 4 * (j % 2) + c, (j // 2) * P:(j // 2 + 1) * P], ident[:])
                    mm.then_inc(out_turned, 1)

            def turn_values(g):
                chunk_kept(8 + 3 * g)
                pe.wait_ge(turned_kept, i * 8 + 10)
                pe.wait_ge(p_kept, i * 12 + 4 * g + 1)
                pe.wait_ge(pv_kept, i * 12 + 4 * g + 1)
                for j in range(2):
                    for c in range(4):
                        k = 4 * j + c
                        mm = t_.transpose((A1, A2)[j][:, c * P:(c + 1) * P], tn[g % 2][:, k * P:(k + 1) * P], ident[:])
                    mm.then_inc(v_turned, 1)

            def attend(g, x):
                if x == 0:
                    turn_values(g)
                if x < 4:
                    pe.wait_ge(roped, i * 6 + 2 * g + 2)
                    pe.wait_ge(masked, i * 24 + 8 * g + 2 * x + 1)
                    for u in range(2):
                        t, b = 2 * x + u, blocks(g, 2 * x + u)
                        mm = t_.matmul(A0[:, u * 2 * P:u * 2 * P + b * P], qa[:, g % 2, 0, t * P:(t + 1) * P],
                                       qa[:, g % 2, 1, (t + 1 - b) * P:(t + 1) * P], start=True, stop=True)
                    mm.then_inc(score_out, 1)
                if x >= 2:
                    pe.wait_ge(p_kept, i * 12 + 4 * g + x)
                    pe.wait_ge(v_kept, i * 6 + 2 * g + 2)
                    pe.wait_ge(pv_kept, i * 12 + 4 * g + x - 1)
                    for u in range(2):
                        t, b = 2 * (x - 2) + u, blocks(g, 2 * (x - 2) + u)
                        for j in range(b):
                            mm = t_.matmul(A2[:, u * P:(u + 1) * P], vt[:, t + 1 - b + j, :], pT[:, u, j, :],
                                           start=(j == 0), stop=(j == b - 1))
                    mm.then_inc(pv_out, 1)
                if 1 <= x <= 4:
                    pe.wait_ge(exp_done, i * 24 + 8 * g + 2 * x)
                    pe.wait_ge(p_kept, i * 12 + 4 * g + x)
                    pe.wait_ge(v_kept, i * 6 + 2 * g + 2)
                    for u in range(2):
                        for j in range(blocks(g, 2 * (x - 1) + u)):
                            mm = t_.transpose(A1[:, (2 * u + j) * P:(2 * u + j + 1) * P],
                                              sm[:, (x - 1) % 2, u, j * P:(j + 1) * P], ident[:])
                    mm.then_inc(p_turned, 1)

            for n in range(MAIN):
                c, g = n - 7, (n - 9) // 3
                project(n, 0)
                if 3 <= n <= 6:
                    turn_chunk(n - 1)
                if n == 4:
                    head_qk(range(0, 4))
                if n == 5:
                    head_qk(range(4, 8))
                if n == 6:
                    scores_and_keys(0)
                if 0 <= c < NCH:
                    numerator(c)
                if n >= 9:
                    attend(g, 2 * (n - 9 - 3 * g))
                project(n, 1)
                if 0 <= c < NCH - 1:
                    state_update(c)
                    scores_and_keys(c + 1)
                if n == 15:
                    turn_output()
                if n >= 9:
                    attend(g, 2 * (n - 9 - 3 * g) + 1)

    def scalar(act):
        A = nc.scalar.activation
        for h in range(2):
            act.sem_inc(kept[h], 1)
        act.sem_inc(qk_kept, 2)
        act.sem_inc(pv_kept, 1)

        with act.Fori(0, HEADS) as i:
            def keep(n, h):
                act.wait_ge(proj, i * 2 * MAIN + 2 * n + h + 5)
                src, fn = ps[:, h, :], ACT.Copy
                tok = slice(h * HALF, (h + 1) * HALF)
                if n < 2:
                    if n == 1 and h == 0:
                        act.wait_ge(ua_done, i + 1)
                    dst = tn[n][:, tok]
                elif n < QKV:
                    if n < 4 and h == 0:
                        act.wait_ge(conv_done, i * 2 + n - 1)
                    dst, fn = tn[n % 2][:, tok], (ACT.Copy if n < OA else ACT.Sigmoid)
                elif n < ZA:
                    g, j = (n - QKV) // 3, (n - QKV) % 3
                    dst = stored(tn[g % 2] if j == 2 else qa[:, g % 2, j, :], g, h * HALF, HALF)
                    src = src.rearrange("p (u r) -> p r u", r=DIL[g])
                elif n < ZB:
                    if n == ZA and h == 0:
                        act.wait_ge(roped, i * 6 + 6)
                    if n == ZA + 1 and h == 0:
                        act.wait_ge(um_done, i * 2 + 1)
                    dst = sg[:, tok]
                else:
                    if h == 0:
                        act.wait_ge(out_used, i * 4 + 8)
                    dst = szb[:, tok]
                A(dst, src, fn).then_inc(kept[h], 1)

            def z_sigmoid(n):
                act.wait_ge(kept[0], i * MAIN + n + 2)
                act.wait_ge(kept[1], i * MAIN + n + 2)
                if n > ZA:
                    act.wait_ge(um_done, i * 2 + n - ZA)
                A(tn[1], szb if n == ZB else sg[:], ACT.Sigmoid).then_inc(z_sig, 1)

            def conv_sigmoid(q):
                act.wait_ge(conv_done, i * 2 + q + 1)
                if q:
                    act.wait_ge(xc_done, i * 2 + 1)
                A(sg[:], cv[:], ACT.Sigmoid).then_inc(conv_sig, 1)

            def head_keep(js):
                for j in js:
                    w, e, h = j // 4, j // 2 % 2, j % 2
                    act.wait_ge(qk_out, i * 8 + j + 1)
                    A((qm, km)[w][:, e, h * HALF:(h + 1) * HALF], (M0, M1)[h], ACT.Copy,
                      scale=KSCALE if w else 1.0).then_inc(qk_kept, 1)

            def intra_weights():
                act.wait_ge(e_arg, i + 1)
                for c in range(NCH):
                    ins = A(ew[:, c, :], ew[:, c, :], ACT.Exp, bias=hc[:, c, 0:1])
                ins.then_inc(e_exp, 1)

            def inter(c):
                act.wait_ge(num_out, i * 8 + c + 1)
                act.wait_ge(num_kept, i * 8 + c + 1)
                if c:
                    act.wait_ge(squares, i * 8 + c)
                A(hin[:], M2[:, 0:DH + 1], ACT.Copy, scale=hc[:, c, 1:2]).then_inc(inter_kept, 1)
                act.wait_ge(gated, i * 8 + c + 1)
                A(hin[:, 0:DH], og[:, c, :], ACT.Square, accum_out=vr[:, 0, c:c + 1]).then_inc(squares, 1)

            def rstd():
                act.wait_ge(var_done, i + 1)
                A(vr[:, 2, :], vr[:, 1, :], ACT.Ln).then_inc(act_s, 1)
                act.wait_ge(act_s, i + 1)
                A(vr[:, 3, :], vr[:, 2, :], ACT.Exp, scale=-0.5).then_inc(ln_done, 1)

            def attend(g, x):
                if x >= 2:
                    s = x - 2
                    act.wait_ge(pv_out, i * 12 + 4 * g + s + 1)
                    A(num[g][:, 2 * P * s:2 * P * (s + 1)], A2[:, 0:2 * P], ACT.Copy).then_inc(pv_kept, 1)
                if x < 4:
                    act.wait_ge(max_done, i * 12 + 4 * g + x + 1)
                    for u in range(2):
                        b = blocks(g, 2 * x + u)
                        A(sm[:, x % 2, u, 0:b * P], sm[:, x % 2, u, 0:b * P], ACT.Exp, bias=nm[:, x % 2, u:u + 1],
                          accum_out=st[:, g, 2 * x + u, 1:2]).then_inc(exp_done, 1)

            for n in range(MAIN):
                c, g = n - 7, (n - 9) // 3
                if n == ZB:
                    act.wait_ge(ct_arg, i + 1)
                    A(cw[:, 1], cw[:, 1], ACT.Exp).then_inc(ct_exp, 1)
                keep(n, 0)
                if 1 <= n <= 2:
                    conv_sigmoid(n - 1)
                if n == 3:
                    intra_weights()
                if n == 4:
                    head_keep(range(0, 4))
                if n == 5:
                    head_keep(range(4, 8))
                if 0 <= c < NCH:
                    inter(c)
                if n >= 9:
                    attend(g, 2 * (n - 9 - 3 * g))
                keep(n, 1)
                if n == 14:
                    rstd()
                if n >= ZA:
                    z_sigmoid(n)
                if n >= 9:
                    attend(g, 2 * (n - 9 - 3 * g) + 1)

    def vector(dve):
        v = nc.vector
        ones = v.memset(v1[:, :, DH:DH + 2], 1.0)
        ones.then_inc(ready, 1)
        v.memset(turn[:, :, 0:3], 0.0).then_inc(ready, 1)
        for s, k in ((turned_kept, 2), (num_kept, 1), (normed, 1), (out_used, 4), (p_kept, 1), (masked, 1), (ua_done, 1)):
            dve.sem_inc(s, k)
        dve.wait_ge(hp_in, 16)
        dve.wait_ge(ready, 2)

        with dve.Fori(0, HEADS) as i:
            step = Steps(dve, dve_s, i, DVE_STEPS)

            def chunk_kept(n):
                for h in range(2):
                    dve.wait_ge(kept[h], i * MAIN + n + 2)

            def conv(q):
                chunk_kept(q)
                if q:
                    dve.wait_ge(xc_done, i * 2 + 1)
                else:
                    dve.wait_ge(ua_done, i + 1)
                x = turn[:, q, :]
                step(v.tensor_scalar(cv[:], x[:, 3:3 + S], hp[:, q, 3:4], hp[:, q, 4:5], ALU.mult, ALU.add))
                for j in range(3):
                    ins = v.scalar_tensor_tensor(cv[:], x[:, j:j + S], hp[:, q, j:j + 1], cv[:], ALU.mult, ALU.add)
                    if j < 2:
                        step(ins)
                ins.then_inc(conv_done, 1)

            def conv_gate(q):
                dve.wait_ge(conv_sig, i * 2 + q + 1)
                dve.wait_ge(um_out[q], (i + 1) * 16)
                v.tensor_tensor(xc[:, q, :], cv[:], sg[:], ALU.mult).then_inc(xc_done, 1)

            def intra_args():
                dve.wait_ge(e_in, (i + 1) * 16)
                v.tensor_tensor(ew[:], ew[:], band[:, 0:P].unsqueeze(1).broadcast_to([P, NCH, P]), ALU.add).then_inc(e_arg, 1)

            def turn_chunk(n):
                if n == OA:
                    dve.wait_ge(ua_out, (i + 1) * 16)
                for j in range(2):
                    dve.wait_ge(turned, i * 8 + (n - VA) * 2 + j + 1)
                    to = (v1 if n < OA else og)[:, 4 * j:4 * j + 4, (n % 2) * P:(n % 2 + 1) * P]
                    v.tensor_copy(to, (A0, A1)[j].rearrange("p (c e) -> p c e", c=4)).then_inc(turned_kept, 1)

            def rope(n):
                g, j = (n - QKV) // 3, (n - QKV) % 3
                chunk_kept(n)
                if g + j:
                    dve.wait_ge(roped, i * 6 + 2 * g + j)
                else:
                    dve.wait_ge(xc_done, i * 2 + 2)
                v.tensor_copy(small[:, 3:4], zero[:])
                x, rot = qa[0:ROPE, g % 2, j, :], sg[0:ROPE, :]
                step(v.stream_shuffle(rot, x, [(m + ROPE // 2) % ROPE for m in range(ROPE)]))
                step(v.tensor_tensor(stored(rot, g), stored(rot, g), order(sinT, g), ALU.mult))
                step(v.tensor_tensor(stored(x, g), stored(x, g), order(cosT, g), ALU.mult))
                v.tensor_tensor(x, x, rot, ALU.add).then_inc(roped, 1)

            def weigh(c):
                dve.wait_ge(sk_out, i * 8 + c + 1)
                if c == 0:
                    dve.wait_ge(e_exp, i + 1)
                v.tensor_tensor(sw[:, c % 2, :], M0[:, 0:P], ew[:, c, :], ALU.mult).then_inc(sw_done, 1)
                v.tensor_scalar(kw[:, c % 2, :], M0[:, P:P + DH], hc[:, c, 3:4], KSCALE, ALU.mult, ALU.mult).then_inc(sw_done, 1)

            def head_out(c):
                dve.wait_ge(inter_kept, i * 8 + c + 1)
                if c:
                    dve.wait_ge(gated, i * 8 + c)
                v.tensor_tensor(hnb[:], M1[:, 0:DH + 1], hin[:], ALU.add).then_inc(num_kept, 1)
                dve.wait_ge(num_kept, i * 8 + c + 2)
                den = hnb[:, DH:DH + 1]
                step(v.tensor_scalar(small[:, 0:1], den, -1.0, None, ALU.mult))
                step(v.scalar_tensor_tensor(small[:, 1:2], den, hc[:, c, 2:3], small[:, 0:1], ALU.max, ALU.max))
                step(v.reciprocal(small[:, 2:3], small[:, 1:2]))
                v.scalar_tensor_tensor(og[:, c, :], hnb[:, 0:DH], small[:, 2:3], og[:, c, :], ALU.mult, ALU.mult)\
                    .then_inc(gated, 1)

            def state(c):
                dve.wait_ge(upd_out, i * 7 + c + 1)
                if c == 0:
                    dve.wait_ge(dec_in, (i + 1) * 16)
                for d in range(2):
                    v.scalar_tensor_tensor(cst[:, d, :], cst[:, d, :], dec[:, c:c + 1], (M1, M2)[d][:, 0:DH + 1],
                                           ALU.mult, ALU.add).then_inc(state_done, 1)

            def head_norm():
                dve.wait_ge(squares, i * 8 + 8)
                v.tensor_scalar(vr[:, 1, :], vr[:, 0, :], 1.0 / DH, EPS, ALU.mult, ALU.add).then_inc(var_done, 1)
                for q in range(2):
                    v.tensor_scalar(xc[:, q, :], xc[:, q, :], hp[:, q, 5:6], None, ALU.mult)
                dve.wait_ge(ln_done, i + 1)
                step(v.tensor_tensor(vr[:, 4, :], vr[:, 3, :], vr[:, 3, :], ALU.mult))
                step(v.tensor_tensor(vr[:, 4, :], vr[:, 4, :], vr[:, 1, :], ALU.mult))
                step(v.tensor_scalar(vr[:, 4, :], vr[:, 4, :], -0.5, 1.5, ALU.mult, ALU.add))
                step(v.tensor_tensor(vr[:, 5, :], vr[:, 4, :], vr[:, 3, :], ALU.mult))
                v.tensor_tensor(og[:], og[:], vr[:, 5, :].unsqueeze(2).broadcast_to([P, NCH, DH]), ALU.mult).then_inc(normed, 1)

            def head_scaled():
                for j in range(4):
                    q, h = j // 2, j % 2
                    dve.wait_ge(out_turned, i * 4 + j + 1)
                    part = xc[:, q, h * HALF:(h + 1) * HALF]
                    v.scalar_tensor_tensor(part, (M0, M1, M2, M0)[j], hp[:, q, 6:7], part, ALU.mult, ALU.add).then_inc(out_used, 1)

            def silu_za(q):
                dve.wait_ge(z_sig, i * 3 + q + 1)
                step(v.tensor_tensor(sg[:], sg[:], tn[1], ALU.mult))
                if q == 0:
                    dve.wait_ge(out_used, i * 4 + 8)
                v.tensor_tensor(xc[:, q, :], xc[:, q, :], sg[:], ALU.mult).then_inc(um_done, 1)

            def attend(g, x):
                if x == 0:
                    for j in range(2):
                        dve.wait_ge(v_turned, i * 6 + 2 * g + j + 1)
                        v.tensor_copy(vt[:, 4 * j:4 * j + 4, :], (A1, A2)[j].rearrange("p (c e) -> p c e", c=4)).then_inc(v_kept, 1)
                if x < 4:
                    dve.wait_ge(score_out, i * 12 + 4 * g + x + 1)
                    v.tensor_copy(small[:, 3:4], zero[:])
                    for u in range(2):
                        t, b = 2 * x + u, blocks(g, 2 * x + u)
                        mask = diag[:] if g == 2 else band[:, (2 - b) * P:2 * P]
                        v.tensor_tensor_reduce(sm[:, x % 2, u, 0:b * P], A0[:, u * 2 * P:u * 2 * P + b * P], mask, SCALE, -3e38,
                                               ALU.add, ALU.max, st[:, g, t, 0:1]).then_inc(masked, 1)
                    dve.wait_ge(masked, i * 24 + 8 * g + 2 * x + 3)
                    v.tensor_scalar(nm[:, x % 2, :], st[:, g, 2 * x:2 * x + 2, 0], -1.0, None, ALU.mult).then_inc(max_done, 1)
                if 1 <= x <= 4:
                    dve.wait_ge(p_turned, i * 12 + 4 * g + x)
                    bs = [blocks(g, 2 * (x - 1) + u) for u in range(2)]
                    bank = A1.rearrange("p (u b q) -> p u b q", u=2, b=2)
                    if bs[0] == bs[1]:
                        ins = v.tensor_copy(pT[:, :, 0:bs[0], :], bank[:, :, 0:bs[0], :])
                    else:
                        for u in range(2):
                            ins = v.tensor_copy(pT[:, u, 0:bs[u], :], bank[:, u, 0:bs[u], :])
                    ins.then_inc(p_kept, 1)

            def weigh_groups():
                dve.wait_ge(ct_in, (i + 1) * 16)
                mx, dn = ct[:, :, :, 0], ct[:, :, :, 1]
                top, ex, wt, pr = cw[:, 3, 0, :], cw[:, 1], cw[:, 2], cw[:, 0]
                step(v.tensor_tensor(top, mx[:, 0, :], mx[:, 1, :], ALU.max))
                step(v.tensor_tensor(top, top, mx[:, 2, :], ALU.max))
                v.tensor_tensor(ex, mx, top.unsqueeze(1).broadcast_to([P, GROUPS, NCH]), ALU.subtract).then_inc(ct_arg, 1)
                dve.wait_ge(ct_exp, i + 1)
                step(v.tensor_tensor(pr, ex, dn, ALU.mult))
                step(v.tensor_tensor(cw[:, 3, 1, :], pr[:, 0, :], pr[:, 1, :], ALU.add))
                step(v.tensor_tensor(cw[:, 3, 1, :], cw[:, 3, 1, :], pr[:, 2, :], ALU.add))
                step(v.reciprocal(cw[:, 3, 2, :], cw[:, 3, 1, :]))
                v.tensor_tensor(wt, ex, cw[:, 3, 2, :].unsqueeze(1).broadcast_to([P, GROUPS, NCH]), ALU.mult).then_inc(cw_done, 1)

            def scale_group(g):
                if g == 2:
                    dve.wait_ge(pv_kept, i * 12 + 13)
                dve.wait_ge(cb_in[g], (i + 1) * 16)
                step(v.tensor_tensor(stored(num[g], g), stored(num[g], g), order(cb[g], g), ALU.mult))

            def merge_groups():
                for g in (0, 1):
                    scale_group(g)
                step(v.tensor_tensor(order(num[0], 1), order(num[0], 1), stored(num[1], 1), ALU.add))
                scale_group(2)
                step(v.tensor_tensor(order(num[0], 2), order(num[0], 2), stored(num[2], 2), ALU.add))
                dve.wait_ge(z_sig, i * 3 + 3)
                step(v.tensor_tensor(szb, szb, tn[1], ALU.mult))
                v.tensor_tensor(szb, szb, num[0], ALU.mult).then_inc(ua_done, 1)

            step(v.tensor_copy(hp[:], hpa[:, bass.ds(i, 1)].rearrange("p o q w -> p (o q) w")))
            step(v.tensor_copy(hc[:], cols[:, :, :, bass.ds(i, 1)].rearrange("p c q o -> p c (q o)")))
            step(v.memset(cst[:], 0.0))
            for n in range(MAIN):
                c, g = n - 7, (n - 9) // 3
                if 1 <= n <= 2:
                    conv(n - 1)
                    if n == 1:
                        conv_gate(0)
                if n == 2:
                    conv_gate(1)
                    intra_args()
                if QKV <= n - 1 < ZA and (n - 1 - QKV) % 3 < 2:
                    rope(n - 1)
                if 3 <= n <= 6:
                    turn_chunk(n - 1)
                if n == 6:
                    weigh(0)
                if 0 <= c < NCH:
                    head_out(c)
                if n == ZB:
                    weigh_groups()
                if n >= 9:
                    attend(g, 2 * (n - 9 - 3 * g))
                if 0 <= c < NCH - 1:
                    state(c)
                    weigh(c + 1)
                if n == 14:
                    head_norm()
                if n == 15:
                    head_scaled()
                if n == 15 or n == 16:
                    silu_za(n - 15)
                if n >= 9:
                    attend(g, 2 * (n - 9 - 3 * g) + 1)
            merge_groups()
            step.end()

    return {"sync": sync, "gpsimd": gpsimd, "tensor": tensor, "scalar": scalar, "vector": vector}


def gates_at(m):
    return 2 * m if m < 2 else 4 * m - 2


def branches_at(m):
    return 4 + 4 * m if m < KT - 1 else 4 * KT - 2


def merge(nc, a, sem, ps, T):
    h_hi, h_lo, um_d, ua_d, mg_d, zero = (T[n] for n in ("h_hi", "h_lo", "um_d", "ua_d", "mg_d", "zero"))
    w_in, um_out, kept, tile_in, w_split, pool_s, proj = (T[n] for n in ("w_in", "um_out", "kept", "tile_in", "w_split", "pool_s", "proj"))
    out_used, masked, p_kept, pv_kept, ua_out = (T[n] for n in ("out_used", "masked", "p_kept", "pv_kept", "ua_out"))
    w_hi_done, w_lo_done, mg_out, merged_half = (T[n] for n in ("w_hi_done", "w_lo_done", "mg_out", "merged_half"))
    b_hi_done, b_lo_done = T["b_hi_done"], T["b_lo_done"]
    raw, whi, wlo, qa, mg = (T["kept_on"][n] for n in ("wraw", "whi", "wlo", "qa", "num1"))
    b_raw, b_hi, b_lo, w_out_raw = (T[n] for n in ("b_raw", "b_hi", "b_lo", "w_out_raw"))
    KA = HEADS
    KB = KT + KA
    Q0 = HEADS * MAIN
    SPLIT0, PROJ0 = 2 + Q0, 4 + 2 * Q0
    GATES_DONE = PROJ0 + 2 * (gates_at(KT - 1) + 2)
    dve_s, sig_done = sem("dve_merge"), T["sig_done"]
    width = lambda l: KA * P if l >= 4 and l % 2 == 1 and (l >= 28 or l % 4 == 1) else D

    def sync(sp):
        ahead = a["w_all"][Q0 + 5:Q0 + 29].rearrange("(t j) p c -> t j p c", j=8)

        def load(l):
            sp.wait_ge(w_split, Q0 + l + 1)
            sp.dma_start(raw[:, l % 2, 0:width(l)], a["w_all"][Q0 + l, :, 0:width(l)]).then_inc(w_in[l % 2], 16)

        load(3)
        sp.wait_ge(um_out[0], 16 * HEADS + 16)
        sp.wait_ge(um_out[1], 16 * HEADS + 16)
        sp.wait_ge(ua_out, 16 * HEADS + 16)
        for k in range(KT):
            sp.dma_start(b_raw[:, k, :], um_d[k // 2, k % 2]).then_inc(tile_in[k], 16)
        load(4)
        for k in range(KT, KB):
            sp.dma_start(b_raw[:, k, :], ua_d[k - KT]).then_inc(tile_in[k], 16)
        with sp.Fori(0, KT // 2 - 1) as t:
            for l in range(5, 13):
                sp.wait_ge(w_split, t * 8 + (Q0 + l + 1))
                sp.dma_start(raw[:, l % 2, 0:width(l)], ahead[bass.ds(t, 1), l - 5, :, 0:width(l)].rearrange("o p c -> (o p) c"))\
                  .then_inc(w_in[l % 2], 16)
        load(29)
        load(30)
        sp.wait_ge(proj, GATES_DONE)
        for k in range(KT):
            sp.dma_start(w_out_raw[:, k, :], a["w_out"][k * P:(k + 1) * P, :]).then_inc(tile_in[k], 16)
        load(31)

    def gpsimd(pool):
        def split(l, at):
            n = width(l)
            pool.wait_ge(proj, 2 * at + (PROJ0 - 2))
            pool.wait_ge(w_in[l % 2], 8 * at + (8 * (Q0 - l % 2) + 16))
            nc.gpsimd.tensor_tensor(whi[:, l % 2, 0:n], raw[:, l % 2, 0:n], zero[:].broadcast_to([P, n]), ALU.add).then_inc(pool_s, 1)
            pool.wait_ge(pool_s, at + (Q0 + 1))
            nc.gpsimd.tensor_tensor(wlo[:, l % 2, 0:n], raw[:, l % 2, 0:n], whi[:, l % 2, 0:n].bitcast(F32), ALU.subtract)\
              .then_inc(w_split, 1)

        for l in range(4):
            split(l, l)
        with pool.Fori(0, KT // 2 - 1) as t:
            for j in range(8):
                split(4 + j, t * 8 + (4 + j))
        for l in range(28, 32):
            split(l, l)

    def tensor(pe):
        def product(l, at, j, bank_free, k0, kn, x_hi, x_lo, x_done=None):
            pe.wait_ge(w_split, at + (SPLIT0 + 1))
            for h in range(2):
                bank_free(h)
                for k in range(kn):
                    if x_done is not None and h == 0:
                        pe.wait_ge(x_done, k0 + k + 1)
                    mm = three_pass(nc.tensor, ps[:, 2 * j + h, :], whi[:, l % 2, k * P:(k + 1) * P], wlo[:, l % 2, k * P:(k + 1) * P],
                                    x_hi[:, k0 + k, h * HALF:(h + 1) * HALF], x_lo[:, k0 + k, h * HALF:(h + 1) * HALF],
                                    k == 0, k == kn - 1)
                mm.then_inc(proj, 1)

        def gates(l, at, m):
            for j in range(2):
                def sigmoid_read(h):
                    if isinstance(m, int) and m == 0:
                        if j == 0:
                            pe.wait_ge(kept[h], HEADS * MAIN + 1)
                        else:
                            pe.wait_ge(out_used, 4 * HEADS + 4)
                    else:
                        pe.wait_ge(sig_done, 4 * m + (2 * j + h - 3))
                product(l + j, at + j, j, sigmoid_read, 0, KT, h_hi, h_lo)

        def branches(l, at, m):
            def merged(h):
                pe.wait_ge(merged_half, 4 * m + (2 * h + 1))
            product(l, at, 2, merged, 0, KT, b_hi, b_lo, b_lo_done)
            product(l + 1, at + 1, 3, merged, KT, KA, b_hi, b_lo, b_lo_done)

        for m in range(2):
            gates(2 * m, 2 * m, m)
        pe.wait_ge(out_used, 4 * HEADS + 4)
        pe.wait_ge(masked, 24 * HEADS + 1)
        pe.wait_ge(p_kept, 12 * HEADS + 1)
        pe.wait_ge(pv_kept, 12 * HEADS + 1)
        with pe.Fori(0, KT // 2 - 1) as t:
            for b in range(2):
                branches(4 + 4 * b, t * 8 + (4 + 4 * b), t * 2 + b)
                gates(6 + 4 * b, t * 8 + (6 + 4 * b), t * 2 + (b + 2))
        for m in (KT - 2, KT - 1):
            branches(branches_at(m), branches_at(m), m)



    def scalar(act):
        A = nc.scalar.activation

        def sigmoids(m, b, j, at):
            for h in range(2):
                act.wait_ge(proj, 2 * at + (PROJ0 + h + 1))
                A(qa[:, b, j, h * HALF:(h + 1) * HALF], ps[:, 2 * j + h, :], ACT.Sigmoid).then_inc(sig_done, 1)

        def split_high(ks):
            for k in ks:
                act.wait_ge(tile_in[k], 16)
                A(b_hi[:, k, :], b_raw[:, k, :], ACT.Copy).then_inc(b_hi_done, 1)

        act.sem_inc(mg_out, 16)
        for j, ks in enumerate((range(0, 3), range(3, 6), range(6, 9), range(9, 12))):
            sigmoids(j // 2, j // 2, j % 2, j)
            split_high(ks)
        with act.Fori(0, KT // 2 - 1) as t:
            for b in range(2):
                act.wait_ge(merged_half, t * 8 + (4 * b + 8))
                act.dma_start(mg_d[bass.ds(t * 2 + b, 1)].rearrange("o p s -> (o p) s"), mg[:]).then_inc(mg_out, 16)
                for j in range(2):
                    sigmoids(t * 2 + (b + 2), b, j, t * 8 + (4 * b + 6 + j))
        for k in range(KT):
            if k == 2:
                act.wait_ge(merged_half, 4 * (KT - 1) + 4)
                act.dma_start(mg_d[KT - 2], mg[:]).then_inc(mg_out, 16)
            act.wait_ge(tile_in[k], 32)
            A(h_hi[:, k, :], w_out_raw[:, k, :], ACT.Copy).then_inc(w_hi_done, 1)
        act.wait_ge(merged_half, 4 * KT + 4)
        act.dma_start(mg_d[KT - 1], mg[:]).then_inc(mg_out, 16)

    def vector(dve):
        v = nc.vector

        def merge_tile(m, b, at):
            for h in range(2):
                tok = slice(h * HALF, (h + 1) * HALF)
                sa, sc = qa[:, b, 0, tok], qa[:, b, 1, tok]
                dve.wait_ge(sig_done, 4 * m + 4)
                dve.wait_ge(proj, 2 * at + (PROJ0 + h + 1))
                if h == 0:
                    dve.wait_ge(mg_out, 16 * m + 16)
                v.tensor_tensor(mg[:, tok], sa, ps[:, 4 + h, :], ALU.mult).then_inc(dve_s, 1)
                v.tensor_tensor(sc, sc, ps[:, 6 + h, :], ALU.mult).then_inc(merged_half, 1)
                dve.wait_ge(dve_s, 2 * m + (h + 1))
                dve.wait_ge(merged_half, 4 * m + (2 * h + 5))
                v.tensor_tensor(mg[:, tok], mg[:, tok], sc, ALU.add).then_inc(merged_half, 1)

        def w_out_low(ks):
            for k in ks:
                dve.wait_ge(w_hi_done, k + 1)
                v.tensor_tensor(h_lo[:, k, :], w_out_raw[:, k, :], h_hi[:, k, :].bitcast(F32), ALU.subtract).then_inc(w_lo_done, 1)

        dve.sem_inc(merged_half, 4)
        for k in range(KB):
            dve.wait_ge(b_hi_done, k + 1)
            v.tensor_tensor(b_lo[:, k, :], b_raw[:, k, :], b_hi[:, k, :].bitcast(F32), ALU.subtract).then_inc(b_lo_done, 1)
        with dve.Fori(0, KT // 2 - 1) as t:
            for b in range(2):
                merge_tile(t * 2 + b, b, t * 8 + (4 * b + 5))
        w_out_low(range(0, 2))
        merge_tile(KT - 2, 0, branches_at(KT - 2) + 1)
        w_out_low(range(2, KT))
        merge_tile(KT - 1, 1, branches_at(KT - 1) + 1)

    return {"sync": sync, "gpsimd": gpsimd, "tensor": tensor, "scalar": scalar, "vector": vector}


def finish(nc, a, out, sem, ps, T):
    mg_d, mod_d, w_hi, w_lo, zero = (T[n] for n in ("mg_d", "mod_d", "h_hi", "h_lo", "zero"))
    w_lo_done, mg_out, merged_half, proj, sig_done = (T[n] for n in ("w_lo_done", "mg_out", "merged_half", "proj", "sig_done"))
    m_hi, m_lo, gate, gf, xt, y, junk, sc = T["finishing"].values()
    mg = T["kept_on"]["num1"]
    mr = T["kept_on"]["qa"][:, 0].rearrange("p b (k c) -> p b k c", k=KT)
    row_in, m_in, x_in = sem("row_in"), [sem("m_in0"), sem("m_in1")], [sem("xr_in0"), sem("xr_in1")]
    m_hi_done, m_split, prod, added = (sem(n) for n in ("m_hi_done", "m_split", "prod", "added"))
    sq_done, ln_done, var_done, y_done, act_s, dve_s = (sem(n) for n in ("sq_done", "lnf_done", "varf_done", "y_done", "act_fin", "dve_fin"))
    y_out = [sem("y_out0"), sem("y_out1")]
    PER = 12
    BRANCH_DONE = 4 + 2 * (HEADS * MAIN + branches_at(KT - 1) + 1)

    def sync(sp):
        for b in range(2):
            sp.sem_inc(y_out[b], 16)
        sp.wait_ge(proj, BRANCH_DONE)
        sp.dma_start(gate[:], mod_d[0:1, 2 * D:3 * D].broadcast_to([P, D])).then_inc(row_in, 16)
        sp.dma_start(gf[:], a["g_final"].broadcast_to([P, D])).then_inc(row_in, 16)
        with sp.Fori(0, NCH // 2) as t:
            for b in range(2):
                sp.wait_ge(y_done, t * 2 + b + 1)
                sp.dma_start(out[bass.ds((t * 2 + b) * P, P), :], y[:, b, :]).then_inc(y_out[b], 16)
        for b in range(2):
            sp.wait_ge(y_out[b], 16 * (NCH // 2) + 16)

    def gpsimd(pool):
        rows = mg_d.rearrange("k p s -> p k s")

        def split(b, ks, m_raw, done):
            nc.gpsimd.tensor_tensor(m_hi[:, b, ks], m_raw, zero[:].unsqueeze(2).broadcast_to([P, ks.stop - ks.start, P]), ALU.add)\
              .then_inc(m_hi_done, 1)
            pool.wait_ge(m_hi_done, done)
            return nc.gpsimd.tensor_tensor(m_lo[:, b, ks], m_raw, m_hi[:, b, ks].bitcast(F32), ALU.subtract)

        pool.wait_ge(mg_out, 16 * KT)
        pool.dma_start(mr[:, 0, 0:KT - 1], rows[:, 0:KT - 1, 0:P]).then_inc(m_in[0], 16)
        pool.wait_ge(proj, BRANCH_DONE)
        pool.wait_ge(m_in[0], 16)
        split(0, slice(0, KT - 1), mr[:, 0, 0:KT - 1], 1)
        pool.wait_ge(merged_half, 4 * KT + 2)
        split(0, slice(KT - 1, KT), mg[:, 0:P].unsqueeze(1), 2).then_inc(m_split, 1)
        pool.wait_ge(mg_out, 16 * KT + 16)
        pool.dma_start(mr[:, 1], rows[:, :, P:2 * P]).then_inc(m_in[1], 16)
        pool.wait_ge(m_in[1], 16)
        split(1, slice(0, KT), mr[:, 1], 3).then_inc(m_split, 1)
        with pool.Fori(1, NCH // 2) as t:
            for b in range(2):
                pool.wait_ge(m_split, t * 2 + (b - 1))
                pool.dma_start(mr[:, b], rows[:, :, bass.ds((t * 2 + b) * P, P)]).then_inc(m_in[b], 16)
                pool.wait_ge(prod, t * 4 + (2 * b - 2))
                pool.wait_ge(m_in[b], t * 16 + 16)
                split(b, slice(0, KT), mr[:, b], t * 2 + (b + 2)).then_inc(m_split, 1)

    def tensor(pe):
        pe.wait_ge(sig_done, 4 * KT)
        with pe.Fori(0, NCH // 2) as t:
            for b in range(2):
                pe.wait_ge(m_split, t * 2 + b + 1)
                pe.wait_ge(added, t * 2 + b + 1)
                for h in range(2):
                    for k in range(KT):
                        if b == 0 and h == 0:
                            pe.wait_ge(w_lo_done, k + 1)
                        cols = slice(h * HALF, (h + 1) * HALF)
                        mm = three_pass(nc.tensor, ps[:, 2 * b + h, :], m_hi[:, b, k, :], m_lo[:, b, k, :], w_hi[:, k, cols],
                                        w_lo[:, k, cols], k == 0, k == KT - 1)
                    mm.then_inc(prod, 1)

    def scalar(act):
        A = nc.scalar.activation
        act.wait_ge(proj, BRANCH_DONE)
        with act.Fori(0, NCH // 2) as t:
            for b in range(2):
                act.wait_ge(added, t * 2 + b + 1)
                act.dma_start(xt[:, b, :], a["x"][bass.ds((t * 2 + b) * P, P), :]).then_inc(x_in[b], 16)
                act.wait_ge(var_done, t * 4 + 2 * b + 1)
                A(junk[:], y[:, b, :], ACT.Square, accum_out=sc[:, b, 0:1]).then_inc(sq_done, 1)
                act.wait_ge(var_done, t * 4 + 2 * b + 2)
                A(sc[:, b, 2:3], sc[:, b, 1:2], ACT.Ln).then_inc(act_s, 1)
                act.wait_ge(act_s, t * 2 + b + 1)
                A(sc[:, b, 3:4], sc[:, b, 2:3], ACT.Exp, scale=-0.5).then_inc(ln_done, 1)

    def vector(dve):
        v = nc.vector
        dve.sem_inc(added, 2)
        dve.wait_ge(row_in, 32)
        with dve.Fori(0, NCH // 2) as t:
            step = Steps(dve, dve_s, t, PER)
            for b in range(2):
                dve.wait_ge(prod, t * 4 + 2 * b + 2)
                dve.wait_ge(y_out[b], (t + 1) * 16)
                step(v.tensor_tensor(y[:, b, :], gate[:], ps[:, 2 * b:2 * b + 2, :].rearrange("p h c -> p (h c)"), ALU.mult))
                dve.wait_ge(x_in[b], (t + 1) * 16)
                step(v.tensor_tensor(y[:, b, :], y[:, b, :], xt[:, b, :], ALU.add))
                v.tensor_copy(sc[:, b, 5:6], y[:, b, 0:1]).then_inc(var_done, 1)
                v.tensor_copy(sc[:, b, 4:5], y[:, b, 0:1]).then_inc(added, 1)
                dve.wait_ge(sq_done, t * 2 + b + 1)
                v.tensor_scalar(sc[:, b, 1:2], sc[:, b, 0:1], 1.0 / D, EPS, ALU.mult, ALU.add).then_inc(var_done, 1)
                dve.wait_ge(ln_done, t * 2 + b + 1)
                r, w = sc[:, b, 3:4], sc[:, b, 4:5]
                step(v.scalar_tensor_tensor(w, r, sc[:, b, 1:2], r, ALU.mult, ALU.mult))
                step(v.tensor_scalar(w, w, -0.5, 1.5, ALU.mult, ALU.add))
                step(v.tensor_tensor(sc[:, b, 5:6], r, w, ALU.mult))
                step(v.tensor_scalar(y[:, b, :], y[:, b, :], sc[:, b, 5:6], None, ALU.mult))
                v.tensor_tensor(y[:, b, :], y[:, b, :], gf[:], ALU.mult).then_inc(y_done, 1)
            step.end()

    return {"sync": sync, "gpsimd": gpsimd, "tensor": tensor, "scalar": scalar, "vector": vector}


def kernel(**inputs):
    import concourse.bacc as bacc
    from concourse.bass_utils import run_bass_kernel_spmd

    x = {k: np.asarray(v) for k, v in inputs.items()}
    w_in = x["w_in"][0]

    def tiles(w):
        return np.ascontiguousarray(w.reshape(-1, P, w.shape[1]).transpose(1, 0, 2)).reshape(P, -1)

    mw = HEADS * DH
    gate0 = 4 * mw
    att0 = gate0 + 2 * HEADS
    qkv = GROUPS * HEADS * P
    zb0 = att0 + 3 * qkv
    main = np.empty((HEADS, MAIN, P, D), np.float32)
    for i in range(HEADS):
        starts = [0 + DH * i, DH * i + P, mw + DH * i, mw + DH * i + P, 2 * mw + DH * i, 2 * mw + DH * i + P]
        for g in range(GROUPS):
            starts += [att0 + j * qkv + (g * HEADS + i) * P for j in range(3)]
        starts += [3 * mw + DH * i, 3 * mw + DH * i + P, zb0 + i * P]
        for n, c in enumerate(starts):
            main[i, n] = tiles(w_in[:, c:c + P])
    gates = np.zeros((D, P), np.float32)
    gates[:, 0:HEADS] = w_in[:, gate0:gate0 + HEADS]
    gates[:, 32:32 + HEADS] = w_in[:, gate0 + HEADS:gate0 + 2 * HEADS]
    gate_bias = np.zeros((P, 2), np.float32)
    gate_bias[0:HEADS, 0] = x["b_igate"][0]
    gate_bias[32:32 + HEADS, 1] = x["b_fgate"][0]
    ga0 = zb0 + HEADS * P
    merging = np.zeros((4 * KT, P, D), np.float32)
    for m in range(KT):
        c = slice(m * P, (m + 1) * P)
        merging[gates_at(m)] = tiles(w_in[:, ga0:ga0 + D][:, c])
        merging[gates_at(m) + 1] = tiles(w_in[:, ga0 + D:ga0 + 2 * D][:, c])
        merging[branches_at(m)] = tiles(x["w_out_mlstm"][0][:, c])
        merging[branches_at(m) + 1, :, 0:HEADS * P] = tiles(x["w_out_attn"][0][:, c])
    hp = np.zeros((P, HEADS, 2, 8), np.float32)
    per = lambda w: w.reshape(HEADS, 2, P).transpose(2, 0, 1)
    for j in range(4):
        hp[..., j] = per(x["w_conv"][0, j])
    hp[..., 4], hp[..., 5], hp[..., 6] = per(x["b_conv"][0]), per(x["skip_mlstm"][0]), per(x["g_mlstm_head"][0])
    wqk = np.stack([x["w_q_mlstm"][0], x["w_k_mlstm"][0]], 1)
    wqk = np.ascontiguousarray(wqk.reshape(HEADS, 2, 2, P, DH).transpose(0, 3, 1, 2, 4))
    half = ROPE // 2
    freq = THETA ** (-np.arange(half, dtype=np.float32) / half)
    rope = np.stack([np.tile(freq, 2), np.repeat([-1.0, 1.0], half)], 1).astype(np.float32)
    arrays = {
        "x": x["x"][0], "c_cols": np.ascontiguousarray(x["c"].reshape(KT, P).T), "positions": x["positions"].astype(np.int32),
        "w_ada": x["w_ada"][0], "b_ada": x["b_ada"], "g_cols": np.ascontiguousarray(x["g_norm"].reshape(KT, P).T),
        "gate_bias": gate_bias, "rope_const": rope, "w_gates": tiles(gates), "w_all": np.concatenate([main.reshape(-1, P, D), merging]), "head_params": hp, "w_qk": wqk,
        "w_out": x["w_out"][0], "g_final": x["g_final"].reshape(1, D),
    }
    nc = bacc.Bacc("TRN2", target_bir_lowering=False, num_devices=1)
    feed, aps = {}, {}
    for k, v in arrays.items():
        feed["in_" + k] = np.ascontiguousarray(v)
        aps[k] = nc.dram_tensor("in_" + k, v.shape, mybir.dt.from_np(v.dtype), kind="ExternalInput").ap()
    out = nc.dram_tensor("out_rows", (S, D), F32, kind="ExternalOutput").ap()
    build(nc, aps, out)
    r = run_bass_kernel_spmd(nc, [feed], core_ids=[0])
    return r.results[0]["out_rows"].reshape(1, S, D)
```

```python
from contextlib import ExitStack

import numpy as np
import concourse.bass as bass
from concourse import mybir

F32, F32R, I32 = mybir.dt.float32, mybir.dt.float32r, mybir.dt.int32
ACT, ALU, AX = mybir.ActivationFunctionType, mybir.AluOpType, mybir.AxisListType

P = 128
D = 1024
S = 1024
KT = D // P
HALF = 512
HEADS, DH = 4, 256
NCH = S // P
GROUPS = 3
DIL = (1, 4, 16)
ROPE, THETA = 32, 500000.0
EPS = 1e-6
NEG = -1e30
SCALE = 128.0 ** -0.5
KSCALE = DH ** -0.5
MAIN = 18
XA, VA, OA, QKV, ZA, ZB = 0, 2, 4, 6, 15, 17
TOKEN_BANKS = {VA: (2, 3, 4, 5), OA: (0, 1, 6, 7)}
AHEAD = 4
NADA = 5
PI = float(np.pi)


class Steps:

    def __init__(self, eng, sem, turn=0, per_turn=0):
        self.eng, self.sem, self.base, self.per, self.n = eng, sem, turn * per_turn, per_turn, 0

    def __call__(self, ins):
        self.n += 1
        ins.then_inc(self.sem, 1)
        self.eng.wait_ge(self.sem, self.base + self.n)

    def end(self):
        assert not self.per or self.n == self.per, self.n


def order(ap, g, lo=0, n=S):
    return ap[:, lo:lo + n].rearrange("p (u r) -> p r u", r=DIL[g])


def stored(ap, g, lo=0, n=S):
    d = DIL[g]
    return ap.rearrange("p (r u) -> p r u", r=d)[:, :, lo // d:(lo + n) // d]


def build(nc, a, out):
    with ExitStack() as top:
        def sem(name):
            return top.enter_context(nc.semaphore(name))

        def sb(name, shape, dt=F32, ctx=top):
            return ctx.enter_context(nc.sbuf_tensor(name, shape, dt))

        def dram(name, shape):
            return nc.dram_tensor(name, shape, F32, kind="Internal").ap()

        ps = top.enter_context(nc.psum_tensor("banks", [P, 8, HALF], F32))
        acc_d = dram("gate_products", [P, D])
        rows_d = dram("gate_rows", [HEADS, 4, S])
        r1_d = dram("log_weight_rows", [HEADS, S])
        wi_d = dram("chunk_decay_rows", [HEADS, NCH])
        stat_d = dram("softmax_stats", [GROUPS, S, 2])
        coef_d = dram("group_weights", [GROUPS, S])
        um_d = dram("mlstm_branch", [HEADS, 2, P, S])
        ua_d = dram("attn_branch", [HEADS, P, S])
        mg_d = dram("merged", [KT, P, S])

        ident = sb("ident", [P, P])
        zero = sb("zero", [P, 1])
        band = sb("band", [P, 2 * P])
        diag = sb("diag", [P, P])

        h_hi = sb("h_hi", [P, KT, S], F32R)
        with ExitStack() as ctx:
            raw_lo = sb("raw_lo", [P, KT, D], F32, ctx)
        h_lo = sb("h_lo", [P, KT, S], F32R)

        with ExitStack() as ctx:
            ring = buffers(sb, ctx, RING)
            with ExitStack() as inner:
                setting = buffers(sb, inner, SETTING)
            with ExitStack() as inner:
                xc_hi = sb("xc_hi", [P, 2, S], F32R, inner)
                xc_lo = sb("xc_lo", [P, 2, S], F32R, inner)
                wqk_hi = sb("wqk_hi", [P, 2, 2, DH], F32R, inner)
            kept_on = ring | buffers(sb, ctx, STREAM)
            with ExitStack() as inner:
                mixing = buffers(sb, inner, MIXING)
            with ExitStack() as inner:
                b_hi = sb("b_hi", [P, KT + HEADS, S], F32R, inner)
                with ExitStack() as raw:
                    b_raw = sb("b_raw", [P, KT + HEADS, S], F32, raw)
                b_lo = sb("b_lo", [P, KT + HEADS, S], F32R, inner)
            with ExitStack() as inner:
                finishing = buffers(sb, inner, FINISHING)

        w_in, um_out = [[sem(f"{n}{b}") for b in range(2)] for n in ("w_in", "um_out")]
        kept = [sem("kept0"), sem("kept1")]
        tile_in = [sem(f"tile_in{k}") for k in range(KT + HEADS)]
        w_split, pool_s, proj = sem("w_split"), sem("pool_split"), sem("proj")
        out_used, masked, p_kept, pv_kept, ua_done, ua_out = (sem(n) for n in ("out_used", "masked", "p_kept", "pv_kept", "ua_done", "ua_out"))
        w_hi_done, w_lo_done, sig_done, mg_out = sem("wo_hi_done"), sem("wo_lo_done"), sem("sig_done"), sem("mg_out")
        hp_in, added, rows_ready = sem("hp_in"), sem("added"), sem("rows_ready")
        merged_half, b_hi_done, b_lo_done = sem("merged_half"), sem("b_hi_done"), sem("b_lo_done")

        def first_weights(sp, chunks):
            for q in chunks:
                if q >= 2:
                    sp.wait_ge(w_split, q + 1)
                sp.dma_start(ring["wraw"][:, q % 2, :], a["w_all"][q]).then_inc(w_in[q % 2], 16)

        stages = [setup(nc, a, sem, ps, locals()), mix(nc, a, sem, ps, locals()), merge(nc, a, sem, ps, locals()), finish(nc, a, out, sem, ps, locals())]
        block = top.enter_context(nc.Block())

        @block.sync
        def _(sp):
            for stage in stages:
                stage["sync"](sp)

        @block.gpsimd
        def _(pool):
            for stage in stages:
                stage["gpsimd"](pool)

        @block.tensor
        def _(pe):
            for stage in stages:
                stage["tensor"](pe)

        @block.scalar
        def _(act):
            for stage in stages:
                stage["scalar"](act)

        @block.vector
        def _(dve):
            for stage in stages:
                stage["vector"](dve)


def buffers(sb, ctx, table):
    return {name: sb(name, shape, dt, ctx) for name, shape, dt in table}


RING = [("wraw", [P, 2, D], F32), ("whi", [P, 2, D], F32R), ("wlo", [P, 2, D], F32R)]
SETTING = [
    ("s_xnT", [P, KT, S], F32),
    ("s_gw_raw", [P, KT, P], F32), ("s_gw_hi", [P, KT, P], F32R), ("s_gw_lo", [P, KT, P], F32R), ("s_sq", [P, D], F32),
    ("s_cc", [P, 3, KT], F32), ("s_crow", [P, 3, D], F32),
    ("s_gn", [P, KT], F32), ("s_bc", [P, 2 * KT], F32), ("s_ms", [P, 3, KT], F32), ("s_xs", [P, 6, KT], F32),
    ("s_gb", [P, 2], F32), ("s_rc", [ROPE, 2], F32), ("s_halfpi", [P, 1], F32),
    ("s_angle", [ROPE, 3, S], F32), ("s_acc_g", [P, D], F32), ("s_wada", [P, NADA, D], F32), ("s_starts", [HEADS, S], F32),
    ("s_mprev", [HEADS, NCH], F32), ("s_wlast", [HEADS, NCH], F32),
]
STREAM = [
    ("qa", [P, 2, 2, S], F32),
    ("num1", [P, S], F32),
]
MIXING = [
    ("v1", [P, NCH, DH + 2], F32), ("og", [P, NCH, DH], F32),
    ("hp", [P, 2, 8], F32), ("hc", [P, 4, NCH], F32),
    ("gr", [4 * NCH, P], F32),
    ("turn", [P, 2, 3 + S], F32),
    ("cv", [P, S], F32), ("sg", [P, S], F32), ("xc", [P, 2, S], F32),
    ("wqk", [P, 2, 2, DH], F32), ("ew", [P, NCH, P], F32), ("dec", [P, NCH], F32),
    ("wqk_lo", [P, 2, 2, DH], F32R),
    ("qm", [P, 2, S], F32), ("km", [P, 2, S], F32),
    ("sw", [P, 2, P], F32), ("kw", [P, 2, DH], F32), ("cst", [P, 2, DH + 1], F32),
    ("hin", [P, DH + 1], F32), ("hnb", [P, DH + 1], F32), ("small", [P, 4], F32), ("vr", [P, 6, NCH], F32),
    ("vt", [P, NCH, P], F32), ("sm", [P, 2, 2, 2 * P], F32), ("pT", [P, 2, 2, P], F32),
    ("nm", [P, 2, 2], F32), ("st", [P, GROUPS, NCH, 2], F32), ("ct", [P, GROUPS, NCH, 2], F32), ("cw", [P, 4, GROUPS, NCH], F32),
    ("hpa", [P, HEADS, 2, 8], F32), ("cosT", [ROPE, S], F32), ("sinT", [ROPE, S], F32),
]
FINISHING = [
    ("m_hi", [P, 2, KT, P], F32R), ("m_lo", [P, 2, KT, P], F32R),
    ("gate", [P, D], F32), ("gf", [P, D], F32),
    ("bg", [P, D], F32), ("ones", [P, P], F32), ("x_rows", [P, 2, D], F32), ("y", [P, 2, D], F32),
    ("junk", [P, D], F32), ("row_stats", [P, 2, 7], F32),
]


def setup(nc, a, sem, ps, T):
    ident, zero, band, diag = T["ident"], T["zero"], T["band"], T["diag"]
    h_hi, h_lo, x_raw = T["h_hi"], T["h_lo"], T["raw_lo"]
    cosT, sinT = T["mixing"]["cosT"], T["mixing"]["sinT"]
    tile_in, acc_d, rows_d, r1_d, wi_d = T["tile_in"], T["acc_d"], T["rows_d"], T["r1_d"], T["wi_d"]
    xnT, gw_raw, gw_hi, gw_lo, sq, cc, crow, gn, bc, ms, xs, gb, rc, halfpi, angle, acc_g, wada, starts, mprev, wlast = \
        T["setting"].values()

    posi = angle[:, 1, :].bitcast(I32)
    small_in, c_in, pos_in, gw_in = sem("small_in"), sem("c_in"), sem("pos_in"), sem("gw_in")
    ada_in = [sem(f"ada_in{j}") for j in range(NADA)]
    ada_used, gw_split, consts, rope_s = sem("ada_used"), sem("gw_split"), sem("consts"), sem("rope_steps")
    c_sig, c_silu, x_sq, x_var, x_ln, x_norm, x_turned = \
        (sem(n) for n in ("c_sig", "c_silu", "x_sq", "x_var", "x_ln", "x_norm", "x_turned"))
    x_kept = sem("x_kept")
    ms_ready, h_full, g_ready = (sem(n) for n in ("ms_ready", "h_full", "g_ready"))
    DVE_HIGH, DVE_LOW = (5, 7), (5, 6, 7)
    h_high = [sem("h_high_act"), sem("h_high_dve")]
    h_low = [sem("h_low_pool"), sem("h_low_dve")]

    def high_done(eng, k):
        on = k in DVE_HIGH
        eng.wait_ge(h_high[on], sum((j in DVE_HIGH) == on for j in range(k + 1)))

    def low_done(eng, k):
        on = k in DVE_LOW
        eng.wait_ge(h_low[on], sum((j in DVE_LOW) == on for j in range(k + 1)))
    dve_s, act_s, pool_s = sem("dve_setup"), sem("act_setup"), sem("pool_setup")
    rows_ready = T["rows_ready"]
    rope_arg, rope_abs, gate_abs, gate_ls, setup_out = (sem(n) for n in ("rope_arg", "rope_abs", "gate_abs", "gate_ls", "setup_out"))

    def sync(sp):
        def load_ada(j):
            if j >= NADA:
                sp.wait_ge(ada_used, j - NADA + 1)
            src = a["w_ada_cols"][j] if j < 2 * KT else a["w_ada_gate"][(j - 2 * KT) * P:(j - 2 * KT + 1) * P, :]
            sp.dma_start(wada[:, j % NADA, :], src).then_inc(ada_in[j % NADA], 16)

        sp.dma_start(crow[:, 0, :], a["c_row"].broadcast_to([P, D])).then_inc(c_in, 16)
        sp.dma_start(cc[:, 0, :], a["c_cols"]).then_inc(c_in, 16)
        for t in range(NCH):
            if t == NCH - 1:
                sp.dma_start(T["mixing"]["hpa"][:], a["head_params"]).then_inc(T["hp_in"], 16)
            sp.dma_start(x_raw[:, t, :], a["x"][t * P:(t + 1) * P, :]).then_inc(tile_in[t], 16)
        for j in range(2 * KT):
            load_ada(j)
        T["first_weights"](sp, range(0, 2))
        for j in range(2 * KT, 3 * KT):
            load_ada(j)
            if j == 2 * KT + 4:
                T["first_weights"](sp, range(2, AHEAD))
        sp.wait_ge(ada_used, 3 * KT)
        sp.dma_start(acc_d, acc_g[:]).then_inc(setup_out, 16)
        sp.wait_ge(rows_ready, 4)
        sp.dma_start(rows_d.rearrange("h q s -> h q s"), xnT[0:HEADS, 0:4, :]).then_inc(setup_out, 16)
        sp.dma_start(r1_d, xnT[0:HEADS, 4, :]).then_inc(setup_out, 16)
        sp.dma_start(wi_d, wlast[0:HEADS, :]).then_inc(setup_out, 16)
        sp.wait_ge(setup_out, 64)

    def gpsimd(pool):
        nc.gpsimd.memset(zero[:], 0.0).then_inc(pool_s, 1)
        nc.gpsimd.memset(ident[:], 0.0).then_inc(pool_s, 1)
        nc.gpsimd.memset(band[:], 0.0).then_inc(pool_s, 1)
        nc.gpsimd.memset(diag[:], 0.0).then_inc(pool_s, 1)
        nc.gpsimd.memset(halfpi[:], PI / 2).then_inc(pool_s, 1)
        nc.gpsimd.memset(starts[:], 1.0).then_inc(pool_s, 1)
        nc.gpsimd.memset(mprev[:], 0.0).then_inc(pool_s, 1)
        pool.wait_ge(pool_s, 7)
        nc.gpsimd.affine_select(out=ident[:], in_=ident[:], compare_op=ALU.not_equal, fill=1.0, base=0,
                                pattern=[[-1, P]], channel_multiplier=1).then_inc(consts, 1)
        nc.gpsimd.affine_select(out=band[:, 0:P], in_=band[:, 0:P], compare_op=ALU.is_ge, fill=NEG, base=0,
                                pattern=[[1, P]], channel_multiplier=-1).then_inc(consts, 1)
        nc.gpsimd.affine_select(out=band[:, P:], in_=band[:, P:], compare_op=ALU.is_ge, fill=NEG, base=0,
                                pattern=[[-1, P]], channel_multiplier=1).then_inc(consts, 1)
        nc.gpsimd.affine_select(out=diag[:], in_=diag[:], compare_op=ALU.is_ge, fill=NEG, base=0,
                                pattern=[[-1, P]], channel_multiplier=1).then_inc(consts, 1)
        nc.gpsimd.memset(starts[:, 0::P], 0.0).then_inc(consts, 1)
        pool.wait_ge(consts, 5)
        nc.gpsimd.memset(diag[64:128, 0:64], NEG).then_inc(consts, 1)
        pool.wait_ge(consts, 6)
        pool.wait_ge(gw_in, 16)
        nc.gpsimd.tensor_tensor(gw_hi[:], gw_raw[:], zero[:].unsqueeze(2).broadcast_to([P, KT, P]), ALU.add).then_inc(gw_split, 1)
        pool.wait_ge(gw_split, 1)
        nc.gpsimd.tensor_tensor(gw_lo[:], gw_raw[:], gw_hi[:].bitcast(F32), ALU.subtract).then_inc(gw_split, 1)
        for k in [k for k in range(KT) if k not in DVE_LOW]:
            high_done(pool, k)
            nc.gpsimd.tensor_tensor(h_lo[:, k, :], xnT[:, k, :], h_hi[:, k, :].bitcast(F32), ALU.subtract).then_inc(h_low[0], 1)

    def scalar(act):
        for b in range(2):
            act.sem_inc(T["kept"][b], 1)
        A = nc.scalar.activation
        step = Steps(act, act_s)
        act.dma_start(posi, a["positions"].partition_broadcast(ROPE)).then_inc(pos_in, 16)
        act.dma_start(rc[:], a["rope_const"]).then_inc(small_in, 16)
        act.dma_start(gn[:], a["g_cols"]).then_inc(small_in, 16)
        act.dma_start(bc[:], a["b_cols"]).then_inc(small_in, 16)
        act.dma_start(gb[:], a["gate_bias"]).then_inc(small_in, 16)
        act.dma_start(gw_raw[:], a["w_gates"].rearrange("p (k c) -> p k c", k=KT)).then_inc(gw_in, 16)
        act.wait_ge(c_in, 32)
        A(crow[:, 1, :], crow[:, 0, :], ACT.Sigmoid).then_inc(c_sig, 1)
        A(cc[:, 1, :], cc[:, 0, :], ACT.Sigmoid).then_inc(c_sig, 1)
        act.wait_ge(small_in, 64)
        for t in range(NCH):
            act.wait_ge(tile_in[t], 16)
            if t:
                act.wait_ge(x_sq, t)
            A(sq[:], x_raw[:, t, :], ACT.Square, accum_out=xs[:, 0, t:t + 1]).then_inc(x_sq, 1)
        act.wait_ge(x_var, 1)
        step(A(xs[:, 2, :], xs[:, 1, :], ACT.Ln))
        A(xs[:, 3, :], xs[:, 2, :], ACT.Exp, scale=-0.5).then_inc(x_ln, 1)
        act.wait_ge(rope_arg, 1)
        act.wait_ge(consts, 6)
        A(sinT[:], angle[:, 2, :], ACT.Sin).then_inc(rope_abs, 1)
        step(A(angle[:, 1, :], angle[:, 2, :], ACT.Abs))
        A(cosT[:], angle[:, 1, :], ACT.Sin, scale=-1.0, bias=halfpi[0:ROPE, :]).then_inc(rope_abs, 1)
        for t in range(NCH):
            act.wait_ge(x_turned, t + 1)
            for h in range(2):
                A(xnT[:, 4 * h:4 * h + 4, t * P:(t + 1) * P], ps[:, 4 + 2 * (t % 2) + h, :].rearrange("p (k c) -> p k c", k=4),
                  ACT.Copy).then_inc(x_kept, 1)
        act.wait_ge(x_kept, 2 * NCH)
        for k in range(KT):
            act.wait_ge(ms_ready, k + 1)
            A(xnT[:, k, :], xnT[:, k, :], ACT.Identity, scale=ms[:, 0, k:k + 1], bias=ms[:, 1, k:k + 1]).then_inc(h_full, 1)
            if k not in DVE_HIGH:
                act.wait_ge(h_full, k + 1)
                A(h_hi[:, k, :], xnT[:, k, :], ACT.Copy).then_inc(h_high[0], 1)
        act.wait_ge(g_ready, 2)
        low_done(act, max(k for k in range(KT) if k not in DVE_LOW))
        low_done(act, max(DVE_LOW))
        step(A(xnT[0:HEADS, 2, :], ps[32:32 + HEADS, 2:4, :], ACT.Abs, bias=gb[32:32 + HEADS, 1:2]))
        A(xnT[0:HEADS, 0, :], ps[0:HEADS, 2:4, :], ACT.Identity, bias=gb[0:HEADS, 0:1]).then_inc(gate_abs, 1)
        step(A(xnT[0:HEADS, 2, :], xnT[0:HEADS, 2, :], ACT.Exp, scale=-1.0))
        A(xnT[0:HEADS, 2, :], xnT[0:HEADS, 2, :], ACT.Ln, bias=1.0).then_inc(gate_ls, 1)

    def vector(dve):
        step = Steps(dve, dve_s)
        v = nc.vector
        dve.sem_inc(T["ua_done"], 1)
        dve.wait_ge(c_sig, 2)
        v.tensor_tensor(crow[:, 1, :], crow[:, 0, :], crow[:, 1, :], ALU.mult).then_inc(c_silu, 1)
        v.tensor_tensor(cc[:, 1, :], cc[:, 0, :], cc[:, 1, :], ALU.mult).then_inc(c_silu, 1)
        dve.wait_ge(c_silu, 2)
        dve.wait_ge(small_in, 64)

        def modulation(k):
            for j in (2, 1):
                n = 2 * k + 2 - j
                dve.wait_ge(ada_in[n % NADA], 16 * (n // NADA + 1))
                if n:
                    dve.wait_ge(ada_used, n)
                v.tensor_tensor_reduce(crow[:, 2, :], wada[:, n % NADA, :], crow[:, 1, :], 1.0,
                                       bc[:, (j - 1) * KT + k:(j - 1) * KT + k + 1], ALU.mult, ALU.add, ms[:, j, k:k + 1])\
                    .then_inc(ada_used, 1)
            dve.wait_ge(ada_used, 2 * k + 2)
            v.scalar_tensor_tensor(ms[:, 0, k:k + 1], ms[:, 2, k:k + 1], 1.0, gn[:, k:k + 1], ALU.add, ALU.mult).then_inc(ms_ready, 1)

        def high(k):
            dve.wait_ge(h_full, k + 1)
            v.tensor_copy(h_hi[:, k, :], xnT[:, k, :]).then_inc(h_high[1], 1)

        def low(k):
            high_done(dve, k)
            v.tensor_tensor(h_lo[:, k, :], xnT[:, k, :], h_hi[:, k, :].bitcast(F32), ALU.subtract).then_inc(h_low[1], 1)

        dve.wait_ge(pos_in, 16)
        ang, kk, tmp = (angle[:, j, :] for j in range(3))
        step(v.tensor_copy(tmp, posi))
        step(v.tensor_scalar(ang, tmp, rc[:, 0:1], None, ALU.mult))
        step(v.tensor_scalar(kk, ang, 1.0 / (2 * PI), 12582912.0, ALU.mult, ALU.add))
        step(v.tensor_scalar(kk, kk, 12582912.0, None, ALU.subtract))
        c1 = 6.28125
        c2 = float(np.float32(np.round((2 * PI - c1) * 2 ** 19) / 2 ** 19))
        c3 = float(np.float32(2 * PI - c1 - c2))
        for c in (c1, c2, c3):
            step(v.scalar_tensor_tensor(ang, kk, -c, ang, ALU.mult, ALU.add))
        v.tensor_scalar(tmp, ang, 3.1415925, -3.1415925, ALU.min, ALU.max).then_inc(rope_arg, 1)
        dve.wait_ge(x_sq, NCH)
        v.tensor_scalar(xs[:, 1, :], xs[:, 0, :], 1.0 / D, EPS, ALU.mult, ALU.add).then_inc(x_var, 1)
        modulation(0)
        dve.wait_ge(x_ln, 1)
        r, w = xs[:, 3, :], xs[:, 4, :]
        step(v.tensor_tensor(w, r, r, ALU.mult))
        step(v.tensor_tensor(w, w, xs[:, 1, :], ALU.mult))
        step(v.tensor_scalar(w, w, -0.5, 1.5, ALU.mult, ALU.add))
        step(v.tensor_tensor(xs[:, 5, :], r, w, ALU.mult))
        for t in range(NCH):
            v.tensor_scalar(x_raw[:, t, :], x_raw[:, t, :], xs[:, 5, t:t + 1], None, ALU.mult).then_inc(x_norm, 1)
        for k in range(1, KT):
            modulation(k)
        for k in range(KT):
            if k in DVE_HIGH:
                high(k)
            if k in DVE_LOW:
                low(k)
        dve.wait_ge(ada_used, 2 * KT)
        for k in range(KT):
            n = 2 * KT + k
            part = wada[:, n % NADA, :]
            dve.wait_ge(ada_in[n % NADA], 16 * (n // NADA + 1))
            if k:
                dve.wait_ge(ada_used, n)
                v.scalar_tensor_tensor(acc_g[:], part, cc[:, 1, k:k + 1], acc_g[:], ALU.mult, ALU.add).then_inc(ada_used, 1)
            else:
                v.tensor_scalar(acc_g[:], part, cc[:, 1, 0:1], None, ALU.mult).then_inc(ada_used, 1)
        row = lambda j: xnT[0:HEADS, j, :]
        by_chunk = lambda j: row(j).rearrange("p (c t) -> p c t", c=NCH)
        dve.wait_ge(gate_abs, 1)
        dve.wait_ge(consts, 6)
        step(v.tensor_scalar(row(7), ps[32:32 + HEADS, 2:4, :], gb[32:32 + HEADS, 1:2], 0.0, ALU.add, ALU.min))
        for s, n in ((T["out_used"], 4), (T["masked"], 1)):
            dve.sem_inc(s, n)
        dve.wait_ge(gate_ls, 1)
        step(v.tensor_tensor(row(7), row(7), row(2), ALU.subtract))
        step(v.tensor_tensor_scan(row(5), starts[:], row(7), 0.0, ALU.mult, ALU.add))
        step(v.tensor_tensor_scan(row(2), row(7), row(0), 0.0, ALU.add, ALU.max))
        step(v.tensor_tensor(row(4), row(5), row(2), ALU.subtract))
        step(v.tensor_copy(mprev[:, 1:NCH], row(2)[:, P - 1:S - P:P]))
        step(v.tensor_tensor(by_chunk(1), by_chunk(4), mprev[:].unsqueeze(2).broadcast_to([HEADS, NCH, P]), ALU.add))
        v.tensor_copy(wlast[:], row(1)[:, P - 1::P]).then_inc(rows_ready, 1)
        v.tensor_scalar(row(2), row(2), -1.0, None, ALU.mult).then_inc(rows_ready, 1)
        v.tensor_tensor(row(0), row(0), row(5), ALU.subtract).then_inc(rows_ready, 1)
        dve.wait_ge(rows_ready, 3)
        v.tensor_tensor(by_chunk(3), by_chunk(0), by_chunk(4)[:, :, P - 1:P].broadcast_to([HEADS, NCH, P]), ALU.add)\
            .then_inc(rows_ready, 1)
        dve.wait_ge(rope_abs, 2)
        step(v.tensor_scalar(sinT[:], sinT[:], rc[:, 1:2], None, ALU.mult))

    def tensor(pe):
        t_ = nc.tensor
        pe.sem_inc(T["proj"], 4)
        pe.wait_ge(consts, 1)
        for t in range(NCH):
            pe.wait_ge(x_norm, t + 1)
            if t >= 2:
                pe.wait_ge(x_kept, 2 * t - 2)
            for d in range(KT):
                mm = t_.transpose(ps[:, 4 + 2 * (t % 2) + d // 4, (d % 4) * P:(d % 4 + 1) * P], x_raw[:, t, d * P:(d + 1) * P],
                                  ident[:])
            mm.then_inc(x_turned, 1)
        pe.wait_ge(gw_split, 2)
        for k in range(KT):
            low_done(pe, k)
            for h in range(2):
                mm = three_pass(t_, ps[:, 2 + h, :], gw_hi[:, k, :], gw_lo[:, k, :], h_hi[:, k, h * HALF:(h + 1) * HALF],
                                h_lo[:, k, h * HALF:(h + 1) * HALF], k == 0, k == KT - 1)
                if k == KT - 1:
                    mm.then_inc(g_ready, 1)

    return {"sync": sync, "gpsimd": gpsimd, "tensor": tensor, "scalar": scalar, "vector": vector}


def three_pass(t_, out, w_hi, w_lo, x_hi, x_lo, first, last):
    t_.matmul(out, w_hi, x_hi, start=first, stop=False)
    t_.matmul(out, w_hi, x_lo, start=False, stop=False)
    return t_.matmul(out, w_lo, x_hi, start=False, stop=last)


def mix(nc, a, sem, ps, T):
    ident, zero, band, diag, h_hi, h_lo = (T[n] for n in ("ident", "zero", "band", "diag", "h_hi", "h_lo"))
    rows_d, r1_d, wi_d, stat_d, coef_d, um_d, ua_d = (T[n] for n in ("rows_d", "r1_d", "wi_d", "stat_d", "coef_d", "um_d", "ua_d"))
    w_in, um_out, kept, w_split, pool_s, proj = (T[n] for n in ("w_in", "um_out", "kept", "w_split", "pool_s", "proj"))
    out_used, masked, p_kept, pv_kept, ua_done, ua_out = (T[n] for n in ("out_used", "masked", "p_kept", "pv_kept", "ua_done", "ua_out"))
    wraw, whi, wlo, qa, num1 = (T["kept_on"][n] for n in ("wraw", "whi", "wlo", "qa", "num1"))
    v1, og, hp, hc, gr, turn, cv, sg, xc, wqk, ew, dec, wqk_lo, qm, km, sw, kw, cst, hin, hnb, small, vr, vt, sm, pT, nm, st, ct, cw, \
        hpa, cosT, sinT = T["mixing"].values()
    DVE_STEPS = 68
    xc_hi, xc_lo, wqk_hi = T["xc_hi"], T["xc_lo"], T["wqk_hi"]
    M0, M1, M2, A0, A1, A2 = (ps[:, b, :] for b in range(2, 8))
    og_flat = og[:].rearrange("p c e -> p (c e)")
    szb = og_flat[:, 0:S]
    num = [cv[:], num1[:], km[:, 1, :]]
    cb = [qm[:, 0, :], qm[:, 1, :], km[:, 0, :]]
    tn = [turn[:, b, 3:3 + S] for b in range(2)]

    summed, o_sig = sem("summed"), sem("o_sig")
    xc_high_done, xc_split, wqk_split = sem("xc_high_done"), sem("xc_split"), sem("wqk_split")
    hp_in, ready, gr_in, hc_turned, hc_done = (T["hp_in"], *(sem(n) for n in ("mix_ready", "gr_in", "hc_turned", "hc_done")))
    conv_done, conv_sig, xc_done, e_in, dec_in, wqk_in = (sem(n) for n in ("conv_done", "conv_sig", "xc_done", "e_in", "dec_in", "wqk_in"))
    e_arg, e_exp, qk_out, qk_kept = (sem(n) for n in ("e_arg", "e_exp", "qk_out", "qk_kept"))
    sk_out, sw_done, num_out, inter_kept, num_kept, gated = (sem(n) for n in ("sk_out", "sw_done", "num_out", "inter_kept", "num_kept", "gated"))
    squares, upd_out, state_done, var_done, ln_done, normed = (sem(n) for n in ("squares", "upd_out", "state_done", "var_done", "ln_done", "normed"))
    out_turned, z_sig, um_done, dve_s, act_s = (sem(n) for n in ("out_turned", "z_sig", "um_done", "dve_mix", "act_mix"))
    roped, v_turned, v_kept, score_out, max_done = (sem(n) for n in ("roped", "v_turned", "v_kept", "score_out", "max_done"))
    exp_done, p_turned, pv_out = (sem(n) for n in ("exp_done", "p_turned", "pv_out"))
    stat_out = [sem(f"stat_out{g}") for g in range(GROUPS)]
    ct_in, ct_arg, ct_exp, cw_done, coef_out = (sem(n) for n in ("ct_in", "ct_arg", "ct_exp", "cw_done", "coef_out"))
    cb_in = [sem(f"cb_in{g}") for g in range(GROUPS)]

    def stat_dest(g):
        if g == 0:
            return [(st[:, 0], stat_d[0].rearrange("(c p) w -> p c w", p=P))]
        if g == 1:
            x = stat_d[1].rearrange("(b p r) w -> r p b w", p=P, r=4)
            return [(st[:, 1, 2 * r:2 * r + 2, :], x[r]) for r in range(4)]
        x = stat_d[2].rearrange("(u c h) w -> h u c w", c=NCH, h=2)
        return [(st[64 * h:64 * h + 64, 2], x[h]) for h in range(2)]

    STATS = (1, 4, 2)

    def sync(sp):
        ahead = a["w_all"][AHEAD:AHEAD + HEADS * MAIN].rearrange("(i n) p c -> i n p c", n=MAIN)

        def weigh_groups(i):
            for g in range(GROUPS):
                sp.wait_ge(stat_out[g], i * (16 * STATS[g]) + 16 * STATS[g])
            sp.dma_start(ct[:].rearrange("p g c w -> p g (c w)"), stat_d.rearrange("g (p c) w -> p g (c w)", c=NCH)).then_inc(ct_in, 16)
            sp.wait_ge(cw_done, i + 1)
            sp.dma_start(coef_d.rearrange("g (p c) -> p g c", c=NCH), cw[:, 2]).then_inc(coef_out, 16)
            sp.wait_ge(coef_out, i * 16 + 16)
            for g in range(GROUPS):
                sp.dma_start(cb[g], coef_d[g:g + 1, :].broadcast_to([P, S])).then_inc(cb_in[g], 16)

        for b in range(2):
            sp.sem_inc(um_out[b], 16)
        sp.sem_inc(ua_out, 16)
        with sp.Fori(0, HEADS) as i:
            sp.wait_ge(normed, i + 1)
            sp.dma_start(wqk[:], a["w_qk"][bass.ds(i, 1)].rearrange("o p j k e -> (o p) j k e")).then_inc(wqk_in, 16)
            sp.dma_start(gr[:], rows_d[bass.ds(i, 1)].rearrange("o q (c p) -> (o q c) p", p=P)).then_inc(gr_in, 16)
            sp.dma_start(ew[:].rearrange("p c t -> p (c t)"), r1_d[bass.ds(i, 1), :].broadcast_to([P, S])).then_inc(e_in, 16)
            sp.dma_start(dec[:], wi_d[bass.ds(i, 1), :].broadcast_to([P, NCH])).then_inc(dec_in, 16)
            for n in range(MAIN):
                if n == 16:
                    weigh_groups(i)
                b = (n + AHEAD) % 2
                sp.wait_ge(w_split, i * MAIN + (n + AHEAD + 1))
                sp.dma_start(wraw[:, b, :], ahead[bass.ds(i, 1), n].rearrange("o p c -> (o p) c")).then_inc(w_in[b], 16)
                if n in (11, 14, 15):
                    g = (11, 14, 15).index(n)
                    sp.wait_ge(exp_done, i * 24 + 8 * g + 8)
                    for src, dst in stat_dest(g):
                        sp.dma_start(dst, src).then_inc(stat_out[g], 16)
            for q in range(2):
                sp.wait_ge(um_done, i * 2 + q + 1)
                sp.dma_start(um_d[bass.ds(i, 1), q].rearrange("o p s -> (o p) s"), xc[:, q, :]).then_inc(um_out[q], 16)
            sp.wait_ge(ua_done, i + 2)
            sp.dma_start(ua_d[bass.ds(i, 1)].rearrange("o p s -> (o p) s"), szb).then_inc(ua_out, 16)

    def gpsimd(pool):
        pool.sem_inc(w_split, 2)
        with pool.Fori(0, HEADS) as i:
            for n in range(MAIN):
                raw, hi, lo = wraw[:, n % 2, :], whi[:, n % 2, :], wlo[:, n % 2, :]
                pool.wait_ge(proj, i * 2 * MAIN + 2 * n + 2)
                pool.wait_ge(w_in[n % 2], (i * (MAIN // 2) + n // 2 + 1) * 16)
                nc.gpsimd.tensor_tensor(hi, raw, zero[:].broadcast_to([P, D]), ALU.add).then_inc(pool_s, 1)
                pool.wait_ge(pool_s, i * MAIN + n + 1)
                nc.gpsimd.tensor_tensor(lo, raw, hi.bitcast(F32), ALU.subtract).then_inc(w_split, 1)
                if n == 3:
                    pool.wait_ge(wqk_in, (i + 1) * 16)
                    pool.wait_ge(ua_done, i + 1)
                    flat = lambda w: w[:].rearrange("p j k e -> p (j k e)")
                    nc.gpsimd.tensor_tensor(flat(wqk_hi), flat(wqk), zero[:].broadcast_to([P, D]), ALU.add).then_inc(wqk_split, 1)
                    pool.wait_ge(wqk_split, i * 2 + 1)
                    nc.gpsimd.tensor_tensor(flat(wqk_lo), flat(wqk), flat(wqk_hi).bitcast(F32), ALU.subtract).then_inc(wqk_split, 1)

    def blocks(g, tile):
        return 2 if (g == 0 and tile > 0) or (g == 1 and tile % 2 == 1) else 1

    def tensor(pe):
        t_ = nc.tensor
        with pe.Fori(0, HEADS) as i:
            def project(n, h):
                pe.wait_ge(w_split, i * MAIN + n + 3)
                pe.wait_ge(kept[h], i * MAIN + n + 1)
                for k in range(KT):
                    mm = three_pass(t_, ps[:, h, :], whi[:, n % 2, k * P:(k + 1) * P], wlo[:, n % 2, k * P:(k + 1) * P],
                                    h_hi[:, k, h * HALF:(h + 1) * HALF], h_lo[:, k, h * HALF:(h + 1) * HALF],
                                    k == 0, k == KT - 1)
                mm.then_inc(proj, 1)

            def chunk_kept(n):
                for h in range(2):
                    pe.wait_ge(kept[h], i * MAIN + n + 2)

            def project_tokens(n, h):
                pe.wait_ge(w_split, i * MAIN + n + 3)
                if n == VA and h == 0:
                    pe.wait_ge(out_used, i * 4 + 4)
                    pe.wait_ge(masked, i * 24 + 1)
                if n == OA and h == 0:
                    pe.wait_ge(kept[0], i * MAIN + XA + 3)
                    pe.wait_ge(kept[1], i * MAIN + XA + 3)
                if n == OA and h == 1:
                    pe.wait_ge(p_kept, i * 12 + 1)
                    pe.wait_ge(pv_kept, i * 12 + 1)
                    pe.wait_ge(hc_done, i * 3 + 2)
                if n in (VA + 1, OA + 1):
                    pe.wait_ge(kept[h], i * MAIN + n + 1)
                for c in range(4 * h, 4 * h + 4):
                    to = ps[:, TOKEN_BANKS[n // 2 * 2][c // 2], (c % 2) * DH:(c % 2 + 1) * DH]
                    for j in range(KT // 2):
                        k = n % 2 * (KT // 2) + j
                        w = slice(j * DH, (j + 1) * DH)
                        mm = three_pass(t_, to, h_hi[:, k, c * P:(c + 1) * P], h_lo[:, k, c * P:(c + 1) * P],
                                        whi[:, n % 2, w], wlo[:, n % 2, w], j == 0, j == KT // 2 - 1)
                mm.then_inc(proj, 1)

            def head_qk(js):
                pe.wait_ge(wqk_split, i * 2 + 2)
                pe.wait_ge(xc_split, i * 2 + 2)
                pe.wait_ge(kept[0], i * MAIN + VA + 3)
                pe.wait_ge(out_used, i * 4 + 4)
                for j in js:
                    pe.wait_ge(qk_kept, i * 8 + j + 1)
                    w, e, h = j // 4, j // 2 % 2, j % 2
                    for d in range(2):
                        tok = slice(h * HALF, (h + 1) * HALF)
                        mm = three_pass(t_, (M0, M1)[h], wqk_hi[:, w, d, e * P:(e + 1) * P], wqk_lo[:, w, d, e * P:(e + 1) * P],
                                        xc_hi[:, d, tok], xc_lo[:, d, tok], d == 0, d == 1)
                    mm.then_inc(qk_out, 1)

            def scores_and_keys(c):
                pe.wait_ge(qk_kept, i * 8 + 10)
                if c:
                    pe.wait_ge(sw_done, i * 16 + 2 * c)
                cs = slice(c * P, (c + 1) * P)
                for d in range(2):
                    t_.matmul(M0[:, 0:P], km[:, d, cs], qm[:, d, cs], start=(d == 0), stop=(d == 1))
                for d in range(2):
                    mm = t_.transpose(M0[:, P + d * P:P + (d + 1) * P], km[:, d, cs], ident[:])
                mm.then_inc(sk_out, 1)

            def numerator(c):
                if c == 0:
                    pe.wait_ge(summed, i * 4 + 2)
                pe.wait_ge(sw_done, i * 16 + 2 * c + 2)
                if c:
                    pe.wait_ge(state_done, i * 14 + 2 * c)
                t_.matmul(M1[:, 0:DH + 1], sw[:, c % 2, :], v1[:, c, 0:DH + 1], start=True, stop=True)
                for d in range(2):
                    mm = t_.matmul(M2[:, 0:DH + 1], qm[:, d, c * P:(c + 1) * P], cst[:, d, :], start=(d == 0), stop=(d == 1))
                mm.then_inc(num_out, 1)

            def state_update(c):
                pe.wait_ge(num_kept, i * 8 + c + 2)
                for d in range(2):
                    mm = t_.matmul((M1, M2)[d][:, 0:DH + 1], kw[:, c % 2, d * P:(d + 1) * P], v1[:, c, 0:DH + 1],
                                   start=True, stop=True)
                mm.then_inc(upd_out, 1)

            def turn_output():
                pe.wait_ge(normed, i + 2)
                for j in range(4):
                    if j == 3:
                        pe.wait_ge(out_used, i * 4 + 5)
                    for c in range(4):
                        mm = t_.transpose((M0, M1, M2, M0)[j][:, c * P:(c + 1) * P],
                                          og[:, 4 * (j % 2) + c, (j // 2) * P:(j // 2 + 1) * P], ident[:])
                    mm.then_inc(out_turned, 1)

            def turn_values(g):
                chunk_kept(8 + 3 * g)
                pe.wait_ge(p_kept, i * 12 + 4 * g + 1)
                pe.wait_ge(pv_kept, i * 12 + 4 * g + 1)
                for j in range(2):
                    for c in range(4):
                        k = 4 * j + c
                        mm = t_.transpose((A1, A2)[j][:, c * P:(c + 1) * P], tn[g % 2][:, k * P:(k + 1) * P], ident[:])
                    mm.then_inc(v_turned, 1)

            def attend(g, x):
                if x == 0:
                    turn_values(g)
                if x < 4:
                    pe.wait_ge(roped, i * 6 + 2 * g + 2)
                    pe.wait_ge(masked, i * 24 + 8 * g + 2 * x + 1)
                    for u in range(2):
                        t, b = 2 * x + u, blocks(g, 2 * x + u)
                        mm = t_.matmul(A0[:, u * 2 * P:u * 2 * P + b * P], qa[:, g % 2, 0, t * P:(t + 1) * P],
                                       qa[:, g % 2, 1, (t + 1 - b) * P:(t + 1) * P], start=True, stop=True)
                    mm.then_inc(score_out, 1)
                if x >= 2:
                    pe.wait_ge(p_kept, i * 12 + 4 * g + x)
                    pe.wait_ge(v_kept, i * 6 + 2 * g + 2)
                    pe.wait_ge(pv_kept, i * 12 + 4 * g + x - 1)
                    for u in range(2):
                        t, b = 2 * (x - 2) + u, blocks(g, 2 * (x - 2) + u)
                        for j in range(b):
                            mm = t_.matmul(A2[:, u * P:(u + 1) * P], vt[:, t + 1 - b + j, :], pT[:, u, j, :],
                                           start=(j == 0), stop=(j == b - 1))
                    mm.then_inc(pv_out, 1)
                if 1 <= x <= 4:
                    pe.wait_ge(exp_done, i * 24 + 8 * g + 2 * x)
                    pe.wait_ge(p_kept, i * 12 + 4 * g + x)
                    pe.wait_ge(v_kept, i * 6 + 2 * g + 2)
                    for u in range(2):
                        for j in range(blocks(g, 2 * (x - 1) + u)):
                            mm = t_.transpose(A1[:, (2 * u + j) * P:(2 * u + j + 1) * P],
                                              sm[:, (x - 1) % 2, u, j * P:(j + 1) * P], ident[:])
                    mm.then_inc(p_turned, 1)

            for n in range(MAIN):
                c, g = n - 7, (n - 9) // 3
                product = project_tokens if VA <= n < QKV else project
                product(n, 0)
                if n == 4:
                    head_qk(range(0, 4))
                if n == 5:
                    head_qk(range(4, 8))
                if n == 6:
                    scores_and_keys(0)
                if 0 <= c < NCH:
                    numerator(c)
                if n >= 9:
                    attend(g, 2 * (n - 9 - 3 * g))
                product(n, 1)
                if n == 2:
                    pe.wait_ge(gr_in, (i + 1) * 16)
                    pe.wait_ge(pv_kept, i * 12 + 1)
                    t_.matmul(A2[:, 0:4 * NCH], gr[:], ident[0:4 * NCH, 0:4 * NCH], start=True, stop=True).then_inc(hc_turned, 1)
                if 0 <= c < NCH - 1:
                    state_update(c)
                    scores_and_keys(c + 1)
                if n == 15:
                    turn_output()
                if n >= 9:
                    attend(g, 2 * (n - 9 - 3 * g) + 1)

    def scalar(act):
        A = nc.scalar.activation
        act.sem_inc(qk_kept, 2)
        act.sem_inc(pv_kept, 1)

        with act.Fori(0, HEADS) as i:
            def keep(n, h):
                act.wait_ge(proj, i * 2 * MAIN + 2 * n + h + 5)
                src, fn = ps[:, h, :], ACT.Copy
                tok = slice(h * HALF, (h + 1) * HALF)
                if n < 2:
                    if n == 1 and h == 0:
                        act.wait_ge(ua_done, i + 1)
                    dst = tn[n][:, tok]
                elif n < QKV:
                    if n == VA and h == 0:
                        act.wait_ge(T["rows_ready"], 3)
                    if n == OA and h == 0:
                        act.wait_ge(ua_out, (i + 1) * 16)
                    if n == OA + 1:
                        act.wait_ge(summed, i * 4 + h + 1)
                    b = TOKEN_BANKS[n // 2 * 2][2 * h]
                    src = ps[:, b:b + 2, :].rearrange("p b (c e) -> p (b c) e", e=DH)
                    dst = tn[h].rearrange("p (c e) -> p c e", e=DH) if n % 2 else (v1, og)[n // OA][:, 4 * h:4 * h + 4, 0:DH]
                elif n < ZA:
                    g, j = (n - QKV) // 3, (n - QKV) % 3
                    dst = stored(tn[g % 2] if j == 2 else qa[:, g % 2, j, :], g, h * HALF, HALF)
                    src = src.rearrange("p (u r) -> p r u", r=DIL[g])
                elif n < ZB:
                    if n == ZA and h == 0:
                        act.wait_ge(roped, i * 6 + 6)
                    if n == ZA + 1 and h == 0:
                        act.wait_ge(um_done, i * 2 + 1)
                    dst = sg[:, tok]
                else:
                    if h == 0:
                        act.wait_ge(out_used, i * 4 + 8)
                    dst = szb[:, tok]
                A(dst, src, fn).then_inc(kept[h], 1)

            def o_sigmoid(h):
                act.wait_ge(summed, i * 4 + h + 3)
                part = og[:, 4 * h:4 * h + 4, :]
                A(part, part, ACT.Sigmoid).then_inc(o_sig, 1)

            def z_sigmoid(n):
                act.wait_ge(kept[0], i * MAIN + n + 2)
                act.wait_ge(kept[1], i * MAIN + n + 2)
                if n > ZA:
                    act.wait_ge(um_done, i * 2 + n - ZA)
                A(tn[1], szb if n == ZB else sg[:], ACT.Sigmoid).then_inc(z_sig, 1)

            def conv_sigmoid(q):
                act.wait_ge(conv_done, i * 2 + q + 1)
                if q:
                    act.wait_ge(xc_done, i * 2 + 1)
                A(sg[:], cv[:], ACT.Sigmoid).then_inc(conv_sig, 1)

            def xc_high(q):
                act.wait_ge(xc_done, i * 2 + q + 1)
                A(xc_hi[:, q, :], xc[:, q, :], ACT.Copy).then_inc(xc_high_done, 1)

            def head_keep(js):
                for j in js:
                    w, e, h = j // 4, j // 2 % 2, j % 2
                    act.wait_ge(qk_out, i * 8 + j + 1)
                    A((qm, km)[w][:, e, h * HALF:(h + 1) * HALF], (M0, M1)[h], ACT.Copy,
                      scale=KSCALE if w else 1.0).then_inc(qk_kept, 1)

            def intra_weights():
                act.wait_ge(e_arg, i + 1)
                act.wait_ge(hc_turned, i + 1)
                A(hc[:, 0, :], A2[:, 0:NCH], ACT.Copy).then_inc(hc_done, 1)
                A(hc[:, 1:4, :], A2[:, NCH:4 * NCH].rearrange("p (q c) -> p q c", q=3), ACT.Exp).then_inc(hc_done, 1)
                act.wait_ge(dec_in, (i + 1) * 16)
                A(dec[:], dec[:], ACT.Exp).then_inc(hc_done, 1)
                act.wait_ge(hc_done, i * 3 + 3)
                for c in range(NCH):
                    ins = A(ew[:, c, :], ew[:, c, :], ACT.Exp, bias=hc[:, 0, c:c + 1])
                ins.then_inc(e_exp, 1)

            def inter(c):
                act.wait_ge(num_out, i * 8 + c + 1)
                act.wait_ge(num_kept, i * 8 + c + 1)
                if c:
                    act.wait_ge(squares, i * 8 + c)
                A(hin[:], M2[:, 0:DH + 1], ACT.Copy, scale=hc[:, 1, c:c + 1]).then_inc(inter_kept, 1)
                act.wait_ge(gated, i * 8 + c + 1)
                A(hin[:, 0:DH], og[:, c, :], ACT.Square, accum_out=vr[:, 0, c:c + 1]).then_inc(squares, 1)

            def rstd():
                act.wait_ge(var_done, i + 1)
                A(vr[:, 2, :], vr[:, 1, :], ACT.Ln).then_inc(act_s, 1)
                act.wait_ge(act_s, i + 1)
                A(vr[:, 3, :], vr[:, 2, :], ACT.Exp, scale=-0.5).then_inc(ln_done, 1)

            def attend(g, x):
                if x >= 2:
                    s = x - 2
                    act.wait_ge(pv_out, i * 12 + 4 * g + s + 1)
                    A(num[g][:, 2 * P * s:2 * P * (s + 1)], A2[:, 0:2 * P], ACT.Copy).then_inc(pv_kept, 1)
                if x < 4:
                    act.wait_ge(max_done, i * 12 + 4 * g + x + 1)
                    for u in range(2):
                        b = blocks(g, 2 * x + u)
                        A(sm[:, x % 2, u, 0:b * P], sm[:, x % 2, u, 0:b * P], ACT.Exp, bias=nm[:, x % 2, u:u + 1],
                          accum_out=st[:, g, 2 * x + u, 1:2]).then_inc(exp_done, 1)

            for n in range(MAIN):
                c, g = n - 7, (n - 9) // 3
                keep(n, 0)
                if n == 2:
                    conv_sigmoid(0)
                if n == 3:
                    xc_high(1)
                    intra_weights()
                if n == 4:
                    head_keep(range(0, 4))
                if n == 5:
                    head_keep(range(4, 8))
                if 0 <= c < NCH:
                    inter(c)
                if n >= 9:
                    attend(g, 2 * (n - 9 - 3 * g))
                if n == ZB:
                    act.wait_ge(ct_arg, i + 1)
                    A(cw[:, 1], cw[:, 1], ACT.Exp).then_inc(ct_exp, 1)
                if n == QKV:
                    o_sigmoid(0)
                keep(n, 1)
                if n == QKV:
                    o_sigmoid(1)
                if n == 2:
                    conv_sigmoid(1)
                    xc_high(0)
                if n == 14:
                    rstd()
                if n >= ZA:
                    z_sigmoid(n)
                if n >= 9:
                    attend(g, 2 * (n - 9 - 3 * g) + 1)

    def vector(dve):
        v = nc.vector
        ones = v.memset(v1[:, :, DH:DH + 2], 1.0)
        ones.then_inc(ready, 1)
        v.memset(turn[:, :, 0:3], 0.0).then_inc(ready, 1)
        for s, k in ((num_kept, 1), (normed, 1), (p_kept, 1)):
            dve.sem_inc(s, k)
        dve.wait_ge(hp_in, 16)
        dve.wait_ge(ready, 2)

        with dve.Fori(0, HEADS) as i:
            step = Steps(dve, dve_s, i, DVE_STEPS)

            def chunk_kept(n):
                for h in range(2):
                    dve.wait_ge(kept[h], i * MAIN + n + 2)

            def conv(q):
                chunk_kept(q)
                if q:
                    dve.wait_ge(xc_done, i * 2 + 1)
                else:
                    dve.wait_ge(ua_done, i + 1)
                x = turn[:, q, :]
                step(v.tensor_scalar(cv[:], x[:, 3:3 + S], hp[:, q, 3:4], hp[:, q, 4:5], ALU.mult, ALU.add))
                for j in range(3):
                    ins = v.scalar_tensor_tensor(cv[:], x[:, j:j + S], hp[:, q, j:j + 1], cv[:], ALU.mult, ALU.add)
                    if j < 2:
                        step(ins)
                ins.then_inc(conv_done, 1)

            def conv_gate(q):
                dve.wait_ge(conv_sig, i * 2 + q + 1)
                dve.wait_ge(um_out[q], (i + 1) * 16)
                v.tensor_tensor(xc[:, q, :], cv[:], sg[:], ALU.mult).then_inc(xc_done, 1)

            def xc_low(q):
                dve.wait_ge(xc_high_done, i * 2 + q + 1)
                v.tensor_tensor(xc_lo[:, q, :], xc[:, q, :], xc_hi[:, q, :].bitcast(F32), ALU.subtract).then_inc(xc_split, 1)

            def intra_args():
                dve.wait_ge(e_in, (i + 1) * 16)
                v.tensor_tensor(ew[:], ew[:], band[:, 0:P].unsqueeze(1).broadcast_to([P, NCH, P]), ALU.add).then_inc(e_arg, 1)

            def add_half(n, h):
                dve.wait_ge(kept[h], i * MAIN + n + 2)
                part = (v1, og)[n // OA][:, 4 * h:4 * h + 4, 0:DH]
                v.tensor_tensor(part, part, tn[h].rearrange("p (c e) -> p c e", e=DH), ALU.add).then_inc(summed, 1)

            def rope(n):
                g, j = (n - QKV) // 3, (n - QKV) % 3
                chunk_kept(n)
                if g + j:
                    dve.wait_ge(roped, i * 6 + 2 * g + j)
                else:
                    dve.wait_ge(xc_done, i * 2 + 2)
                v.tensor_copy(small[:, 3:4], zero[:])
                x, rot = qa[0:ROPE, g % 2, j, :], sg[0:ROPE, :]
                step(v.stream_shuffle(rot, x, [(m + ROPE // 2) % ROPE for m in range(ROPE)]))
                step(v.tensor_tensor(stored(rot, g), stored(rot, g), order(sinT, g), ALU.mult))
                step(v.tensor_tensor(stored(x, g), stored(x, g), order(cosT, g), ALU.mult))
                v.tensor_tensor(x, x, rot, ALU.add).then_inc(roped, 1)

            def weigh(c):
                dve.wait_ge(sk_out, i * 8 + c + 1)
                if c == 0:
                    dve.wait_ge(e_exp, i + 1)
                v.tensor_tensor(sw[:, c % 2, :], M0[:, 0:P], ew[:, c, :], ALU.mult).then_inc(sw_done, 1)
                v.tensor_scalar(kw[:, c % 2, :], M0[:, P:P + DH], hc[:, 3, c:c + 1], None, ALU.mult).then_inc(sw_done, 1)

            def head_out(c):
                if c == 0:
                    dve.wait_ge(o_sig, i * 2 + 2)
                dve.wait_ge(inter_kept, i * 8 + c + 1)
                if c:
                    dve.wait_ge(gated, i * 8 + c)
                v.tensor_tensor(hnb[:], M1[:, 0:DH + 1], hin[:], ALU.add).then_inc(num_kept, 1)
                dve.wait_ge(num_kept, i * 8 + c + 2)
                den = hnb[:, DH:DH + 1]
                step(v.tensor_scalar(small[:, 0:1], den, -1.0, None, ALU.mult))
                step(v.scalar_tensor_tensor(small[:, 1:2], den, hc[:, 2, c:c + 1], small[:, 0:1], ALU.max, ALU.max))
                step(v.reciprocal(small[:, 2:3], small[:, 1:2]))
                v.scalar_tensor_tensor(og[:, c, :], hnb[:, 0:DH], small[:, 2:3], og[:, c, :], ALU.mult, ALU.mult)\
                    .then_inc(gated, 1)

            def state(c):
                dve.wait_ge(upd_out, i * 7 + c + 1)
                for d in range(2):
                    v.scalar_tensor_tensor(cst[:, d, :], cst[:, d, :], dec[:, c:c + 1], (M1, M2)[d][:, 0:DH + 1],
                                           ALU.mult, ALU.add).then_inc(state_done, 1)

            def head_norm():
                dve.wait_ge(squares, i * 8 + 8)
                v.tensor_scalar(vr[:, 1, :], vr[:, 0, :], 1.0 / DH, EPS, ALU.mult, ALU.add).then_inc(var_done, 1)
                for q in range(2):
                    v.tensor_scalar(xc[:, q, :], xc[:, q, :], hp[:, q, 5:6], None, ALU.mult)
                dve.wait_ge(ln_done, i + 1)
                step(v.tensor_tensor(vr[:, 4, :], vr[:, 3, :], vr[:, 3, :], ALU.mult))
                step(v.tensor_tensor(vr[:, 4, :], vr[:, 4, :], vr[:, 1, :], ALU.mult))
                step(v.tensor_scalar(vr[:, 4, :], vr[:, 4, :], -0.5, 1.5, ALU.mult, ALU.add))
                step(v.tensor_tensor(vr[:, 5, :], vr[:, 4, :], vr[:, 3, :], ALU.mult))
                v.tensor_tensor(og[:], og[:], vr[:, 5, :].unsqueeze(2).broadcast_to([P, NCH, DH]), ALU.mult).then_inc(normed, 1)

            def head_scaled():
                for j in range(4):
                    q, h = j // 2, j % 2
                    dve.wait_ge(out_turned, i * 4 + j + 1)
                    part = xc[:, q, h * HALF:(h + 1) * HALF]
                    v.scalar_tensor_tensor(part, (M0, M1, M2, M0)[j], hp[:, q, 6:7], part, ALU.mult, ALU.add).then_inc(out_used, 1)

            def silu_za(q):
                dve.wait_ge(z_sig, i * 3 + q + 1)
                step(v.tensor_tensor(sg[:], sg[:], tn[1], ALU.mult))
                if q == 0:
                    dve.wait_ge(out_used, i * 4 + 8)
                v.tensor_tensor(xc[:, q, :], xc[:, q, :], sg[:], ALU.mult).then_inc(um_done, 1)

            def attend(g, x):
                if x == 0:
                    for j in range(2):
                        dve.wait_ge(v_turned, i * 6 + 2 * g + j + 1)
                        v.tensor_copy(vt[:, 4 * j:4 * j + 4, :], (A1, A2)[j].rearrange("p (c e) -> p c e", c=4)).then_inc(v_kept, 1)
                if x < 4:
                    dve.wait_ge(score_out, i * 12 + 4 * g + x + 1)
                    v.tensor_copy(small[:, 3:4], zero[:])
                    for u in range(2):
                        t, b = 2 * x + u, blocks(g, 2 * x + u)
                        mask = diag[:] if g == 2 else band[:, (2 - b) * P:2 * P]
                        v.tensor_tensor_reduce(sm[:, x % 2, u, 0:b * P], A0[:, u * 2 * P:u * 2 * P + b * P], mask, SCALE, -3e38,
                                               ALU.add, ALU.max, st[:, g, t, 0:1]).then_inc(masked, 1)
                    dve.wait_ge(masked, i * 24 + 8 * g + 2 * x + 3)
                    v.tensor_scalar(nm[:, x % 2, :], st[:, g, 2 * x:2 * x + 2, 0], -1.0, None, ALU.mult).then_inc(max_done, 1)
                if 1 <= x <= 4:
                    dve.wait_ge(p_turned, i * 12 + 4 * g + x)
                    bs = [blocks(g, 2 * (x - 1) + u) for u in range(2)]
                    bank = A1.rearrange("p (u b q) -> p u b q", u=2, b=2)
                    if bs[0] == bs[1]:
                        ins = v.tensor_copy(pT[:, :, 0:bs[0], :], bank[:, :, 0:bs[0], :])
                    else:
                        for u in range(2):
                            ins = v.tensor_copy(pT[:, u, 0:bs[u], :], bank[:, u, 0:bs[u], :])
                    ins.then_inc(p_kept, 1)

            def weigh_groups():
                dve.wait_ge(ct_in, (i + 1) * 16)
                mx, dn = ct[:, :, :, 0], ct[:, :, :, 1]
                top, ex, wt, pr = cw[:, 3, 0, :], cw[:, 1], cw[:, 2], cw[:, 0]
                step(v.tensor_tensor(top, mx[:, 0, :], mx[:, 1, :], ALU.max))
                step(v.tensor_tensor(top, top, mx[:, 2, :], ALU.max))
                v.tensor_tensor(ex, mx, top.unsqueeze(1).broadcast_to([P, GROUPS, NCH]), ALU.subtract).then_inc(ct_arg, 1)
                dve.wait_ge(ct_exp, i + 1)
                step(v.tensor_tensor(pr, ex, dn, ALU.mult))
                step(v.tensor_tensor(cw[:, 3, 1, :], pr[:, 0, :], pr[:, 1, :], ALU.add))
                step(v.tensor_tensor(cw[:, 3, 1, :], cw[:, 3, 1, :], pr[:, 2, :], ALU.add))
                step(v.reciprocal(cw[:, 3, 2, :], cw[:, 3, 1, :]))
                v.tensor_tensor(wt, ex, cw[:, 3, 2, :].unsqueeze(1).broadcast_to([P, GROUPS, NCH]), ALU.mult).then_inc(cw_done, 1)

            def scale_group(g):
                if g == 2:
                    dve.wait_ge(pv_kept, i * 12 + 13)
                dve.wait_ge(cb_in[g], (i + 1) * 16)
                step(v.tensor_tensor(stored(num[g], g), stored(num[g], g), order(cb[g], g), ALU.mult))

            def merge_groups():
                for g in (0, 1):
                    scale_group(g)
                step(v.tensor_tensor(order(num[0], 1), order(num[0], 1), stored(num[1], 1), ALU.add))
                scale_group(2)
                step(v.tensor_tensor(order(num[0], 2), order(num[0], 2), stored(num[2], 2), ALU.add))
                dve.wait_ge(z_sig, i * 3 + 3)
                step(v.tensor_tensor(szb, szb, tn[1], ALU.mult))
                v.tensor_tensor(szb, szb, num[0], ALU.mult).then_inc(ua_done, 1)

            step(v.tensor_copy(hp[:], hpa[:, bass.ds(i, 1)].rearrange("p o q w -> p (o q) w")))
            step(v.memset(cst[:], 0.0))
            for n in range(MAIN):
                c, g = n - 7, (n - 9) // 3
                if n - 1 in (VA + 1, OA + 1):
                    for h in range(2):
                        add_half(n - 1, h)
                if 1 <= n <= 2:
                    conv(n - 1)
                    if n == 1:
                        conv_gate(0)
                if n == 2:
                    conv_gate(1)
                    xc_low(0)
                    intra_args()
                    xc_low(1)
                if QKV <= n - 1 < ZA and (n - 1 - QKV) % 3 < 2:
                    rope(n - 1)
                if n == 6:
                    weigh(0)
                if 0 <= c < NCH:
                    head_out(c)
                if n >= 9:
                    attend(g, 2 * (n - 9 - 3 * g))
                if n == ZB:
                    weigh_groups()
                if 0 <= c < NCH - 1:
                    state(c)
                    weigh(c + 1)
                if n == 14:
                    head_norm()
                if n == 15:
                    head_scaled()
                if n == 15 or n == 16:
                    silu_za(n - 15)
                if n >= 9:
                    attend(g, 2 * (n - 9 - 3 * g) + 1)
            merge_groups()
            step.end()

    return {"sync": sync, "gpsimd": gpsimd, "tensor": tensor, "scalar": scalar, "vector": vector}


def gates_at(m):
    return 2 * m if m < 2 else 4 * m - 2


def branches_at(m):
    return 4 + 4 * m if m < KT - 1 else 4 * KT - 2


def merge(nc, a, sem, ps, T):
    h_hi, h_lo, um_d, ua_d, mg_d, zero = (T[n] for n in ("h_hi", "h_lo", "um_d", "ua_d", "mg_d", "zero"))
    w_in, um_out, kept, tile_in, w_split, pool_s, proj = (T[n] for n in ("w_in", "um_out", "kept", "tile_in", "w_split", "pool_s", "proj"))
    out_used, masked, p_kept, pv_kept, ua_out = (T[n] for n in ("out_used", "masked", "p_kept", "pv_kept", "ua_out"))
    w_hi_done, w_lo_done, mg_out, merged_half = (T[n] for n in ("w_hi_done", "w_lo_done", "mg_out", "merged_half"))
    b_hi_done, b_lo_done = T["b_hi_done"], T["b_lo_done"]
    raw, whi, wlo, qa, mg = (T["kept_on"][n] for n in ("wraw", "whi", "wlo", "qa", "num1"))
    b_raw, b_hi, b_lo, raw_lo = (T[n] for n in ("b_raw", "b_hi", "b_lo", "raw_lo"))
    KA = HEADS
    KB = KT + KA
    Q0 = HEADS * MAIN
    SPLIT0, PROJ0 = 2 + Q0, 4 + 2 * Q0
    GATES_DONE = PROJ0 + 2 * (gates_at(KT - 1) + 2)
    dve_s, sig_done = sem("dve_merge"), T["sig_done"]
    width = lambda l: KA * P if l >= 4 and l % 2 == 1 and (l >= 28 or l % 4 == 1) else D

    def sync(sp):
        ahead = a["w_all"][Q0 + 5:Q0 + 29].rearrange("(t j) p c -> t j p c", j=8)

        def load(l):
            sp.wait_ge(w_split, Q0 + l + 1)
            sp.dma_start(raw[:, l % 2, 0:width(l)], a["w_all"][Q0 + l, :, 0:width(l)]).then_inc(w_in[l % 2], 16)

        sp.wait_ge(um_out[0], 16 * HEADS + 16)
        sp.wait_ge(um_out[1], 16 * HEADS + 16)
        sp.wait_ge(ua_out, 16 * HEADS + 16)
        for k in range(KT):
            sp.dma_start(b_raw[:, k, :], um_d[k // 2, k % 2]).then_inc(tile_in[k], 16)
        load(4)
        for k in range(KT, KB):
            sp.dma_start(b_raw[:, k, :], ua_d[k - KT]).then_inc(tile_in[k], 16)
        with sp.Fori(0, KT // 2 - 1) as t:
            for l in range(5, 13):
                sp.wait_ge(w_split, t * 8 + (Q0 + l + 1))
                sp.dma_start(raw[:, l % 2, 0:width(l)], ahead[bass.ds(t, 1), l - 5, :, 0:width(l)].rearrange("o p c -> (o p) c"))\
                  .then_inc(w_in[l % 2], 16)
        load(29)
        load(30)
        sp.wait_ge(proj, GATES_DONE)
        for k in range(KT):
            sp.dma_start(raw_lo[:, k, :], a["w_out"][k * P:(k + 1) * P, :]).then_inc(tile_in[k], 16)
        load(31)

    def gpsimd(pool):
        def split(l, at):
            n = width(l)
            pool.wait_ge(proj, 2 * at + (PROJ0 - 2))
            pool.wait_ge(w_in[l % 2], 8 * at + (8 * (Q0 - l % 2) + 16))
            nc.gpsimd.tensor_tensor(whi[:, l % 2, 0:n], raw[:, l % 2, 0:n], zero[:].broadcast_to([P, n]), ALU.add).then_inc(pool_s, 1)
            pool.wait_ge(pool_s, at + (Q0 + 1))
            nc.gpsimd.tensor_tensor(wlo[:, l % 2, 0:n], raw[:, l % 2, 0:n], whi[:, l % 2, 0:n].bitcast(F32), ALU.subtract)\
              .then_inc(w_split, 1)

        for l in range(4):
            split(l, l)
        with pool.Fori(0, KT // 2 - 1) as t:
            for j in range(8):
                split(4 + j, t * 8 + (4 + j))
        for l in range(28, 32):
            split(l, l)

    def tensor(pe):
        def product(l, at, j, bank_free, k0, kn, x_hi, x_lo, x_done=None):
            pe.wait_ge(w_split, at + (SPLIT0 + 1))
            for h in range(2):
                bank_free(h)
                for k in range(kn):
                    if x_done is not None and h == 0:
                        pe.wait_ge(x_done, k0 + k + 1)
                    mm = three_pass(nc.tensor, ps[:, 2 * j + h, :], whi[:, l % 2, k * P:(k + 1) * P], wlo[:, l % 2, k * P:(k + 1) * P],
                                    x_hi[:, k0 + k, h * HALF:(h + 1) * HALF], x_lo[:, k0 + k, h * HALF:(h + 1) * HALF],
                                    k == 0, k == kn - 1)
                mm.then_inc(proj, 1)

        def gates(l, at, m):
            for j in range(2):
                def sigmoid_read(h):
                    if isinstance(m, int) and m == 0:
                        if j == 0:
                            pe.wait_ge(kept[h], HEADS * MAIN + 1)
                        else:
                            pe.wait_ge(out_used, 4 * HEADS + 4)
                    else:
                        pe.wait_ge(sig_done, 4 * m + (2 * j + h - 3))
                product(l + j, at + j, j, sigmoid_read, 0, KT, h_hi, h_lo)

        def branches(l, at, m):
            def merged(h):
                pe.wait_ge(merged_half, 4 * m + (2 * h + 1))
            product(l, at, 2, merged, 0, KT, b_hi, b_lo, b_lo_done)
            product(l + 1, at + 1, 3, merged, KT, KA, b_hi, b_lo, b_lo_done)

        for m in range(2):
            gates(2 * m, 2 * m, m)
        pe.wait_ge(out_used, 4 * HEADS + 4)
        pe.wait_ge(masked, 24 * HEADS + 1)
        pe.wait_ge(p_kept, 12 * HEADS + 1)
        pe.wait_ge(pv_kept, 12 * HEADS + 1)
        with pe.Fori(0, KT // 2 - 1) as t:
            for b in range(2):
                branches(4 + 4 * b, t * 8 + (4 + 4 * b), t * 2 + b)
                gates(6 + 4 * b, t * 8 + (6 + 4 * b), t * 2 + (b + 2))
        for m in (KT - 2, KT - 1):
            branches(branches_at(m), branches_at(m), m)



    def scalar(act):
        A = nc.scalar.activation

        def sigmoids(m, b, j, at):
            for h in range(2):
                act.wait_ge(proj, 2 * at + (PROJ0 + h + 1))
                A(qa[:, b, j, h * HALF:(h + 1) * HALF], ps[:, 2 * j + h, :], ACT.Sigmoid).then_inc(sig_done, 1)

        def split_high(ks):
            for k in ks:
                act.wait_ge(tile_in[k], 32 if k < KT else 16)
                A(b_hi[:, k, :], b_raw[:, k, :], ACT.Copy).then_inc(b_hi_done, 1)

        act.sem_inc(mg_out, 16)
        for j, ks in enumerate((range(0, 3), range(3, 6), range(6, 9), range(9, 12))):
            sigmoids(j // 2, j // 2, j % 2, j)
            split_high(ks)
        with act.Fori(0, KT // 2 - 1) as t:
            for b in range(2):
                act.wait_ge(merged_half, t * 8 + (4 * b + 8))
                act.dma_start(mg_d[bass.ds(t * 2 + b, 1)].rearrange("o p s -> (o p) s"), mg[:]).then_inc(mg_out, 16)
                for j in range(2):
                    sigmoids(t * 2 + (b + 2), b, j, t * 8 + (4 * b + 6 + j))
        for k in range(KT):
            if k == 2:
                act.wait_ge(merged_half, 4 * (KT - 1) + 4)
                act.dma_start(mg_d[KT - 2], mg[:]).then_inc(mg_out, 16)
            act.wait_ge(tile_in[k], 48)
            A(h_hi[:, k, :], raw_lo[:, k, :], ACT.Copy).then_inc(w_hi_done, 1)
        act.wait_ge(merged_half, 4 * KT + 4)
        act.dma_start(mg_d[KT - 1], mg[:]).then_inc(mg_out, 16)

    def vector(dve):
        v = nc.vector

        def merge_tile(m, b, at):
            for h in range(2):
                tok = slice(h * HALF, (h + 1) * HALF)
                sa, sc = qa[:, b, 0, tok], qa[:, b, 1, tok]
                dve.wait_ge(sig_done, 4 * m + 4)
                dve.wait_ge(proj, 2 * at + (PROJ0 + h + 1))
                if h == 0:
                    dve.wait_ge(mg_out, 16 * m + 16)
                v.tensor_tensor(mg[:, tok], sa, ps[:, 4 + h, :], ALU.mult).then_inc(dve_s, 1)
                v.tensor_tensor(sc, sc, ps[:, 6 + h, :], ALU.mult).then_inc(merged_half, 1)
                dve.wait_ge(dve_s, 2 * m + (h + 1))
                dve.wait_ge(merged_half, 4 * m + (2 * h + 5))
                v.tensor_tensor(mg[:, tok], mg[:, tok], sc, ALU.add).then_inc(merged_half, 1)

        def w_out_low(ks):
            for k in ks:
                dve.wait_ge(w_hi_done, k + 1)
                v.tensor_tensor(h_lo[:, k, :], raw_lo[:, k, :], h_hi[:, k, :].bitcast(F32), ALU.subtract).then_inc(w_lo_done, 1)

        dve.sem_inc(merged_half, 4)
        dve.sem_inc(T["added"], 4)
        for k in range(KB):
            dve.wait_ge(b_hi_done, k + 1)
            v.tensor_tensor(b_lo[:, k, :], b_raw[:, k, :], b_hi[:, k, :].bitcast(F32), ALU.subtract).then_inc(b_lo_done, 1)
        with dve.Fori(0, KT // 2 - 1) as t:
            for b in range(2):
                merge_tile(t * 2 + b, b, t * 8 + (4 * b + 5))
        w_out_low(range(0, 2))
        merge_tile(KT - 2, 0, branches_at(KT - 2) + 1)
        w_out_low(range(2, KT))
        merge_tile(KT - 1, 1, branches_at(KT - 1) + 1)

    return {"sync": sync, "gpsimd": gpsimd, "tensor": tensor, "scalar": scalar, "vector": vector}


def finish(nc, a, out, sem, ps, T):
    mg_d, acc_d, w_hi, w_lo, zero = (T[n] for n in ("mg_d", "acc_d", "h_hi", "h_lo", "zero"))
    w_lo_done, mg_out, merged_half, proj, sig_done = (T[n] for n in ("w_lo_done", "mg_out", "merged_half", "proj", "sig_done"))
    m_hi, m_lo, gate, gf, bg, ones, xt, y, junk, sc = T["finishing"].values()
    mg = T["kept_on"]["num1"]
    mr = T["kept_on"]["qa"][:, 0].rearrange("p b (k c) -> p b k c", k=KT)
    gate_in, ones_set, gate_out = sem("gate_in"), sem("ones_set"), sem("gate_out")
    gate_kept = sem("gate_kept")
    row_in, m_in, x_in = sem("row_in"), [sem("m_in0"), sem("m_in1")], [sem("xr_in0"), sem("xr_in1")]
    m_part = sem("m_part")
    m_hi_done, m_split, prod, added = sem("m_hi_done"), sem("m_split"), sem("prod"), T["added"]
    sq_done, ln_done, var_done, y_done, act_s, dve_s = (sem(n) for n in ("sq_done", "lnf_done", "varf_done", "y_done", "act_fin", "dve_fin"))
    y_out = [sem("y_out0"), sem("y_out1")]
    PER = 12
    BRANCH_DONE = 4 + 2 * (HEADS * MAIN + branches_at(KT - 1) + 1)

    def sync(sp):
        for b in range(2):
            sp.sem_inc(y_out[b], 16)
        sp.wait_ge(proj, BRANCH_DONE)
        sp.dma_start(gate[:], acc_d).then_inc(gate_in, 16)
        sp.dma_start(bg[:], a["b_gate"].broadcast_to([P, D])).then_inc(row_in, 16)
        sp.dma_start(gf[:], a["g_final"].broadcast_to([P, D])).then_inc(row_in, 16)
        with sp.Fori(0, NCH // 2) as t:
            for b in range(2):
                sp.wait_ge(y_done, t * 4 + 2 * b + 2)
                sp.dma_start(out[bass.ds((t * 2 + b) * P, P), :], y[:, b, :]).then_inc(y_out[b], 16)
        for b in range(2):
            sp.wait_ge(y_out[b], 16 * (NCH // 2) + 16)

    def gpsimd(pool):
        rows = mg_d.rearrange("k p s -> p k s")

        def split(b, ks, m_raw, done):
            nc.gpsimd.tensor_tensor(m_hi[:, b, ks], m_raw, zero[:].unsqueeze(2).broadcast_to([P, ks.stop - ks.start, P]), ALU.add)\
              .then_inc(m_hi_done, 1)
            pool.wait_ge(m_hi_done, done)
            return nc.gpsimd.tensor_tensor(m_lo[:, b, ks], m_raw, m_hi[:, b, ks].bitcast(F32), ALU.subtract)

        pool.wait_ge(mg_out, 16 * KT)
        for b in range(2):
            pool.dma_start(mr[:, b, 0:KT - 1], rows[:, 0:KT - 1, b * P:(b + 1) * P]).then_inc(m_in[b], 16)
        pool.wait_ge(proj, BRANCH_DONE)
        nc.gpsimd.memset(ones[:], 1.0).then_inc(ones_set, 1)
        pool.wait_ge(m_in[0], 16)
        split(0, slice(0, KT - 1), mr[:, 0, 0:KT - 1], 1).then_inc(m_part, 1)
        pool.wait_ge(merged_half, 4 * KT + 2)
        split(0, slice(KT - 1, KT), mg[:, 0:P].unsqueeze(1), 2).then_inc(m_split, 1)
        pool.wait_ge(m_in[1], 16)
        split(1, slice(0, KT - 1), mr[:, 1, 0:KT - 1], 3).then_inc(m_part, 1)
        split(1, slice(KT - 1, KT), mg[:, P:2 * P].unsqueeze(1), 4).then_inc(m_split, 1)
        pool.wait_ge(mg_out, 16 * KT + 16)
        pool.wait_ge(m_part, 2)
        with pool.Fori(1, NCH // 2) as t:
            for b in range(2):
                pool.wait_ge(m_split, t * 2 + (b - 1))
                pool.dma_start(mr[:, b], rows[:, :, bass.ds((t * 2 + b) * P, P)]).then_inc(m_in[b], 16)
                pool.wait_ge(prod, t * 4 + (2 * b - 2))
                pool.wait_ge(m_in[b], t * 16 + 16)
                split(b, slice(0, KT), mr[:, b], t * 2 + (b + 3)).then_inc(m_split, 1)

    def tensor(pe):
        pe.wait_ge(sig_done, 4 * KT)
        pe.wait_ge(gate_in, 16)
        pe.wait_ge(ones_set, 1)
        for h in range(2):
            mm = nc.tensor.matmul(ps[:, 2 + h, :], ones[:], gate[:, h * HALF:(h + 1) * HALF], start=True, stop=True)
        mm.then_inc(gate_out, 1)
        with pe.Fori(0, NCH // 2) as t:
            for b in range(2):
                pe.wait_ge(m_split, t * 2 + b + 1)
                if b == 1:
                    pe.wait_ge(gate_kept, 1)
                pe.wait_ge(added, t * 4 + 2 * b + 2)
                for h in range(2):
                    for k in range(KT):
                        if b == 0 and h == 0:
                            pe.wait_ge(w_lo_done, k + 1)
                        cols = slice(h * HALF, (h + 1) * HALF)
                        mm = three_pass(nc.tensor, ps[:, 2 * b + h, :], m_hi[:, b, k, :], m_lo[:, b, k, :], w_hi[:, k, cols],
                                        w_lo[:, k, cols], k == 0, k == KT - 1)
                    mm.then_inc(prod, 1)

    def scalar(act):
        A = nc.scalar.activation
        act.wait_ge(proj, BRANCH_DONE + 2)
        with act.Fori(0, NCH // 2) as t:
            for b in range(2):
                act.wait_ge(added, t * 4 + 2 * b + 2)
                act.dma_start(xt[:, b, :], a["x"][bass.ds((t * 2 + b) * P, P), :]).then_inc(x_in[b], 16)
                for h in range(2):
                    act.wait_ge(added, t * 4 + 2 * b + h + 5)
                    A(junk[:, h * HALF:(h + 1) * HALF], y[:, b, h * HALF:(h + 1) * HALF], ACT.Square,
                      accum_out=sc[:, b, 6 * h:6 * h + 1]).then_inc(sq_done, 1)
                act.wait_ge(var_done, t * 2 + b + 1)
                A(sc[:, b, 2:3], sc[:, b, 1:2], ACT.Ln).then_inc(act_s, 1)
                act.wait_ge(act_s, t * 2 + b + 1)
                A(sc[:, b, 3:4], sc[:, b, 2:3], ACT.Exp, scale=-0.5).then_inc(ln_done, 1)

    def vector(dve):
        v = nc.vector
        dve.wait_ge(row_in, 32)
        dve.wait_ge(gate_out, 1)
        v.tensor_tensor(gate[:], bg[:], ps[:, 2:4, :].rearrange("p h c -> p (h c)"), ALU.add).then_inc(gate_kept, 1)
        dve.wait_ge(gate_kept, 1)
        with dve.Fori(0, NCH // 2) as t:
            step = Steps(dve, dve_s, t, PER)
            for b in range(2):
                for h in range(2):
                    cols = slice(h * HALF, (h + 1) * HALF)
                    dve.wait_ge(prod, t * 4 + 2 * b + h + 1)
                    if h == 0:
                        dve.wait_ge(y_out[b], (t + 1) * 16)
                    step(v.tensor_tensor(y[:, b, cols], gate[:, cols], ps[:, 2 * b + h, :], ALU.mult))
                    if h == 0:
                        dve.wait_ge(x_in[b], (t + 1) * 16)
                    v.tensor_tensor(y[:, b, cols], y[:, b, cols], xt[:, b, cols], ALU.add).then_inc(added, 1)
                dve.wait_ge(sq_done, t * 4 + 2 * b + 2)
                step(v.tensor_tensor(sc[:, b, 4:5], sc[:, b, 0:1], sc[:, b, 6:7], ALU.add))
                v.tensor_scalar(sc[:, b, 1:2], sc[:, b, 4:5], 1.0 / D, EPS, ALU.mult, ALU.add).then_inc(var_done, 1)
                dve.wait_ge(ln_done, t * 2 + b + 1)
                r, w = sc[:, b, 3:4], sc[:, b, 4:5]
                step(v.scalar_tensor_tensor(w, r, sc[:, b, 1:2], r, ALU.mult, ALU.mult))
                step(v.tensor_scalar(w, w, -0.5, 1.5, ALU.mult, ALU.add))
                step(v.tensor_tensor(sc[:, b, 5:6], r, w, ALU.mult))
                for h in range(2):
                    cols = slice(h * HALF, (h + 1) * HALF)
                    v.scalar_tensor_tensor(y[:, b, cols], y[:, b, cols], sc[:, b, 5:6], gf[:, cols], ALU.mult, ALU.mult)\
                        .then_inc(y_done, 1)
            step.end()

    return {"sync": sync, "gpsimd": gpsimd, "tensor": tensor, "scalar": scalar, "vector": vector}


def kernel(**inputs):
    import concourse.bacc as bacc
    from concourse.bass_utils import run_bass_kernel_spmd

    x = {k: np.asarray(v) for k, v in inputs.items()}
    w_in = x["w_in"][0]

    def tiles(w):
        return np.ascontiguousarray(w.reshape(-1, P, w.shape[1]).transpose(1, 0, 2)).reshape(P, -1)

    mw = HEADS * DH
    gate0 = 4 * mw
    att0 = gate0 + 2 * HEADS
    qkv = GROUPS * HEADS * P
    zb0 = att0 + 3 * qkv
    main = np.empty((HEADS, MAIN, P, D), np.float32)
    for i in range(HEADS):
        starts = [DH * i, DH * i + P]
        for g in range(GROUPS):
            starts += [att0 + j * qkv + (g * HEADS + i) * P for j in range(3)]
        starts += [3 * mw + DH * i, 3 * mw + DH * i + P, zb0 + i * P]
        for n, c in zip((*range(VA), *range(QKV, MAIN)), starts):
            main[i, n] = tiles(w_in[:, c:c + P])
        for n, c in ((VA, mw + DH * i), (OA, 2 * mw + DH * i)):
            for h in range(2):
                main[i, n + h] = tiles(w_in[h * D // 2:(h + 1) * D // 2, c:c + DH])
    gates = np.zeros((D, P), np.float32)
    gates[:, 0:HEADS] = w_in[:, gate0:gate0 + HEADS]
    gates[:, 32:32 + HEADS] = w_in[:, gate0 + HEADS:gate0 + 2 * HEADS]
    gate_bias = np.zeros((P, 2), np.float32)
    gate_bias[0:HEADS, 0] = x["b_igate"][0]
    gate_bias[32:32 + HEADS, 1] = x["b_fgate"][0]
    ga0 = zb0 + HEADS * P
    merging = np.zeros((4 * KT, P, D), np.float32)
    for m in range(KT):
        c = slice(m * P, (m + 1) * P)
        merging[gates_at(m)] = tiles(w_in[:, ga0:ga0 + D][:, c])
        merging[gates_at(m) + 1] = tiles(w_in[:, ga0 + D:ga0 + 2 * D][:, c])
        merging[branches_at(m)] = tiles(x["w_out_mlstm"][0][:, c])
        merging[branches_at(m) + 1, :, 0:HEADS * P] = tiles(x["w_out_attn"][0][:, c])
    hp = np.zeros((P, HEADS, 2, 8), np.float32)
    per = lambda w: w.reshape(HEADS, 2, P).transpose(2, 0, 1)
    for j in range(4):
        hp[..., j] = per(x["w_conv"][0, j])
    hp[..., 4], hp[..., 5], hp[..., 6] = per(x["b_conv"][0]), per(x["skip_mlstm"][0]), per(x["g_mlstm_head"][0])
    wqk = np.stack([x["w_q_mlstm"][0], x["w_k_mlstm"][0]], 1)
    wqk = np.ascontiguousarray(wqk.reshape(HEADS, 2, 2, P, DH).transpose(0, 3, 1, 2, 4))
    half = ROPE // 2
    freq = THETA ** (-np.arange(half, dtype=np.float32) / half)
    rope = np.stack([np.tile(freq, 2), np.repeat([-1.0, 1.0], half)], 1).astype(np.float32)
    arrays = {
        "x": x["x"][0], "c_cols": np.ascontiguousarray(x["c"].reshape(KT, P).T), "positions": x["positions"].astype(np.int32),
        "c_row": x["c"],
        "w_ada_cols": np.stack([x["w_ada"][0, :, j * D + k * P:j * D + (k + 1) * P].T for k in range(KT) for j in (1, 0)]),
        "w_ada_gate": x["w_ada"][0, :, 2 * D:], "b_cols": np.ascontiguousarray(x["b_ada"][0, :2 * D].reshape(2 * KT, P).T), "b_gate": np.ascontiguousarray(x["b_ada"][:, 2 * D:]),
        "g_cols": np.ascontiguousarray(x["g_norm"].reshape(KT, P).T),
        "gate_bias": gate_bias, "rope_const": rope, "w_gates": tiles(gates), "w_all": np.concatenate([main.reshape(-1, P, D), merging]), "head_params": hp, "w_qk": wqk,
        "w_out": x["w_out"][0], "g_final": x["g_final"].reshape(1, D),
    }
    nc = bacc.Bacc("TRN2", target_bir_lowering=False, num_devices=1)
    feed, aps = {}, {}
    for k, v in arrays.items():
        feed["in_" + k] = np.ascontiguousarray(v)
        aps[k] = nc.dram_tensor("in_" + k, v.shape, mybir.dt.from_np(v.dtype), kind="ExternalInput").ap()
    out = nc.dram_tensor("out_rows", (S, D), F32, kind="ExternalOutput").ap()
    build(nc, aps, out)
    r = run_bass_kernel_spmd(nc, [feed], core_ids=[0])
    return r.results[0]["out_rows"].reshape(1, S, D)
```
